# Optimizing a Trainium2 kernel written in Bass

```python
import jax, jax.numpy as jnp
from jax import lax
import numpy as np
import math
import jax
import jax.numpy as jnp

D_MODEL = 2048
BATCH = 1
SEQ = 256
DEPTH = 1

CHUNK = 64
Q_BLOCK = 128
SB_HEADS = 8
SB_HEAD_DIM = 128
SB_WIDTH = SB_HEADS * SB_HEAD_DIM
SGU_GROUPS = 8
SGU_GROUP_DIM = 128
SGU_WIDTH = SGU_GROUPS * SGU_GROUP_DIM
SGU_LEN = 128
D_FF = 4 * D_MODEL
IN_COLS = 3 * SB_WIDTH + 2 * SGU_WIDTH + 2 * D_MODEL
EPS = 1e-6


def rms_norm(x, g):
    xf = x.astype(jnp.float32)
    y = xf * lax.rsqrt(jnp.mean(xf * xf, axis=-1, keepdims=True) + EPS)
    return (y * g.astype(jnp.float32)).astype(x.dtype)

def layer_norm(x, g, b):
    xf = x.astype(jnp.float32)
    mu = jnp.mean(xf, axis=-1, keepdims=True)
    xc = xf - mu
    y = xc * lax.rsqrt(jnp.mean(xc * xc, axis=-1, keepdims=True) + EPS)
    return (y * g.astype(jnp.float32) + b.astype(jnp.float32)).astype(x.dtype)

def stick_breaking_attention(q, k, v):
    seq = q.shape[2]
    scale = SB_HEAD_DIM ** -0.5
    outs = []
    for blk in range(seq // Q_BLOCK):
        q0 = blk * Q_BLOCK
        kend = q0 + Q_BLOCK
        qb = q[:, :, q0:kend].astype(jnp.float32)
        kb = k[:, :, :kend].astype(jnp.float32)
        vb = v[:, :, :kend]
        z = jnp.einsum('bhtd,bhsd->bhts', qb, kb) * scale
        t_idx = q0 + jnp.arange(Q_BLOCK)[:, None]
        s_idx = jnp.arange(kend)[None, :]
        past = s_idx < t_idx
        log_keep = jnp.where(past, jax.nn.log_sigmoid(-z), 0.0)
        tail = lax.cumsum(log_keep, axis=3, reverse=True) - log_keep
        log_a = jax.nn.log_sigmoid(z) + tail
        a = jnp.where(past, jnp.exp(log_a), 0.0)
        outs.append(jnp.einsum('bhts,bhsd->bhtd', a.astype(v.dtype), vb))
    return jnp.concatenate(outs, axis=2)

def spatial_gating(u, v, ln_g, ln_b, w_s, b_s):
    bsz, seq, _ = v.shape
    v = layer_norm(v, ln_g, ln_b)
    vc = v.reshape(bsz, seq // SGU_LEN, SGU_LEN, SGU_GROUPS, SGU_GROUP_DIM)
    pos = jnp.arange(SGU_LEN)
    mask = (pos[None, :] // CHUNK) <= (pos[:, None] // CHUNK)
    w = jnp.where(mask[None], w_s, jnp.zeros_like(w_s))
    mixed = jnp.einsum('gij,bcjgd->bcigd', w, vc) + b_s.T[:, :, None]
    return u * mixed.reshape(bsz, seq, SGU_WIDTH)

def first_inputs(seed: int = 0) -> dict:
    key = jax.random.key(seed)
    ks = jax.random.split(key, 16)
    f32 = jnp.float32
    nrm = lambda k, shape, s: jax.random.normal(k, shape, f32) * s
    return {
        "x": nrm(ks[0], (BATCH, SEQ, D_MODEL), 1.0),
        "g_mix": 1.0 + nrm(ks[1], (DEPTH, D_MODEL), 0.05),
        "w_in": nrm(ks[2], (DEPTH, D_MODEL, IN_COLS), D_MODEL ** -0.5),
        "g_q": 1.0 + nrm(ks[3], (DEPTH, SB_HEADS, SB_HEAD_DIM), 0.05),
        "g_k": 1.0 + nrm(ks[4], (DEPTH, SB_HEADS, SB_HEAD_DIM), 0.05),
        "sgu_ln_g": 1.0 + nrm(ks[5], (DEPTH, SGU_WIDTH), 0.05),
        "sgu_ln_b": nrm(ks[6], (DEPTH, SGU_WIDTH), 0.02),
        "w_spatial": nrm(ks[7], (DEPTH, SGU_GROUPS, SGU_LEN, SGU_LEN), SGU_LEN ** -0.5),
        "b_spatial": 1.0 + nrm(ks[8], (DEPTH, SGU_GROUPS, SGU_LEN), 0.05),
        "w_oa": nrm(ks[9], (DEPTH, SB_WIDTH, D_MODEL), SB_WIDTH ** -0.5),
        "w_ob": nrm(ks[10], (DEPTH, SGU_WIDTH, D_MODEL), SGU_WIDTH ** -0.5),
        "w_out": nrm(ks[11], (DEPTH, D_MODEL, D_MODEL), D_MODEL ** -0.5),
        "g_ff": 1.0 + nrm(ks[12], (DEPTH, D_MODEL), 0.05),
        "w_ff1": nrm(ks[13], (DEPTH, D_MODEL, D_FF), D_MODEL ** -0.5),
        "w_ff2": nrm(ks[14], (DEPTH, D_FF, D_MODEL), D_FF ** -0.5),
    }

def first_block(x, g_mix, w_in, g_q, g_k, sgu_ln_g, sgu_ln_b, w_spatial, b_spatial,
              w_oa, w_ob, w_out, g_ff, w_ff1, w_ff2):
    bsz, seq, _ = x.shape
    splits = [SB_WIDTH, 2 * SB_WIDTH, 3 * SB_WIDTH,
              3 * SB_WIDTH + SGU_WIDTH, 3 * SB_WIDTH + 2 * SGU_WIDTH,
              3 * SB_WIDTH + 2 * SGU_WIDTH + D_MODEL]
    for l in range(DEPTH):
        h = rms_norm(x, g_mix[l])
        proj = h @ w_in[l]
        q, k, v_sb, u, v_sg, gate_a, gate_b = jnp.split(proj, splits, axis=-1)

        q = rms_norm(q.reshape(bsz, seq, SB_HEADS, SB_HEAD_DIM), g_q[l])
        k = rms_norm(k.reshape(bsz, seq, SB_HEADS, SB_HEAD_DIM), g_k[l])
        v_sb = v_sb.reshape(bsz, seq, SB_HEADS, SB_HEAD_DIM)
        o = stick_breaking_attention(q.transpose(0, 2, 1, 3), k.transpose(0, 2, 1, 3),
                                     v_sb.transpose(0, 2, 1, 3))
        y_a = o.transpose(0, 2, 1, 3).reshape(bsz, seq, SB_WIDTH) @ w_oa[l]

        u = jax.nn.gelu(u, approximate=False)
        v_sg = jax.nn.gelu(v_sg, approximate=False)
        s = spatial_gating(u, v_sg, sgu_ln_g[l], sgu_ln_b[l], w_spatial[l], b_spatial[l])
        y_b = s @ w_ob[l]

        merged = jax.nn.sigmoid(gate_a) * y_a + jax.nn.sigmoid(gate_b) * y_b
        x = x + merged @ w_out[l]

        h2 = rms_norm(x, g_ff[l])
        x = x + jnp.square(jax.nn.relu(h2 @ w_ff1[l])) @ w_ff2[l]
    return x


GRID_W = 64
CTX_LEN = 256
D_MIX = D_MODEL
HEAD_DIM = 128
NA_WIDTH = D_MIX // 2
NA_HEADS = NA_WIDTH // HEAD_DIM
NA_KH = 8
NA_KW = 16
FN_WIDTH = D_MIX // 4
FN_GROUPS = 4
FN_GROUP_DIM = FN_WIDTH // FN_GROUPS
HY_WIDTH = D_MIX - NA_WIDTH - FN_WIDTH
HY_ORDER = 2
HY_BANDS = 16
HY_EMB = 1 + 2 * HY_BANDS
HY_FILTER_HIDDEN = 64
HY_FAST_DECAY = 0.3
HY_SLOW_DECAY = 1.5
HY_TARGET = 1e-2
HY_MIN_DECAY = math.log(HY_TARGET) / HY_SLOW_DECAY
HY_MAX_DECAY = math.log(HY_TARGET) / HY_FAST_DECAY
CONV_W = 3
D_FF_2 = 11 * D_MODEL // 4
D_IN = 3 * NA_WIDTH + FN_WIDTH + (HY_ORDER + 1) * HY_WIDTH
N_MOD = 6


def rmsnorm(x, g):
    xf = x.astype(jnp.float32)
    y = xf * lax.rsqrt(jnp.mean(xf * xf, axis=-1, keepdims=True) + EPS)
    return (y * g.astype(jnp.float32)).astype(x.dtype)

def modulate(h, shift, scale):
    return h * (1 + scale) + shift

def dwconv_centred(x, w, b):
    L = x.shape[1]
    pad = CONV_W // 2
    xp = jnp.pad(x, ((0, 0), (pad, pad), (0, 0)))
    return sum(xp[:, j:j + L] * w[j] for j in range(CONV_W)) + b

def heads(t):
    return t.reshape(*t.shape[:-1], NA_HEADS, HEAD_DIM)

def split_projection(p):
    o1, o2, o3 = NA_WIDTH, 2 * NA_WIDTH, 3 * NA_WIDTH
    o4 = o3 + FN_WIDTH
    return p[..., :o1], p[..., o1:o2], p[..., o2:o3], p[..., o3:o4], p[..., o4:]

def neighbourhood_attention(q, k, v, kc, vc, rpb):
    B, L, H, Dh = q.shape
    rows = L // GRID_W
    kh = min(NA_KH, rows)
    n_loc = kh * NA_KW
    scale = Dh ** -0.5
    col = np.arange(GRID_W)
    col_start = np.clip(col - NA_KW // 2, 0, GRID_W - NA_KW)
    col_idx = col_start[:, None] + np.arange(NA_KW)[None, :]
    dcol = col_idx - col[:, None] + (NA_KW - 1)
    rpb_cols = rpb[:, :, dcol]
    kg = k.reshape(B, rows, GRID_W, H, Dh)
    vg = v.reshape(B, rows, GRID_W, H, Dh)
    q_rows = q.reshape(B, rows, GRID_W, H, Dh).transpose(1, 0, 2, 3, 4)

    def row_block(args):
        r, q_r = args
        r0 = jnp.clip(r - kh // 2, 0, rows - kh)
        k_rows = lax.dynamic_slice_in_dim(kg, r0, kh, axis=1)
        v_rows = lax.dynamic_slice_in_dim(vg, r0, kh, axis=1)
        k_win = jnp.take(k_rows, col_idx, axis=2)
        v_win = jnp.take(v_rows, col_idx, axis=2)
        drow = r0 + jnp.arange(kh) - r + (NA_KH - 1)
        bias = jnp.take(rpb_cols, drow, axis=1).transpose(0, 2, 1, 3)
        s_loc = jnp.einsum("bqhd,biqjhd->bhqij", q_r, k_win).astype(jnp.float32) * scale
        s_loc = s_loc + bias.astype(jnp.float32)
        s_ctx = jnp.einsum("bqhd,bchd->bhqc", q_r, kc).astype(jnp.float32) * scale
        s = jnp.concatenate([s_loc.reshape(B, H, GRID_W, n_loc), s_ctx], axis=-1)
        p = jax.nn.softmax(s, axis=-1).astype(v.dtype)
        p_loc = p[..., :n_loc].reshape(B, H, GRID_W, kh, NA_KW)
        return (jnp.einsum("bhqij,biqjhd->bqhd", p_loc, v_win)
                + jnp.einsum("bhqc,bchd->bqhd", p[..., n_loc:], vc))

    out = lax.map(row_block, (jnp.arange(rows), q_rows))
    return out.transpose(1, 0, 2, 3, 4).reshape(B, L, H * Dh)

def context_attention(qc, kc, vc):
    B, Lc, H, Dh = qc.shape
    s = jnp.einsum("bqhd,bkhd->bhqk", qc, kc).astype(jnp.float32) * (Dh ** -0.5)
    p = jax.nn.softmax(s, axis=-1).astype(vc.dtype)
    return jnp.einsum("bhqk,bkhd->bqhd", p, vc).reshape(B, Lc, H * Dh)

def fourier_mix(f):
    B, L, _ = f.shape
    fg = f.astype(jnp.float32).reshape(B, L, FN_GROUPS, FN_GROUP_DIM)
    y = jnp.fft.fft2(fg, axes=(1, 3), norm="ortho").real
    return y.reshape(B, L, FN_WIDTH).astype(f.dtype)

def hyena_kernel_spectrum(L, w1, b1, w2, b2, w3, freq):
    pos = jnp.arange(L, dtype=jnp.float32)[:, None]
    t = pos / max(L - 1, 1)
    bands = jnp.linspace(1e-4, HY_BANDS - 1, HY_BANDS, dtype=jnp.float32)
    ang = bands * (2.0 * math.pi / L) * pos
    z = jnp.concatenate([t, jnp.cos(ang), -jnp.sin(ang)], axis=-1)
    hdn = jnp.sin(freq * (z @ w1 + b1))
    hdn = jnp.sin(freq * (hdn @ w2 + b2))
    h = (hdn @ w3).astype(jnp.float32).reshape(L, HY_ORDER, 2, HY_WIDTH)
    deltas = jnp.linspace(HY_MIN_DECAY, HY_MAX_DECAY, HY_WIDTH, dtype=jnp.float32)
    h = h * jnp.exp(-t * jnp.abs(deltas))[:, None, None, :]
    hf, hb = h[:, :, 0], h[:, :, 1]
    kernel = jnp.concatenate([hf, jnp.zeros_like(hf[:1]), hb[:0:-1]], axis=0)
    return jnp.fft.rfft(kernel, axis=0)

def long_conv(z, k_spec, bias):
    L = z.shape[1]
    zf = z.astype(jnp.float32)
    y = jnp.fft.irfft(jnp.fft.rfft(zf, n=2 * L, axis=1) * k_spec, n=2 * L, axis=1)[:, :L]
    return (y + zf * bias).astype(z.dtype)

def hyena_mix(u, conv_w, conv_b, k_spec, bias):
    u = dwconv_centred(u, conv_w, conv_b)
    v, x1, x2 = jnp.split(u, HY_ORDER + 1, axis=-1)
    z = x1 * long_conv(v, k_spec[:, 0], bias[0])
    return x2 * long_conv(z, k_spec[:, 1], bias[1])

def merge_groups(a, f, hy, g):
    o1, o2 = NA_WIDTH, NA_WIDTH + FN_WIDTH
    return jnp.concatenate([rmsnorm(a, g[:o1]), rmsnorm(f, g[o1:o2]), rmsnorm(hy, g[o2:])], axis=-1)

def conv_gated_mlp(h, w_up, conv_w, conv_b, w_down):
    gate, up = jnp.split(h @ w_up, 2, axis=-1)
    return (jax.nn.gelu(dwconv_centred(gate, conv_w, conv_b), approximate=True) * up) @ w_down

def second_inputs(seed: int = 0) -> dict:
    key = jax.random.key(seed)
    ks = jax.random.split(key, 26)

    def nrm(k, shape, s):
        return s * jax.random.normal(k, shape, dtype=jnp.float32)

    def gain(k, shape):
        return 1.0 + 0.02 * jax.random.normal(k, shape, dtype=jnp.float32)

    return {
        "x": nrm(ks[0], (BATCH, SEQ, D_MODEL), 1.0),
        "c": nrm(ks[1], (BATCH, D_MODEL), 1.0),
        "ctx": nrm(ks[2], (BATCH, CTX_LEN, D_MODEL), 1.0),
        "c_ctx": nrm(ks[3], (D_MODEL,), 1.0),
        "ada_w": nrm(ks[4], (DEPTH, D_MODEL, N_MOD * D_MODEL), 0.3 * D_MODEL ** -0.5),
        "ada_b": nrm(ks[5], (DEPTH, N_MOD * D_MODEL), 0.02),
        "norm1_g": gain(ks[6], (DEPTH, D_MODEL)),
        "norm2_g": gain(ks[7], (DEPTH, D_MODEL)),
        "w_in": nrm(ks[8], (DEPTH, D_MODEL, D_IN), D_MODEL ** -0.5),
        "na_rpb": nrm(ks[9], (DEPTH, NA_HEADS, 2 * NA_KH - 1, 2 * NA_KW - 1), 0.02),
        "hy_conv_w": nrm(ks[10], (DEPTH, CONV_W, (HY_ORDER + 1) * HY_WIDTH), CONV_W ** -0.5),
        "hy_conv_b": nrm(ks[11], (DEPTH, (HY_ORDER + 1) * HY_WIDTH), 0.02),
        "hy_w1": nrm(ks[12], (DEPTH, HY_EMB, HY_FILTER_HIDDEN), HY_EMB ** -0.5),
        "hy_b1": nrm(ks[13], (DEPTH, HY_FILTER_HIDDEN), 0.02),
        "hy_w2": nrm(ks[14], (DEPTH, HY_FILTER_HIDDEN, HY_FILTER_HIDDEN), HY_FILTER_HIDDEN ** -0.5),
        "hy_b2": nrm(ks[15], (DEPTH, HY_FILTER_HIDDEN), 0.02),
        "hy_w3": nrm(ks[16], (DEPTH, HY_FILTER_HIDDEN, HY_ORDER * 2 * HY_WIDTH), HY_FILTER_HIDDEN ** -0.5),
        "hy_freq": gain(ks[17], (DEPTH, HY_FILTER_HIDDEN)),
        "hy_bias": nrm(ks[18], (DEPTH, HY_ORDER, HY_WIDTH), 0.1),
        "mix_norm_g": gain(ks[19], (DEPTH, D_MIX)),
        "w_out": nrm(ks[20], (DEPTH, D_MIX, D_MODEL), D_MIX ** -0.5),
        "ffn_w_up": nrm(ks[21], (DEPTH, D_MODEL, 2 * D_FF_2), D_MODEL ** -0.5),
        "ffn_conv_w": nrm(ks[22], (DEPTH, CONV_W, D_FF_2), CONV_W ** -0.5),
        "ffn_conv_b": nrm(ks[23], (DEPTH, D_FF_2), 0.02),
        "ffn_w_down": nrm(ks[24], (DEPTH, D_FF_2, D_MODEL), D_FF_2 ** -0.5),
        "final_norm_g": gain(ks[25], (D_MODEL,)),
    }

def second_block(x, c, ctx, c_ctx, ada_w, ada_b, norm1_g, norm2_g, w_in, na_rpb,
              hy_conv_w, hy_conv_b, hy_w1, hy_b1, hy_w2, hy_b2, hy_w3, hy_freq, hy_bias,
              mix_norm_g, w_out, ffn_w_up, ffn_conv_w, ffn_conv_b, ffn_w_down, final_norm_g):
    L = x.shape[1]
    Lc = ctx.shape[1]
    xc = ctx
    s_lat = jax.nn.silu(c)
    s_ctx = jax.nn.silu(c_ctx)
    for l in range(DEPTH):
        update_ctx = l < DEPTH - 1
        mod = (s_lat @ ada_w[l] + ada_b[l])[:, None, :]
        sh1, sc1, g1, sh2, sc2, g2 = jnp.split(mod, N_MOD, axis=-1)
        mod_c = s_ctx @ ada_w[l] + ada_b[l]
        csh1, csc1, cg1, csh2, csc2, cg2 = jnp.split(mod_c, N_MOD, axis=-1)
        filt = (hy_w1[l], hy_b1[l], hy_w2[l], hy_b2[l], hy_w3[l], hy_freq[l])

        h = modulate(rmsnorm(x, norm1_g[l]), sh1, sc1)
        hc = modulate(rmsnorm(xc, norm1_g[l]), csh1, csc1)
        q, k, v, f, hy = split_projection(h @ w_in[l])
        if update_ctx:
            qc, kc, vc, fc, hyc = split_projection(hc @ w_in[l])
        else:
            kc, vc = jnp.split(hc @ w_in[l][:, NA_WIDTH:3 * NA_WIDTH], 2, axis=-1)
        kc_h, vc_h = heads(kc), heads(vc)
        a = neighbourhood_attention(heads(q), heads(k), heads(v), kc_h, vc_h, na_rpb[l])
        y = merge_groups(a, fourier_mix(f),
                         hyena_mix(hy, hy_conv_w[l], hy_conv_b[l], hyena_kernel_spectrum(L, *filt), hy_bias[l]),
                         mix_norm_g[l])
        x = x + g1 * (y @ w_out[l])
        if update_ctx:
            ac = context_attention(heads(qc), kc_h, vc_h)
            yc = merge_groups(ac, fourier_mix(fc),
                              hyena_mix(hyc, hy_conv_w[l], hy_conv_b[l], hyena_kernel_spectrum(Lc, *filt), hy_bias[l]),
                              mix_norm_g[l])
            xc = xc + cg1 * (yc @ w_out[l])

        ffn = (ffn_w_up[l], ffn_conv_w[l], ffn_conv_b[l], ffn_w_down[l])
        x = x + g2 * conv_gated_mlp(modulate(rmsnorm(x, norm2_g[l]), sh2, sc2), *ffn)
        if update_ctx:
            xc = xc + cg2 * conv_gated_mlp(modulate(rmsnorm(xc, norm2_g[l]), csh2, csc2), *ffn)
    return rmsnorm(x, final_norm_g)


def setup_inputs(seed=0):
    out = dict(first_inputs(seed))
    for name, value in second_inputs(seed + 1).items():
        if name != "x":
            out[name + "_2"] = value
    return out


def reference(
    x, g_mix, w_in, g_q, g_k, sgu_ln_g, sgu_ln_b, w_spatial, b_spatial, w_oa, w_ob, w_out, g_ff,
    w_ff1, w_ff2, c_2, ctx_2, c_ctx_2, ada_w_2, ada_b_2, norm1_g_2, norm2_g_2, w_in_2, na_rpb_2,
    hy_conv_w_2, hy_conv_b_2, hy_w1_2, hy_b1_2, hy_w2_2, hy_b2_2, hy_w3_2, hy_freq_2, hy_bias_2,
    mix_norm_g_2, w_out_2, ffn_w_up_2, ffn_conv_w_2, ffn_conv_b_2, ffn_w_down_2, final_norm_g_2,
):
    x = first_block(
        x, g_mix, w_in, g_q, g_k, sgu_ln_g, sgu_ln_b, w_spatial, b_spatial, w_oa, w_ob, w_out,
        g_ff, w_ff1, w_ff2,
    )
    return second_block(
        x, c_2, ctx_2, c_ctx_2, ada_w_2, ada_b_2, norm1_g_2, norm2_g_2, w_in_2, na_rpb_2,
        hy_conv_w_2, hy_conv_b_2, hy_w1_2, hy_b1_2, hy_w2_2, hy_b2_2, hy_w3_2, hy_freq_2,
        hy_bias_2, mix_norm_g_2, w_out_2, ffn_w_up_2, ffn_conv_w_2, ffn_conv_b_2, ffn_w_down_2,
        final_norm_g_2,
    )


_drawn_inputs = setup_inputs


def setup_inputs(seed=0):
    import zlib

    import numpy as np

    out = dict(_drawn_inputs(seed))
    spreads = {}
    factors = {'g_q': 7.911,
     'g_k': 7.71,
     'sgu_ln_g': 3.755,
     'sgu_ln_b': 8.0,
     'b_spatial': 3.613,
     'ada_b_2': 3.287,
     'norm1_g_2': 8.0,
     'norm2_g_2': 8.0,
     'na_rpb_2': 64.0,
     'hy_conv_b_2': 33.996,
     'hy_b1_2': 8.0,
     'hy_b2_2': 8.0,
     'hy_freq_2': 8.0,
     'hy_bias_2': 8.0,
     'mix_norm_g_2': 29.558,
     'ffn_conv_b_2': 23.864,
     'final_norm_g_2': 7.538}
    for name, (base, spread) in spreads.items():
        noise = np.random.default_rng([zlib.crc32(name.encode()), seed]).standard_normal(out[name].shape)
        drawn = base * np.exp(spread * noise) if base else spread * noise
        out[name] = jnp.asarray(drawn.astype(out[name].dtype))
    for name, factor in factors.items():
        out[name] = (out[name] * factor).astype(out[name].dtype)
    return out
```

```python
import math
import numpy as np
import concourse.bass as bass
from concourse import mybir
from contextlib import ExitStack

P = 128
T = 256
TT = T // P
D = 2048
KC = D // P
NB = 512
FT = NB // P
SLOTS = 4
HEADS = 8
DH = 128
CHUNK = 64
GRID_W, NA_KH, NA_KW = 64, 8, 16
ROWS = T // GRID_W
FNG = 4
HW = 512
HT = HW // P
D_FF1, D_FF2 = 8192, 5632
STEPS1, STEPS2 = D_FF1 // NB, D_FF2 // NB
N_MOD = 6
EPS = 1e-6
NEG = -1e30
SCALE = DH ** -0.5
L2 = 2 * T

COLS = {}
_n = 0
for _name, _w in [("g_mix", KC), ("g_q", HEADS), ("g_k", HEADS), ("g_ff", KC), ("norm1", KC), ("norm2", KC),
                  ("mix", KC), ("final", KC), ("ada_b", N_MOD * KC), ("hy_w", 3 * 12), ("hy_b", 12),
                  ("hy_bias", 2 * HT), ("ff_w", STEPS2 * 4 * FT), ("c", 2 * KC), ("mlp", 3)]:
    COLS[_name] = (_n, _w)
    _n += _w
NCOLS = _n

G_IN1, N_IN1 = 0, 18
G_ADA, N_ADA_HEAD = 18, 10
G_OAB = G_ADA + N_ADA_HEAD
G_OUT1 = G_OAB + 4
G_FF1 = G_OUT1 + 4
FF1_ITERS = (STEPS1 - 4) // 2
G_FF1_TAIL = G_FF1 + 1 + 3 * (STEPS1 - 2)
G_IN2 = G_FF1_TAIL + 3
G_OUT2 = G_IN2 + 10
G_FF2 = G_OUT2 + 4
FF2_ITERS = (STEPS2 - 3) // 2
G_END = G_FF2 + 3 * STEPS2
Q_FF1 = G_FF1
Q_FF1_TAIL = Q_FF1 + 1 + 6 * (STEPS1 - 2)
Q_IN2 = Q_FF1_TAIL + 1 + 4 + 4
Q_OUT2 = Q_IN2 + 10
Q_FF2 = Q_OUT2 + 4
Q_END = Q_FF2 + 6 * STEPS2
IN2_COLS = [1024, 1536, 2048, 2560, 0, 512, 3072, 3584, 4096, 4608]
E_NORM1, E_OAB, E_OUT1, E_NORM2, E_CTX, E_NORM3, E_OUT2, E_NORM4 = range(8)


class Place:

    def __init__(self, base, i=None, per=0):
        self.base, self.i, self.per = base, i, per

    def plus(self, n):
        return Place(self.base + n, self.i, self.per)

    def value(self, mul=1, plus=0):
        v = self.base * mul + plus
        return v if self.i is None else self.i * (self.per * mul) + v

    def half(self, plus=0):
        v = self.base // 2 + plus
        return v if self.i is None else self.i * (self.per // 2) + v

    @property
    def slot(self):
        return self.base % 2


class Chain:

    def __init__(self, eng, sem):
        self.eng, self.sem, self.n = eng, sem, 0

    def did(self, ins):
        ins.then_inc(self.sem, 1)
        self.n += 1

    def settle(self):
        self.eng.wait_ge(self.sem, self.n)


N_IN, N_FF1, N_CTX, N_MIX_IN, N_A, N_F, N_H, N_FF2, N_LAST = range(9)
ROOT_AFTER = [0, 4, 8, 12, 16, 18, 19, 20, 24]
N_FF2H, N_FINAL = 5, 6


def ff1_place(j):
    return (Place(G_FF1 + 1 + 3 * j.base, j.i, 3 * j.per), Place(Q_FF1 + 1 + 6 * j.base, j.i, 6 * j.per),
            Place(N_ADA_HEAD + j.base, j.i, j.per))


def ff2_place(j):
    return (Place(G_FF2 + 2 + 3 * j.base, j.i, 3 * j.per), Place(Q_FF2 + 2 + 6 * j.base, j.i, 6 * j.per))


def build_program(nc, d, out):
    f32, f32r = mybir.dt.float32, mybir.dt.float32r
    ALU = mybir.AluOpType
    ACT = mybir.ActivationFunctionType
    AX = mybir.AxisListType
    base = 16512

    with ExitStack() as ctx:
        def at(name, shape, offset, dt=f32):
            return nc.alloc_sbuf_tensor_at(name, shape, dt, offset=base + offset)

        def sem(name):
            return ctx.enter_context(nc.semaphore(name))

        K = 1024
        RAW = at("RAW", [P, SLOTS, FT, NB], 0)
        WH = at("WH", [P, 2, FT, NB], 32 * K, f32r)
        WL = at("WL", [P, 2, FT, NB], 48 * K, f32r)
        X = at("X", [P, KC, T], 64 * K)
        XH = at("XH", [P, KC, T], 80 * K, f32r)
        XL = at("XL", [P, KC, T], 96 * K, f32r)
        HH = at("HH", [P, 2, FT, T], 112 * K, f32r)
        HL = at("HL", [P, 2, FT, T], 120 * K, f32r)
        NT = at("NT", [P, KC, T], 112 * K)
        CON = 128 * K
        cols = at("cols", [P, NCOLS], CON)
        small = CON + 2176
        mats = at("mats", [P, 4, P], small)
        mod = at("mod", [P, N_MOD * KC, 2], small + 2048)
        rt = at("rt", [P, 2 * T], small + 2816)
        MR = at("MR", [4, NB], small + 2816)
        csil = at("csil", [P, KC, 4], small + 4864, f32r)
        brow = at("brow", [64, 64], small + 5120)
        ctmp = at("ctmp", [P, 2, KC], small + 5120)
        csig = at("csig", [P, 2, KC], small + 5248)
        gmod = at("gmod", [P, KC], small + 5376)
        lnst = at("lnst", [P, 16], small + 5440)
        cw = at("cw", [P, 4 * FT], small + 5504)
        smx = at("smx", [P, 2, 4], small + 5568)
        sel = at("sel", [4, 2], small + 5600)
        epsc = at("epsc", [P, 1], small + 5632)
        AR = small + 5664
        assert 4 * NCOLS <= 2176
        ones, ident, lower, past = (mats[:, n, :] for n in range(4))

        def col(name, n=0, w=1):
            s = COLS[name][0] + n
            return cols[:, s:s + w]

        qT = at("qT", [P, HEADS, T], AR)
        kT = at("kT", [P, HEADS, T], AR + 8 * K)
        v1 = at("v1", [P, TT, 1024], AR + 16 * K)
        uT = at("uT", [P, 8, T], AR + 24 * K)
        vg = at("vg", [P, TT, 1024], AR + 32 * K)
        ga = at("ga", [P, KC, T], AR + 40 * K)
        gb = at("gb", [P, KC, T], AR + 56 * K)
        lng = at("lng", [P, 1024], AR + 40 * K)
        lnb = at("lnb", [P, 1024], AR + 44 * K)
        bsp = at("bsp", [P, 8, P], AR + 48 * K)
        wsp = at("wsp", [P, 8, P], AR + 52 * K)
        t1 = 112 * K
        qk_sq = at("qk_sq", [P, FT, T], t1)
        zs = at("zs", [P, 2, 384], t1)
        zneg = at("zneg", [P, 2, 384], t1 + 3 * K)
        lk = at("lk", [P, 2, 384], t1 + 6 * K)
        lsg = at("lsg", [P, 2, 384], t1 + 9 * K)
        aw = at("aw", [P, 2, 384], t1 + 12 * K)
        FR = at("FR", [P, FT, T], AR)
        FQ = at("FQ", [P, FT, T], AR + 4 * K)
        GS = at("GS", [P, FT, T], AR + 8 * K)
        CV = at("CV", [P, FT, T], AR + 12 * K)
        CX = at("CX", [P, KC, T], AR)
        q2 = at("q2", [P, HEADS, T], AR)
        k2 = at("k2", [P, HEADS, T], AR + 8 * K)
        v2 = at("v2", [P, TT, 1024], AR + 16 * K)
        kc2 = at("kc2", [P, HEADS, T], AR + 24 * K)
        vc2 = at("vc2", [P, TT, 1024], AR + 32 * K)
        CH = at("CH", [P, KC, T], AR + 40 * K, f32r)
        CL = at("CL", [P, KC, T], AR + 56 * K, f32r)
        bia = at("bia", [P, TT, HEADS * ROWS, GRID_W], AR + 40 * K)
        hyT = at("hyT", [P, 12, T], AR + 56 * K)
        fX = at("fX", [P, TT, 512], AR + 68 * K)
        fY = at("fY", [P, FNG, T], AR + 68 * K)
        bsel = at("bsel", [64, GRID_W, P], 80 * K)
        S2 = at("S2", [P, 2, 2 * T], t1)
        P2 = at("P2", [P, 2, 2 * T], t1 + 4 * K)
        PT = at("PT", [P, 2, 4, T], t1 + 8 * K)
        fcl = at("fcl", [P, TT, 2 * T], AR + 48 * K)
        fcd = at("fcd", [P, 2, P], AR + 52 * K)
        fU = at("fU", [P, FNG, 2 * T], t1)
        hyC = at("hyC", [P, 12, T], AR + 8 * K)
        Gi = at("Gi", [P, 4, T], AR + 20 * K)
        KS = at("KS", [P, 2, 5, HW], AR + 24 * K)
        zt = at("zt", [P, TT, HW], AR + 44 * K)
        YS = at("YS", [P, 4, HW], AR + 48 * K)
        hSD = at("hSD", [P, 2, 2, TT, HW], 80 * K)
        dec = at("dec", [P, 2, TT, HW], 96 * K)
        Ef = at("Ef", [P, TT, 6 * P], 104 * K)
        pz = at("pz", [33, T], 110 * K)
        w1h = at("w1h", [33, 64], 111 * K)
        w2h = at("w2h", [64, 64], 111 * K + 512)
        w3h = at("w3h", [64, 2048], t1)
        hdn = at("hdn", [64, 2, T], t1 + 8 * K)
        sr = at("sr", [64, 3, T], t1 + 10 * K)
        hfb = at("hfb", [P, 2, HW], t1 + 13 * K - K)
        pp = at("pp", [P, 2, 2, HW], t1)
        zT2 = at("zT2", [P, HT, T], t1 + 8 * K)

        PS = ctx.enter_context(nc.psum_tensor("PS", [P, 8, 512], f32))

        def acc_ws(s):
            return PS[:, 2 * s:2 * s + 2, :].rearrange("p b (h t) -> p (b h) t", t=T)

        def acc_as(s):
            return PS[:, 2 * s:2 * s + 2, :]

        def bank(n):
            return PS[:, n, :]

        def ctx_as(n):
            return PS[:, 4 + 2 * (n % 2):6 + 2 * (n % 2), :]

        def ctx_ws(n):
            return ctx_as(n).rearrange("p b (h t) -> p (b h) t", t=T)

        def chunks(w):
            return w.rearrange("(s k p) n -> s p k n", p=P, k=FT)

        w_in, w_out, w_ff1, w_ff2 = map(chunks, (d["w_in"], d["w_out"], d["w_ff1"], d["w_ff2"]))
        w_oa, w_ob, ada_w = map(chunks, (d["w_oa"], d["w_ob"], d["ada_w"]))
        w_in2, w_out2, w_up, w_down = map(chunks, (d["w_in_2"], d["w_out_2"], d["w_up"], d["w_down"]))

        raw_in = [sem(f"raw_in{s}") for s in range(SLOTS)]
        hi_done = sem("hi_done")
        lo_done = sem("lo_done")
        pe_chunk = sem("pe_chunk")
        acc_free = [sem("acc_free0"), sem("acc_free1")]
        x_hi = sem("x_hi")
        x_lo = sem("x_lo")
        act_own = sem("act_own")
        dve_own = sem("dve_own")
        names = (
            "x_in cols_in mats_in eps_set ln_in cx_in brow_in bsel_in four_in e_in mlp_in mlp3_in gi_in outs "
            "norm_sq norm_sum norm_rt norm_h qk_sqd qk_sum qk_rt q_done z_done zs_done zneg_done l_done lk_done "
            "cum_done la_done a_done am_done pv_done o_done ln_var ln_root mix_done sgu_ps s_done b_free merged "
            "csig_done csil_f csil_hi csil_done mt_done mod_done relu_sq hid_hi hid_lo ctx_free bias_ps "
            "bias_done q2_done sc_done sm_done exp_done pn_done tp_done pt_done pv2_done a2_done fu_ps fu_done "
            "fy_ps fy_done hyc_done mlp_ps mlp_arg mlp_sin hf_ps hf_done ks_ps ks_done zt_ps zt_done zf_ps "
            "ys_done yi_ps hz_done cw_done conv_a conv_b conv_done gelu_done").split()
        sm = {n: sem(n) for n in names}

        block = ctx.enter_context(nc.Block())

        @block.sync
        def _(sp):
            def load(group, chunk):
                for s in range(SLOTS):
                    if group.i is not None or group.base >= 1:
                        sp.wait_ge(hi_done, group.value(4, s - 3))
                        sp.wait_ge(lo_done, group.value(4, s - 3))
                    sp.dma_start(RAW[:, s], chunk(s)).then_inc(raw_in[s], 16)

            def wide(view, n0):
                return lambda s: view[s][:, :, n0:n0 + NB]

            def wide_at(view, start):
                return lambda s: view[s][:, :, bass.ds(start, NB)]

            def down(view, j):
                return lambda s: view[j][:, :, s * NB:(s + 1) * NB]

            sp.dma_start(X[:, :, :], d["x"].rearrange("(k p) t -> p k t", p=P)).then_inc(sm["x_in"], 16)
            sp.dma_start(cols[:, :], d["cols"]).then_inc(sm["cols_in"], 16)
            sp.dma_start(mats[:, :, :], d["mats"]).then_inc(sm["mats_in"], 16)
            sp.dma_start(sel[:, :], d["sel"]).then_inc(sm["mats_in"], 16)
            for dst, name in ((lng[:, :], "ln_g"), (lnb[:, :], "ln_b"),
                              (bsp[:, :, :], "b_sp"), (wsp[:, :, :], "w_sp")):
                sp.dma_start(dst, d[name]).then_inc(sm["ln_in"], 16)
            for g in range(N_IN1):
                load(Place(G_IN1 + g), wide(w_in, g * NB))
            with sp.Fori(0, N_ADA_HEAD // 2) as i:
                for m in range(2):
                    load(Place(G_ADA + m, i, 2), wide_at(ada_w, i * (2 * NB) + m * NB))
            for g in range(4):
                load(Place(G_OAB + g),
                     lambda s: (w_oa if s < 2 else w_ob)[s % 2][:, :, g * NB:(g + 1) * NB])
            for g in range(4):
                load(Place(G_OUT1 + g), wide(w_out, g * NB))
            load(Place(G_FF1), wide(w_ff1, 0))
            for j in range(2):
                load(Place(G_FF1 + 1 + 3 * j), wide(ada_w, (N_ADA_HEAD + j) * NB))
                load(Place(G_FF1 + 2 + 3 * j), wide(w_ff1, (j + 1) * NB))
                load(Place(G_FF1 + 3 + 3 * j), down(w_ff2, j))
            with sp.Fori(0, FF1_ITERS) as i:
                for j in (2, 3):
                    load(Place(G_FF1 + 1 + 3 * j, i, 6), wide_at(ada_w, i * (2 * NB) + (N_ADA_HEAD + j) * NB))
                    load(Place(G_FF1 + 2 + 3 * j, i, 6), wide_at(w_ff1, i * (2 * NB) + (j + 1) * NB))
                    load(Place(G_FF1 + 3 + 3 * j, i, 6), down(w_ff2, i * 2 + j))
            load(Place(G_FF1_TAIL), wide(w_ff1, (STEPS1 - 1) * NB))
            load(Place(G_FF1_TAIL + 1), down(w_ff2, STEPS1 - 2))
            load(Place(G_FF1_TAIL + 2), down(w_ff2, STEPS1 - 1))
            sp.wait_ge(sm["hid_lo"], STEPS1)
            sp.dma_start(CX[:, :, :], d["ctx"].rearrange("(k p) t -> p k t", p=P)).then_inc(sm["cx_in"], 16)
            for n, c in enumerate(IN2_COLS):
                load(Place(G_IN2 + n), wide(w_in2, c))
            sp.wait_ge(pe_chunk, 4 * G_OUT2)
            sp.dma_start(brow[:, :], d["brow"]).then_inc(sm["brow_in"], 16)
            sp.dma_start(bsel[:, :, :], d["bsel"]).then_inc(sm["bsel_in"], 16)
            load(Place(G_OUT2), wide(w_out2, 0))
            sp.wait_ge(sm["bias_ps"], 8)
            sp.dma_start(Ef[:, :, :], d["ef"]).then_inc(sm["e_in"], 16)
            sp.dma_start(dec[:, :, :, :], d["dec"]).then_inc(sm["e_in"], 16)
            sp.dma_start(pz[:, :], d["pz"]).then_inc(sm["mlp_in"], 16)
            sp.dma_start(w1h[:, :], d["hy_w1"]).then_inc(sm["mlp_in"], 16)
            sp.dma_start(w2h[:, :], d["hy_w2"]).then_inc(sm["mlp_in"], 16)
            sp.wait_ge(sm["a2_done"], HEADS)
            sp.dma_start(fcl[:, :, :], d["fcl"]).then_inc(sm["four_in"], 16)
            sp.dma_start(fcd[:, :, :], d["fcd"]).then_inc(sm["four_in"], 16)
            sp.dma_start(Gi[:, :, :], d["gi"]).then_inc(sm["gi_in"], 16)
            sp.wait_ge(sm["fy_ps"], FNG)
            sp.dma_start(w3h[:, :], d["hy_w3"]).then_inc(sm["mlp3_in"], 16)
            for g in range(1, 4):
                load(Place(G_OUT2 + g), wide(w_out2, g * NB))
            load(Place(G_FF2), wide(w_up, 0))
            load(Place(G_FF2 + 1), wide(w_up, D_FF2))
            for j in range(2):
                load(Place(G_FF2 + 2 + 3 * j), wide(w_up, (j + 1) * NB))
                load(Place(G_FF2 + 3 + 3 * j), wide(w_up, D_FF2 + (j + 1) * NB))
                load(Place(G_FF2 + 4 + 3 * j), down(w_down, j))
            with sp.Fori(0, FF2_ITERS) as i:
                for j in (2, 3):
                    load(Place(G_FF2 + 2 + 3 * j, i, 6), wide_at(w_up, i * (2 * NB) + (j + 1) * NB))
                    load(Place(G_FF2 + 3 + 3 * j, i, 6), wide_at(w_up, i * (2 * NB) + D_FF2 + (j + 1) * NB))
                    load(Place(G_FF2 + 4 + 3 * j, i, 6), down(w_down, i * 2 + j))
            load(Place(G_END - 1), down(w_down, STEPS2 - 1))
            for n in range(4):
                sp.wait_ge(sm["norm_h"], 4 * N_FINAL + n + 1)
                sp.dma_start(out.rearrange("(k p) t -> p k t", p=P)[:, 4 * n:4 * n + 4, :],
                             NT[:, 4 * n:4 * n + 4, :]).then_inc(sm["outs"], 16)
            sp.wait_ge(sm["outs"], 64)

        @block.scalar
        def _(act):
            own = Chain(act, act_own)
            A = nc.scalar.activation

            def high(g, s):
                act.wait_ge(raw_in[s], g.value(16, 16))
                if g.i is not None or 4 * g.base + s >= 2:
                    act.wait_ge(pe_chunk, g.value(4, s - 1))
                A(WH[:, s % 2], RAW[:, s], ACT.Copy).then_inc(hi_done, 1)

            def group(g, after=None):
                for s in range(SLOTS):
                    high(g, s)
                    if after:
                        after(s)

            def evac(g, q, dst, fn, ws=True):
                act.wait_ge(pe_chunk, g.value(4, 4))
                A(dst, acc_ws(q.slot) if ws else acc_as(q.slot), fn).then_inc(acc_free[q.slot], 1)

            def root(n, total):
                act.wait_ge(sm["norm_sum"], n + 1)
                if n:
                    act.wait_ge(sm["norm_h"], ROOT_AFTER[n])
                A(rt[:, 0:T], bank(4)[:, 0:T], ACT.Sqrt, bias=epsc[:, 0:1],
                  scale=1.0 / total).then_inc(sm["norm_rt"], 1)

            def split_high(src, n, ready=None, count=0):
                if ready is not None:
                    act.wait_ge(ready, count)
                A(XH[:, 4 * n:4 * n + 4, :], src, ACT.Copy).then_inc(x_hi, 1)

            def shifted_high(dst, shift, norm):
                for n in range(4):
                    act.wait_ge(sm["norm_h"], 4 * norm + n + 1)
                    for k in range(4 * n, 4 * n + 4):
                        ins = A(dst[:, k, :], NT[:, k, :], ACT.Identity, bias=shift(k))
                    ins.then_inc(x_hi, 1)

            act.wait_ge(sm["cols_in"], 16)
            act.wait_ge(sm["eps_set"], 1)
            root(N_IN, D)
            for n in range(4):
                split_high(NT[:, 4 * n:4 * n + 4, :], n, sm["norm_h"], 4 * N_IN + n + 1)

            def project_out(g):
                n = g % 2
                m = (g - 10) % 4
                t4 = slice(4 * n, 4 * n + 4)
                c5 = slice(n * NB, (n + 1) * NB)
                q = Place(g)
                if g < 2:
                    evac(q, q, qT[:, t4, :], ACT.Copy)
                elif g < 4:
                    evac(q, q, kT[:, t4, :], ACT.Copy)
                elif g < 6:
                    evac(q, q, v1[:, :, c5], ACT.Copy, ws=False)
                elif g < 8:
                    evac(q, q, uT[:, t4, :], ACT.Gelu)
                elif g < 10:
                    evac(q, q, vg[:, :, c5], ACT.Gelu, ws=False)
                else:
                    evac(q, q, (ga if g < 14 else gb)[:, 4 * m:4 * m + 4, :], ACT.Sigmoid)

            for g in range(10):
                group(Place(g), lambda s: project_out(g - 1) if s == 0 and g else None)
            high(Place(10), 0)
            project_out(9)
            high(Place(10), 1)
            for n in range(8):
                act.wait_ge(sm["qk_sum"], n + 1)
                act.wait_ge(sm["q_done"], n)
                A(rt[:, :], bank(4 + n % 2), ACT.Sqrt, bias=epsc[:, 0:1], scale=1.0 / DH)\
                    .then_inc(sm["qk_rt"], 1)
            for h in range(HEADS):
                b = h % 2
                act.wait_ge(sm["z_done"], h + 1)
                if h >= 2:
                    act.wait_ge(sm["lk_done"], h - 1)
                A(zs[:, b, :], bank(4 + b)[:, 0:384], ACT.Copy, scale=SCALE).then_inc(sm["zs_done"], 1)
                act.wait_ge(sm["zneg_done"], h + 1)
                own.did(A(zneg[:, b, :], zneg[:, b, :], ACT.Exp))
                own.settle()
                A(zneg[:, b, :], zneg[:, b, :], ACT.Ln, bias=1.0).then_inc(sm["l_done"], 1)
                act.wait_ge(sm["la_done"], h + 1)
                if h >= 2:
                    act.wait_ge(sm["pv_done"], h - 1)
                A(aw[:, b, :], lsg[:, b, :], ACT.Exp).then_inc(sm["a_done"], 1)
                act.wait_ge(sm["pv_done"], h + 1)
                A(qT[:, h, :], bank(6 + b)[:, 0:T], ACT.Copy).then_inc(sm["o_done"], 1)
            for t in range(TT):
                act.wait_ge(sm["ln_var"], t + 1)
                A(lnst[:, 14 + t:15 + t], lnst[:, 12 + t:13 + t], ACT.Sqrt, bias=epsc[:, 0:1])\
                    .then_inc(sm["ln_root"], 1)
            act.wait_ge(sm["s_done"], 8)
            high(Place(10), 2)
            high(Place(10), 3)
            for g in range(11, N_IN1):
                group(Place(g), lambda s: project_out(g - 1) if s == 0 else None)

            def ada_row(q, g, a):
                act.wait_ge(pe_chunk, g.value(4, 4))
                if a.i is not None or a.base >= 1:
                    act.wait_ge(sm["mt_done"], a.value())
                A(MR[:, :], acc_as(q.slot)[0:4, 0, :], ACT.Copy).then_inc(acc_free[q.slot], 1)

            A(csig[:, :, :], col("c", 0, 2 * KC).rearrange("p (a k) -> p a k", a=2), ACT.Sigmoid)\
                .then_inc(sm["csig_done"], 1)
            act.wait_ge(sm["csil_f"], 1)
            A(csil[:, :, 0:2], ctmp[:, :, :].rearrange("p a k -> p k a"), ACT.Copy).then_inc(sm["csil_hi"], 1)

            def first_ada(s):
                if s == 0:
                    project_out(N_IN1 - 1)

            def second_ada(s):
                if s == 0:
                    ada_row(Place(G_ADA), Place(G_ADA), Place(0))
                split_high((qT if s < 2 else uT)[:, 4 * (s % 2):4 * (s % 2) + 4, :], s, pe_chunk, 4 * N_IN1)

            group(Place(G_ADA), first_ada)
            group(Place(G_ADA + 1), second_ada)
            with act.Fori(0, N_ADA_HEAD // 2 - 1) as i:
                for m in range(2):
                    g = Place(G_ADA + 1 + m, i, 2)
                    group(g.plus(1), lambda s: ada_row(g, g, Place(1 + m, i, 2)) if s == 0 else None)
            g = Place(G_OAB - 1)
            group(Place(G_OAB), lambda s: ada_row(g, g, Place(N_ADA_HEAD - 1)) if s == 0 else None)
            for g in range(1, 4):
                group(Place(G_OAB + g))
            for n in range(4):
                act.wait_ge(pe_chunk, 4 * G_OUT1)
                split_high(ga[:, 4 * n:4 * n + 4, :], n, sm["merged"], n + 1)
            for g in range(4):
                group(Place(G_OUT1 + g))
            root(N_FF1, D)
            for n in range(4):
                split_high(NT[:, 4 * n:4 * n + 4, :], n, sm["norm_h"], 4 * N_FF1 + n + 1)

            def relu(q, g, j):
                act.wait_ge(pe_chunk, g.value(4, 4))
                if j.i is not None or j.base >= 1:
                    act.wait_ge(sm["relu_sq"], j.value())
                A(FR[:, :, :], acc_ws(q.slot), ACT.Relu).then_inc(acc_free[q.slot], 1)

            def hidden_high(j):
                act.wait_ge(sm["relu_sq"], j.value(1, 1))
                A(HH[:, j.base % 2], FQ[:, :, :], ACT.Copy).then_inc(sm["hid_hi"], 1)

            def ff1_step(j, first=False):
                g, q, a = ff1_place(j)

                def during_mod(s):
                    if first and s == 0:
                        relu(Place(Q_FF1), Place(G_FF1), Place(0))
                    if first and s == 1:
                        hidden_high(Place(0))

                def during_down(s):
                    if s == 0:
                        relu(q.plus(1), g.plus(1), j.plus(1))
                    if s == 1:
                        hidden_high(j.plus(1))

                group(g, during_mod)
                group(g.plus(1), lambda s: ada_row(q, g, a) if s == 0 else None)
                group(g.plus(2), during_down)

            group(Place(G_FF1))
            ff1_step(Place(0), first=True)
            ff1_step(Place(1))
            with act.Fori(0, FF1_ITERS) as i:
                ff1_step(Place(2, i, 2))
                ff1_step(Place(3, i, 2))

            def ff1_tail(s):
                if s == 0:
                    relu(Place(Q_FF1_TAIL), Place(G_FF1_TAIL), Place(STEPS1 - 1))
                if s == 1:
                    hidden_high(Place(STEPS1 - 1))

            group(Place(G_FF1_TAIL))
            group(Place(G_FF1_TAIL + 1), ff1_tail)
            group(Place(G_FF1_TAIL + 2))

            root(N_CTX, D)
            shifted_high(CH, lambda k: mod[:, k, 1:2], N_CTX)
            root(N_MIX_IN, D)
            shifted_high(XH, lambda k: mod[:, k, 0:1], N_MIX_IN)

            def project2_out(n):
                q, g = Place(Q_IN2 + n), Place(G_IN2 + n)
                t4 = slice(4 * (n % 2), 4 * (n % 2) + 4)
                c5 = slice((n % 2) * NB, (n % 2 + 1) * NB)
                if n < 2:
                    evac(g, q, k2[:, t4, :], ACT.Copy)
                    A(kc2[:, t4, :], ctx_ws(n), ACT.Copy).then_inc(sm["ctx_free"], 1)
                elif n < 4:
                    evac(g, q, v2[:, :, c5], ACT.Copy, ws=False)
                    A(vc2[:, :, c5], ctx_as(n), ACT.Copy).then_inc(sm["ctx_free"], 1)
                elif n < 6:
                    evac(g, q, q2[:, t4, :], ACT.Copy)
                elif n == 6:
                    evac(g, q, fX[:, :, :], ACT.Copy, ws=False)
                else:
                    evac(g, q, hyT[:, 4 * (n - 7):4 * (n - 6), :], ACT.Copy)

            for n in range(10):
                group(Place(G_IN2 + n), lambda s: project2_out(n - 1) if s == 0 and n else None)
            project2_out(9)
            act.wait_ge(acc_free[0], (Q_IN2 + 10) // 2)
            act.wait_ge(acc_free[1], (Q_IN2 + 10) // 2)
            A(q2[:, :, :], q2[:, :, :], ACT.Copy, scale=SCALE).then_inc(sm["q2_done"], 1)
            for n in range(8):
                act.wait_ge(sm["bias_ps"], n + 1)
                A(bia[:, :, :, 8 * n:8 * n + 8], bank(4 + n % 4).rearrange("p (c t h) -> p t h c", t=TT, c=8),
                  ACT.Copy).then_inc(sm["bias_done"], 1)
            for u in range(2 * HEADS):
                b = u % 2
                act.wait_ge(sm["sm_done"], u + 1)
                if u >= 2:
                    act.wait_ge(sm["tp_done"], u - 1)
                A(P2[:, b, :], S2[:, b, :], ACT.Exp, bias=smx[:, b, 0:1],
                  accum_out=smx[:, b, 1:2]).then_inc(sm["exp_done"], 1)
                if b == 1:
                    h = u // 2
                    act.wait_ge(sm["pv2_done"], h + 1)
                    A(q2[:, h, :], bank(2 * (h % 2))[:, 0:T], ACT.Copy).then_inc(sm["a2_done"], 1)
            for n in range(FNG):
                act.wait_ge(sm["fu_ps"], n + 1)
                A(fU[:, n, :], bank(4 + n % 2), ACT.Copy).then_inc(sm["fu_done"], 1)
            for n in range(FNG):
                act.wait_ge(sm["fy_ps"], n + 1)
                A(fY[:, n, :], bank(6 + n % 2)[:, 0:T], ACT.Copy).then_inc(sm["fy_done"], 1)
            for n in range(2):
                act.wait_ge(sm["mlp_arg"], n + 1)
                A(hdn[:, n, :], sr[:, 0, :], ACT.Sin).then_inc(sm["mlp_sin"], 1)
            for n in range(10):
                act.wait_ge(sm["ks_ps"], n + 1)
                A(KS[:, n // 5, n % 5, :], bank(6 + n % 2), ACT.Copy).then_inc(sm["ks_done"], 1)
            for n in range(2 * TT):
                act.wait_ge(sm["zt_ps"], n + 1)
                A(zt[:, n % TT, :], bank(4 + n % TT), ACT.Copy).then_inc(sm["zt_done"], 1)
            for n, w in ((N_A, 1024), (N_F, 512), (N_H, 512)):
                root(n, w)
            for n in range(4):
                split_high(NT[:, 4 * n:4 * n + 4, :], n, sm["norm_h"], 4 * N_A + n + 1)
            for g in range(4):
                group(Place(G_OUT2 + g))
            root(N_FF2, D)
            shifted_high(XH, lambda k: mod[:, 3 * KC + k, 0:1], N_FF2H)

            def gate_out(q, g, j):
                act.wait_ge(pe_chunk, g.value(4, 4))
                if j.i is not None or j.base >= 1:
                    act.wait_ge(sm["conv_done"], j.value())
                A(GS[:, :, :], acc_ws(q.slot), ACT.Copy).then_inc(acc_free[q.slot], 1)

            def gate_gelu(j):
                act.wait_ge(sm["conv_done"], j.value(1, 1))
                A(CV[:, :, :], CV[:, :, :], ACT.Gelu_apprx_tanh).then_inc(sm["gelu_done"], 1)

            def during_up(q, g, j):
                def hook(s):
                    if s == 0:
                        gate_out(q, g, j)
                    if s == 3:
                        gate_gelu(j)
                return hook

            def hidden_high2(j):
                act.wait_ge(sm["relu_sq"], j.value(1, STEPS1 + 1))
                A(HH[:, j.base % 2], FQ[:, :, :], ACT.Copy).then_inc(sm["hid_hi"], 1)

            def ff2_step(j, first=False):
                g, q = ff2_place(j)
                group(g, lambda s: hidden_high2(Place(0)) if first and s == 1 else None)
                group(g.plus(1), during_up(q, g, j.plus(1)))
                group(g.plus(2), lambda s: hidden_high2(j.plus(1)) if s == 1 else None)

            group(Place(G_FF2))
            group(Place(G_FF2 + 1), during_up(Place(Q_FF2), Place(G_FF2), Place(0)))
            ff2_step(Place(0), first=True)
            ff2_step(Place(1))
            with act.Fori(0, FF2_ITERS) as i:
                ff2_step(Place(2, i, 2))
                ff2_step(Place(3, i, 2))
            group(Place(G_END - 1))
            root(N_LAST, D)

        @block.vector
        def _(dve):
            own = Chain(dve, dve_own)
            V = nc.vector
            stt, tt, ts = V.scalar_tensor_tensor, V.tensor_tensor, V.tensor_scalar

            def low(g, s):
                dve.wait_ge(hi_done, g.value(4, s + 1))
                if g.i is not None or 4 * g.base + s >= 2:
                    dve.wait_ge(pe_chunk, g.value(4, s - 1))
                tt(WL[:, s % 2], RAW[:, s], WH[:, s % 2].bitcast(f32), ALU.subtract).then_inc(lo_done, 1)

            def group(g, after=None):
                for s in range(SLOTS):
                    low(g, s)
                    if after:
                        after(s)

            def squares(src, n, dst=None):
                tt(NT[:, 4 * n:4 * n + 4, :] if dst is None else dst, src, src, ALU.mult)\
                    .then_inc(sm["norm_sq"], 1)

            def inverse_root(n):
                dve.wait_ge(sm["norm_rt"], n + 1)
                own.did(V.reciprocal(rt[:, 0:T], rt[:, 0:T]))
                own.settle()

            def scaled(src, gain, n):
                for k in range(4):
                    ins = stt(NT[:, 4 * n + k, :], src[:, k, :], gain(4 * n + k), rt[:, 0:T], ALU.mult, ALU.mult)
                ins.then_inc(sm["norm_h"], 1)

            def split_low(e, src, n):
                dve.wait_ge(x_hi, 4 * e + n + 1)
                tt(XL[:, 4 * n:4 * n + 4, :], src, XH[:, 4 * n:4 * n + 4, :].bitcast(f32), ALU.subtract)\
                    .then_inc(x_lo, 1)

            def shifted_low(e, hi, lo, shift):
                for n in range(4):
                    dve.wait_ge(x_hi, 4 * e + n + 1)
                    for k in range(4 * n, 4 * n + 4):
                        ins = stt(lo[:, k, :], NT[:, k, :], shift(k), hi[:, k, :].bitcast(f32),
                                  ALU.add, ALU.subtract)
                    ins.then_inc(x_lo, 1)

            def quarter(x, n):
                return x[:, 4 * n:4 * n + 4, :]

            V.memset(epsc[:, :], EPS).then_inc(sm["eps_set"], 1)
            dve.wait_ge(sm["x_in"], 16)
            for n in range(4):
                squares(quarter(X, n), n)
            dve.wait_ge(sm["cols_in"], 16)
            inverse_root(N_IN)
            for n in range(4):
                scaled(quarter(X, n), lambda k: col("g_mix", k), n)
            for n in range(4):
                split_low(E_NORM1, quarter(NT, n), n)
            for g in range(10):
                group(Place(g))
            low(Place(10), 0)
            low(Place(10), 1)

            dve.wait_ge(acc_free[0], 5)
            dve.wait_ge(acc_free[1], 5)
            for n in range(4):
                src = quarter(qT if n < 2 else kT, n % 2)
                gname = "g_q" if n < 2 else "g_k"
                if n >= 1:
                    dve.wait_ge(sm["qk_sum"], 2 * n)
                tt(qk_sq[:, :, :], src, src, ALU.mult).then_inc(sm["qk_sqd"], 1)
                for half in range(2):
                    dve.wait_ge(sm["qk_rt"], 2 * n + half + 1)
                    own.did(V.reciprocal(rt[:, :], rt[:, :]))
                    own.settle()
                    for m in range(2):
                        h = 2 * half + m
                        ins = stt(src[:, h, :], src[:, h, :], col(gname, 4 * (n % 2) + h),
                                  rt[:, m * T:(m + 1) * T], ALU.mult, ALU.mult)
                    ins.then_inc(sm["q_done"], 1)
            dve.wait_ge(sm["mats_in"], 32)
            for h in range(HEADS):
                b = h % 2
                dve.wait_ge(sm["zs_done"], h + 1)
                stt(zneg[:, b, :], zs[:, b, :], -1.0, zs[:, b, :], ALU.mult, ALU.min).then_inc(sm["zneg_done"], 1)
                dve.wait_ge(sm["l_done"], h + 1)
                own.did(stt(lsg[:, b, :], zs[:, b, :], 0.0, zneg[:, b, :], ALU.min, ALU.subtract))
                own.settle()
                own.did(tt(lk[:, b, :], lsg[:, b, :], zs[:, b, :], ALU.subtract))
                own.settle()
                own.did(tt(lk[:, b, 0:P], lk[:, b, 0:P], past, ALU.mult))
                tt(lk[:, b, T:384], lk[:, b, T:384], past, ALU.mult).then_inc(sm["lk_done"], 1)
                dve.wait_ge(sm["cum_done"], h + 1)
                tt(lsg[:, b, :], bank(4 + b)[:, 0:384], lsg[:, b, :], ALU.add).then_inc(sm["la_done"], 1)
                dve.wait_ge(sm["a_done"], h + 1)
                own.did(tt(aw[:, b, 0:P], aw[:, b, 0:P], past, ALU.mult))
                tt(aw[:, b, T:384], aw[:, b, T:384], past, ALU.mult).then_inc(sm["am_done"], 1)
                own.settle()
            dve.wait_ge(sm["ln_in"], 64)
            for t in range(TT):
                for n in range(2):
                    own.did(V.bn_stats(lnst[:, 6 * n:6 * n + 6], vg[:, t, n * 512:(n + 1) * 512]))
                own.settle()
                own.did(V.bn_aggr(smx[:, t, 0:2], lnst[:, 0:12]))
                own.settle()
                V.tensor_copy(lnst[:, 12 + t:13 + t], smx[:, t, 1:2]).then_inc(sm["ln_var"], 1)
                dve.wait_ge(sm["ln_root"], t + 1)
                own.did(V.reciprocal(smx[:, t, 2:3], lnst[:, 14 + t:15 + t]))
                own.settle()
                own.did(ts(vg[:, t, :], vg[:, t, :], smx[:, t, 0:1], smx[:, t, 2:3], ALU.subtract, ALU.mult))
                own.settle()
                own.did(tt(vg[:, t, :], vg[:, t, :], lng[:, :], ALU.mult))
                own.settle()
                tt(vg[:, t, :], vg[:, t, :], lnb[:, :], ALU.add).then_inc(sm["mix_done"], 1)
            V.memset(wsp[CHUNK:P, :, 0:CHUNK], 0.0).then_inc(sm["mix_done"], 1)
            for g in range(8):
                dve.wait_ge(sm["sgu_ps"], g + 1)
                mixed = zs[:, g % 2, 0:T]
                for c in range(TT):
                    own.did(tt(mixed[:, c * P:(c + 1) * P], bank(4 + g % 2)[:, c * P:(c + 1) * P],
                               bsp[:, g, :], ALU.add))
                own.settle()
                tt(uT[:, g, :], uT[:, g, :], mixed, ALU.mult).then_inc(sm["s_done"], 1)
            low(Place(10), 2)
            low(Place(10), 3)
            for g in range(11, N_IN1):
                group(Place(g))
            dve.wait_ge(sm["csig_done"], 1)
            tt(ctmp[:, :, :], col("c", 0, 2 * KC).rearrange("p (a k) -> p a k", a=2), csig[:, :, :], ALU.mult)\
                .then_inc(sm["csil_f"], 1)
            dve.wait_ge(sm["csil_hi"], 1)
            tt(csil[:, :, 2:4], ctmp[:, :, :].rearrange("p a k -> p k a"), csil[:, :, 0:2].bitcast(f32),
               ALU.subtract).then_inc(sm["csil_done"], 1)

            def mod_out(a):
                dve.wait_ge(sm["mt_done"], a.value(1, 1))
                n = a.value(FT)
                dst = mod[:, n:n + FT, :] if a.i is None else mod[:, bass.ds(n, FT), :]
                V.tensor_copy(dst, bank(7)[:, 0:2 * FT].rearrange("p (f c) -> p f c", c=2))\
                    .then_inc(sm["mod_done"], 1)

            group(Place(G_ADA))

            def second_ada(s):
                split_low(E_OAB, quarter(qT if s < 2 else uT, s % 2), s)
                if s == 3:
                    mod_out(Place(0))

            group(Place(G_ADA + 1), second_ada)
            with dve.Fori(0, N_ADA_HEAD // 2 - 1) as i:
                for m in range(2):
                    group(Place(G_ADA + 2 + m, i, 2), lambda s: mod_out(Place(1 + m, i, 2)) if s == 3 else None)
            group(Place(G_OAB), lambda s: mod_out(Place(N_ADA_HEAD - 1)) if s == 3 else None)

            def merge(g):
                q = Place(G_OAB + g)
                dve.wait_ge(pe_chunk, q.value(4, 4))
                tt(quarter(ga, g), acc_ws(q.slot), quarter(ga, g), ALU.mult).then_inc(acc_free[q.slot], 1)
                tt(quarter(gb, g), ctx_ws(g), quarter(gb, g), ALU.mult).then_inc(sm["b_free"], 1)
                dve.wait_ge(acc_free[q.slot], q.half(1))
                dve.wait_ge(sm["b_free"], g + 1)
                tt(quarter(ga, g), quarter(ga, g), quarter(gb, g), ALU.add).then_inc(sm["merged"], 1)

            for g in range(1, 4):
                group(Place(G_OAB + g), lambda s: merge(g - 1) if s == 0 else None)
            merge(3)
            for n in range(4):
                split_low(E_OUT1, quarter(ga, n), n)

            def residual(g):
                q = Place(G_OUT1 + g)
                dve.wait_ge(pe_chunk, q.value(4, 4))
                tt(quarter(X, g), acc_ws(q.slot), quarter(X, g), ALU.add).then_inc(acc_free[q.slot], 1)

            for g in range(4):
                group(Place(G_OUT1 + g), lambda s: residual(g - 1) if s == 0 and g else None)
            residual(3)
            for n in range(4):
                q = Place(G_OUT1 + n)
                dve.wait_ge(acc_free[q.slot], q.half(1))
                squares(quarter(X, n), n)
            inverse_root(N_FF1)
            for n in range(4):
                scaled(quarter(X, n), lambda k: col("g_ff", k), n)
            for n in range(4):
                split_low(E_NORM2, quarter(NT, n), n)

            def relu_squared(q, j):
                dve.wait_ge(acc_free[q.slot], q.half(1))
                if j.i is not None or j.base >= 1:
                    dve.wait_ge(sm["hid_lo"], j.value())
                tt(FQ[:, :, :], FR[:, :, :], FR[:, :, :], ALU.mult).then_inc(sm["relu_sq"], 1)

            def hidden_low(j, before=0):
                dve.wait_ge(sm["hid_hi"], j.value(1, before + 1))
                tt(HL[:, j.base % 2], FQ[:, :, :], HH[:, j.base % 2].bitcast(f32), ALU.subtract)\
                    .then_inc(sm["hid_lo"], 1)

            def down_out(q, g, s):
                dve.wait_ge(pe_chunk, g.value(4, s + 1))
                tt(quarter(X, s), acc_ws(q.plus(s).slot), quarter(X, s), ALU.add)\
                    .then_inc(acc_free[q.plus(s).slot], 1)

            def ff1_step(j, first=False):
                g, q, a = ff1_place(j)

                def during_mod(s):
                    if first:
                        if s == 0:
                            relu_squared(Place(Q_FF1), Place(0))
                        if s == 1:
                            hidden_low(Place(0))
                    elif s == 0:
                        down_out(q.plus(-4), g.plus(-1), 3)

                def during_down(s):
                    if s == 0:
                        relu_squared(q.plus(1), j.plus(1))
                    if s == 1:
                        hidden_low(j.plus(1))
                    if s:
                        down_out(q.plus(2), g.plus(2), s - 1)

                group(g, during_mod)
                group(g.plus(1), lambda s: mod_out(a) if s == 3 else None)
                group(g.plus(2), during_down)

            group(Place(G_FF1))
            ff1_step(Place(0), first=True)
            ff1_step(Place(1))
            with dve.Fori(0, FF1_ITERS) as i:
                ff1_step(Place(2, i, 2))
                ff1_step(Place(3, i, 2))

            g, q = Place(G_FF1_TAIL), Place(Q_FF1_TAIL)

            def ff1_tail(s):
                if s == 0:
                    relu_squared(q, Place(STEPS1 - 1))
                if s == 1:
                    hidden_low(Place(STEPS1 - 1))
                if s:
                    down_out(q.plus(1), g.plus(1), s - 1)

            group(g, lambda s: down_out(q.plus(-4), g.plus(-1), 3) if s == 0 else None)
            group(g.plus(1), ff1_tail)
            group(g.plus(2), lambda s: down_out(q.plus(5), g.plus(2), s - 1) if s else
                  down_out(q.plus(1), g.plus(1), 3))
            down_out(q.plus(5), g.plus(2), 3)

            dve.wait_ge(sm["mod_done"], N_MOD * KC // FT)
            for a in range(2):
                own.did(tt(mod[:, :, a], mod[:, :, a], col("ada_b", 0, N_MOD * KC), ALU.add))
            own.settle()

            def gain_of(a, scale_at, name):
                own.did(stt(gmod[:, :], mod[:, scale_at:scale_at + KC, a], 1.0, col(name, 0, KC),
                            ALU.add, ALU.mult))

            gain_of(1, KC, "norm1")
            own.settle()
            dve.wait_ge(sm["cx_in"], 16)
            for n in range(4):
                squares(quarter(CX, n), n)
            inverse_root(N_CTX)
            for n in range(4):
                scaled(quarter(CX, n), lambda k: gmod[:, k:k + 1], n)
            shifted_low(E_CTX, CH, CL, lambda k: mod[:, k, 1:2])
            gain_of(0, KC, "norm1")
            own.settle()
            dve.wait_ge(x_lo, 4 * E_CTX + 4)
            dve.wait_ge(acc_free[0], Q_IN2 // 2)
            dve.wait_ge(acc_free[1], Q_IN2 // 2)
            for n in range(4):
                squares(quarter(X, n), n)
            inverse_root(N_MIX_IN)
            for n in range(4):
                scaled(quarter(X, n), lambda k: gmod[:, k:k + 1], n)
            shifted_low(E_NORM3, XH, XL, lambda k: mod[:, k, 0:1])
            for n in range(10):
                group(Place(G_IN2 + n))

            dve.wait_ge(sm["bias_done"], 8)
            for u in range(2 * HEADS):
                b, h, t = u % 2, u // 2, u % 2
                dve.wait_ge(sm["sc_done"], u + 1)
                if u >= 2:
                    dve.wait_ge(sm["exp_done"], u - 1)
                own.did(tt(S2[:, b, 0:T].rearrange("p (r c) -> p r c", c=GRID_W),
                           bank(4 + b)[:, 0:T].rearrange("p (r c) -> p r c", c=GRID_W),
                           bia[:, t, ROWS * h:ROWS * h + ROWS, :], ALU.add))
                own.did(V.tensor_copy(S2[:, b, T:2 * T], bank(4 + b)[:, T:2 * T]))
                own.settle()
                own.did(V.reduce_max(smx[:, b, 3:4], S2[:, b, :], AX.X))
                own.settle()
                ts(smx[:, b, 0:1], smx[:, b, 3:4], -1.0, None, ALU.mult).then_inc(sm["sm_done"], 1)
                dve.wait_ge(sm["exp_done"], u + 1)
                own.did(V.reciprocal(smx[:, b, 2:3], smx[:, b, 1:2]))
                own.settle()
                ts(P2[:, b, :], P2[:, b, :], smx[:, b, 2:3], None, ALU.mult).then_inc(sm["pn_done"], 1)
                dve.wait_ge(sm["tp_done"], u + 1)
                if h >= 2:
                    dve.wait_ge(sm["pv2_done"], h - 1)
                V.tensor_copy(PT[:, h % 2, :, t * P:(t + 1) * P],
                              bank(6 + b).rearrange("p (k q) -> p k q", q=P)).then_inc(sm["pt_done"], 1)

            def conv3(dst, src, tiles, w, done_a, done_b, done):
                for k in range(tiles):
                    ins = ts(dst[:, k, :], src[:, k, :], w(1, k), w(3, k), ALU.mult, ALU.add)
                done_a(ins)
                for k in range(tiles):
                    ins = stt(dst[:, k, 1:T], src[:, k, 0:T - 1], w(0, k), dst[:, k, 1:T], ALU.mult, ALU.add)
                done_b(ins)
                for k in range(tiles):
                    ins = stt(dst[:, k, 0:T - 1], src[:, k, 1:T], w(2, k), dst[:, k, 0:T - 1], ALU.mult, ALU.add)
                done(ins)

            def settled(ins):
                own.did(ins)
                own.settle()

            dve.wait_ge(sm["a2_done"], HEADS)
            conv3(hyC, hyT, 12, lambda j, k: col("hy_b", k) if j == 3 else col("hy_w", 12 * j + k),
                  settled, settled, lambda ins: ins.then_inc(sm["hyc_done"], 1))
            C1, C2 = 6.28125, 0.0019340515136718750
            C3 = 2 * math.pi - C1 - C2
            ROUND = 1.5 * 2 ** 23
            for n in range(2):
                dve.wait_ge(sm["mlp_ps"], n + 1)
                if n:
                    dve.wait_ge(sm["mlp_sin"], 1)
                a, r = sr[:, 0, :], sr[:, 1, :]
                settled(ts(a, bank(4 + n)[0:64, 0:T], cols[0:64, COLS["mlp"][0] + n:COLS["mlp"][0] + n + 1],
                           cols[0:64, COLS["mlp"][0] + 2:COLS["mlp"][0] + 3], ALU.add, ALU.mult))
                settled(ts(r, a, 1 / (2 * math.pi), ROUND, ALU.mult, ALU.add))
                settled(ts(r, r, ROUND, None, ALU.subtract))
                for c in (C1, C2, C3):
                    settled(stt(a, r, -c, a, ALU.mult, ALU.add))
                ts(a, a, 3.1415925, -3.1415925, ALU.min, ALU.max).then_inc(sm["mlp_arg"], 1)
            dve.wait_ge(sm["e_in"], 32)
            for n in range(4):
                o, t = n // 2, n % 2
                dve.wait_ge(sm["hf_ps"], n + 1)
                if n:
                    dve.wait_ge(sm["hf_done"], n)
                for f in range(2):
                    own.did(tt(hfb[:, f, :], bank(4 + 2 * (n % 2) + f), dec[:, f, t, :], ALU.mult))
                own.settle()
                own.did(tt(hSD[:, o, 0, t, :], hfb[:, 0, :], hfb[:, 1, :], ALU.add))
                tt(hSD[:, o, 1, t, :], hfb[:, 0, :], hfb[:, 1, :], ALU.subtract).then_inc(sm["hf_done"], 1)
            for o in range(2):
                dve.wait_ge(sm["zf_ps"], o + 1)
                dve.wait_ge(sm["ks_done"], 10)
                dve.wait_ge(sm["hf_done"], 4)
                if o:
                    dve.wait_ge(sm["ys_done"], o)
                    dve.wait_ge(sm["hz_done"], o)
                re, im = PS[:, 0:2, :], PS[:, 2:4, :]
                own.did(tt(pp[:, 0], re, KS[:, o, 0:2, :], ALU.mult))
                own.did(tt(pp[:, 1], im, KS[:, o, 2:4, :], ALU.mult))
                own.settle()
                own.did(tt(YS[:, 0:2, :], pp[:, 0], pp[:, 1], ALU.subtract))
                own.settle()
                own.did(tt(pp[:, 0], re, KS[:, o, 2:4, :], ALU.mult))
                own.did(tt(pp[:, 1, 0, :], bank(2), KS[:, o, 4, :], ALU.mult))
                own.did(tt(pp[:, 1, 1, :], bank(3), KS[:, o, 1, :], ALU.mult))
                own.settle()
                tt(YS[:, 2:4, :], pp[:, 0], pp[:, 1], ALU.add).then_inc(sm["ys_done"], 1)
                dve.wait_ge(sm["yi_ps"], o + 1)
                dve.wait_ge(sm["ys_done"], o + 1)
                src = hyC[:, 0:HT, :] if o == 0 else zT2
                gate = hyC[:, HT * (o + 1):HT * (o + 2), :]
                dst = zT2 if o == 0 else gate
                tmp = pp[:, 0].rearrange("p a (b t) -> p (a b) t", t=T)
                for k in range(HT):
                    own.did(stt(tmp[:, k, :], src[:, k, :], col("hy_bias", HT * o + k),
                                bank(6 + k // 2)[:, (k % 2) * T:(k % 2 + 1) * T], ALU.mult, ALU.add))
                own.settle()
                tt(dst[:, 0:HT, :], tmp, gate, ALU.mult).then_inc(sm["hz_done"], 1)
            dve.wait_ge(sm["hz_done"], 2)
            dve.wait_ge(sm["fy_done"], FNG)
            mixed = [quarter(q2, 0), quarter(q2, 1), fY[:, :, :], quarter(hyC, 2)]
            for n in range(4):
                squares(mixed[n], n)
            inverse_root(N_A)
            scaled(mixed[0], lambda k: col("mix", k), 0)
            scaled(mixed[1], lambda k: col("mix", k), 1)
            inverse_root(N_F)
            scaled(mixed[2], lambda k: col("mix", k), 2)
            inverse_root(N_H)
            scaled(mixed[3], lambda k: col("mix", k), 3)
            for n in range(4):
                split_low(E_OUT2, quarter(NT, n), n)

            def residual2(g):
                q = Place(Q_OUT2 + g)
                dve.wait_ge(pe_chunk, 4 * (G_OUT2 + g) + 4)
                for k in range(4):
                    ins = stt(X[:, 4 * g + k, :], acc_ws(q.slot)[:, k, :], mod[:, 2 * KC + 4 * g + k, 0:1],
                              X[:, 4 * g + k, :], ALU.mult, ALU.add)
                ins.then_inc(acc_free[q.slot], 1)

            for g in range(4):
                group(Place(G_OUT2 + g), lambda s: residual2(g - 1) if s == 0 and g else None)
            residual2(3)
            gain_of(0, 4 * KC, "norm2")
            for n in range(4):
                q = Place(Q_OUT2 + n)
                dve.wait_ge(acc_free[q.slot], q.half(1))
                squares(quarter(X, n), n)
            inverse_root(N_FF2)
            for n in range(4):
                scaled(quarter(X, n), lambda k: gmod[:, k:k + 1], n)
            shifted_low(E_NORM4, XH, XL, lambda k: mod[:, 3 * KC + k, 0:1])

            def gate_conv(q, j, s):
                w = lambda n, k: cw[:, 4 * k + n:4 * k + n + 1]
                if s == 0:
                    c0 = j.value(4 * FT, COLS["ff_w"][0])
                    src = cols[:, c0:c0 + 4 * FT] if j.i is None else cols[:, bass.ds(c0, 4 * FT)]
                    V.tensor_copy(cw[:, :], src).then_inc(sm["cw_done"], 1)
                    dve.wait_ge(acc_free[q.slot], q.half(1))
                    dve.wait_ge(sm["cw_done"], j.value(1, 1))
                    for k in range(FT):
                        ins = ts(CV[:, k, :], GS[:, k, :], w(1, k), w(3, k), ALU.mult, ALU.add)
                    ins.then_inc(sm["conv_a"], 1)
                if s == 1:
                    dve.wait_ge(sm["conv_a"], j.value(1, 1))
                    for k in range(FT):
                        ins = stt(CV[:, k, 1:T], GS[:, k, 0:T - 1], w(0, k), CV[:, k, 1:T], ALU.mult, ALU.add)
                    ins.then_inc(sm["conv_b"], 1)
                if s == 2:
                    dve.wait_ge(sm["conv_b"], j.value(1, 1))
                    for k in range(FT):
                        ins = stt(CV[:, k, 0:T - 1], GS[:, k, 1:T], w(2, k), CV[:, k, 0:T - 1], ALU.mult, ALU.add)
                    ins.then_inc(sm["conv_done"], 1)

            def gated(q, g, j):
                dve.wait_ge(pe_chunk, g.value(4, 4))
                dve.wait_ge(sm["gelu_done"], j.value(1, 1))
                dve.wait_ge(sm["hid_lo"], j.value(1, STEPS1))
                tt(FQ[:, :, :], acc_ws(q.slot), CV[:, :, :], ALU.mult).then_inc(acc_free[q.slot], 1)
                dve.wait_ge(acc_free[q.slot], q.half(1))
                V.tensor_copy(lnst[0:1, 0:1], FQ[0:1, 0, 0:1]).then_inc(sm["relu_sq"], 1)

            def down_out2(q, g, s):
                dve.wait_ge(pe_chunk, g.value(4, s + 1))
                sl = q.plus(s).slot
                for k in range(4):
                    ins = stt(X[:, 4 * s + k, :], acc_ws(sl)[:, k, :], mod[:, 5 * KC + 4 * s + k, 0:1],
                              X[:, 4 * s + k, :], ALU.mult, ALU.add)
                ins.then_inc(acc_free[sl], 1)

            def ff2_step(j, first=False):
                g, q = ff2_place(j)

                def during_gate(s):
                    if first:
                        if s == 0:
                            gated(Place(Q_FF2 + 1), Place(G_FF2 + 1), Place(0))
                        if s == 1:
                            hidden_low(Place(0), STEPS1)
                    elif s == 0:
                        down_out2(q.plus(-4), g.plus(-1), 3)

                def during_down(s):
                    if s == 0:
                        gated(q.plus(1), g.plus(1), j.plus(1))
                    if s == 1:
                        hidden_low(j.plus(1), STEPS1)
                    if s:
                        down_out2(q.plus(2), g.plus(2), s - 1)

                group(g, during_gate)
                group(g.plus(1), lambda s: gate_conv(q, j.plus(1), s))
                group(g.plus(2), during_down)

            group(Place(G_FF2))
            group(Place(G_FF2 + 1), lambda s: gate_conv(Place(Q_FF2), Place(0), s))
            ff2_step(Place(0), first=True)
            ff2_step(Place(1))
            with dve.Fori(0, FF2_ITERS) as i:
                ff2_step(Place(2, i, 2))
                ff2_step(Place(3, i, 2))
            g, q = Place(G_END - 1), Place(Q_END - 4)
            group(g, lambda s: down_out2(q, g, s - 1) if s else down_out2(q.plus(-4), g.plus(-1), 3))
            down_out2(q, g, 3)
            for n in range(4):
                sl = q.plus(n)
                dve.wait_ge(acc_free[sl.slot], sl.half(1))
                squares(quarter(X, n), n)
            inverse_root(N_LAST)
            for n in range(4):
                scaled(quarter(X, n), lambda k: col("final", k), n)

        @block.tensor
        def _(pe):
            MM = nc.tensor.matmul

            def chunk_ready(g, s):
                pe.wait_ge(lo_done, g.value(4, s + 1))

            def use(q):
                if q.i is not None or q.base >= 2:
                    pe.wait_ge(acc_free[q.slot], q.half())

            def ws(out, k, s, xh, xl, first, last, kk):
                for f in range(FT):
                    cs = slice(f * P, (f + 1) * P)
                    wh, wl = WH[:, s % 2, kk, cs], WL[:, s % 2, kk, cs]
                    MM(out[:, f, :], wh, xh, start=first and f % 2 == 0, stop=False, skip_group_check=True)
                    MM(out[:, f, :], wh, xl, start=False, stop=False, skip_group_check=True)
                    ins = MM(out[:, f, :], wl, xh, start=False, stop=last, skip_group_check=True)
                return ins

            def tok(out, k, s, xh, xl, first, last, kk):
                wh, wl = WH[:, s % 2, kk, :], WL[:, s % 2, kk, :]
                for t in range(TT):
                    h, l = xh[:, t * P:(t + 1) * P], xl[:, t * P:(t + 1) * P]
                    MM(out[:, t, :], h, wh, start=first, stop=False)
                    MM(out[:, t, :], h, wl, start=False, stop=False)
                    ins = MM(out[:, t, :], l, wh, start=False, stop=last)
                return ins

            def wide(g, q, token=False, e=None, ctx_n=None, after=None):
                for s in range(SLOTS):
                    chunk_ready(g, s)
                    if s == 0:
                        use(q)
                    if e is not None:
                        pe.wait_ge(x_lo, 4 * e + s + 1)
                    out = acc_as(q.slot) if token else acc_ws(q.slot)
                    for kk in range(FT):
                        k = 4 * s + kk
                        if ctx_n is not None:
                            o2 = ctx_as(ctx_n) if token else ctx_ws(ctx_n)
                            (tok if token else ws)(o2, k, s, CH[:, k, :], CL[:, k, :], k == 0, k == KC - 1, kk)
                        ins = (tok if token else ws)(out, k, s, XH[:, k, :], XL[:, k, :], k == 0, k == KC - 1, kk)
                    ins.then_inc(pe_chunk, 1)
                    if after:
                        after(s)

            def down(g, q, j, before=0):
                par = j.base % 2
                for s in range(SLOTS):
                    chunk_ready(g, s)
                    use(q.plus(s))
                    if s == 0:
                        pe.wait_ge(sm["hid_lo"], j.value(1, before + 1))
                    out = acc_ws(q.plus(s).slot)
                    for kk in range(FT):
                        ins = ws(out, kk, s, HH[:, par, kk, :], HL[:, par, kk, :], kk == 0, kk == FT - 1, kk)
                    ins.then_inc(pe_chunk, 1)

            def ada(g, q, after=None):
                for s in range(SLOTS):
                    chunk_ready(g, s)
                    if s == 0:
                        use(q)
                    for kk in range(FT):
                        k = 4 * s + kk
                        out = acc_as(q.slot)[0:4, 0, :]
                        MM(out, csil[:, k, :], WH[:, s % 2, kk, :], start=k == 0, stop=False)
                        ins = MM(out, csil[:, k, :], WL[:, s % 2, kk, :], start=False, stop=k == KC - 1)
                    ins.then_inc(pe_chunk, 1)
                    if after:
                        after(s)

            def mod_columns(q, a):
                pe.wait_ge(acc_free[q.slot], q.half(1))
                if a.i is not None or a.base >= 1:
                    pe.wait_ge(sm["mod_done"], a.value())
                for f in range(FT):
                    ins = MM(bank(7)[:, 2 * f:2 * f + 2], MR[:, f * P:(f + 1) * P], sel[:, :], start=True, stop=True)
                ins.then_inc(sm["mt_done"], 1)

            def norm_sum(norm, first_q, tiles, free=None):
                if norm:
                    pe.wait_ge(sm["norm_rt"], norm)
                for k in range(tiles):
                    if k % 4 == 0:
                        pe.wait_ge(sm["norm_sq"], first_q + k // 4 + 1)
                    kk = 4 * (first_q % 4) + k
                    ins = MM(bank(4)[:, 0:T], ones, NT[:, kk, :], start=k == 0, stop=k == tiles - 1)
                ins.then_inc(sm["norm_sum"], 1)

            pe.wait_ge(sm["mats_in"], 32)
            norm_sum(N_IN, 0, KC)
            for g in range(10):
                wide(Place(g), Place(g), token=g in (4, 5, 8, 9), e=E_NORM1 if g == 0 else None)
            for n in range(4):
                pe.wait_ge(sm["qk_sqd"], n + 1)
                for half in range(2):
                    if n:
                        pe.wait_ge(sm["qk_rt"], 2 * n + half - 1)
                    MM(bank(4 + half), ones, qk_sq[:, 2 * half:2 * half + 2, :], start=True, stop=True)\
                        .then_inc(sm["qk_sum"], 1)

            def scores(h):
                b = h % 2
                if h == 0:
                    pe.wait_ge(sm["q_done"], 8)
                if h >= 2:
                    pe.wait_ge(sm["la_done"], h - 1)
                MM(bank(4 + b)[:, 0:T], kT[:, h, 0:P], qT[:, h, :], start=True, stop=True)
                MM(bank(4 + b)[:, T:384], kT[:, h, P:T], qT[:, h, P:T], start=True, stop=True)\
                    .then_inc(sm["z_done"], 1)

            scores(0)
            scores(1)
            for h in range(HEADS):
                b = h % 2
                pe.wait_ge(sm["lk_done"], h + 1)
                MM(bank(4 + b)[:, 0:384], lower, lk[:, b, :], start=True, stop=False)
                MM(bank(4 + b)[:, P:T], ones, lk[:, b, T:384], start=False, stop=True).then_inc(sm["cum_done"], 1)
                pe.wait_ge(sm["am_done"], h + 1)
                if h >= 2:
                    pe.wait_ge(sm["o_done"], h - 1)
                c = slice(h * DH, (h + 1) * DH)
                MM(bank(6 + b)[:, 0:T], v1[:, 0, c], aw[:, b, 0:T], start=True, stop=False)
                MM(bank(6 + b)[:, P:T], v1[:, 1, c], aw[:, b, T:384], start=False, stop=True)\
                    .then_inc(sm["pv_done"], 1)
                if h + 2 < HEADS:
                    scores(h + 2)
            pe.wait_ge(sm["mix_done"], TT + 1)
            for g in range(8):
                if g >= 2:
                    pe.wait_ge(sm["s_done"], g - 1)
                for c in range(TT):
                    ins = MM(bank(4 + g % 2)[:, c * P:(c + 1) * P], vg[:, c, g * P:(g + 1) * P], wsp[:, g, :],
                             start=True, stop=True)
                ins.then_inc(sm["sgu_ps"], 1)
            for g in range(10, N_IN1):
                wide(Place(g), Place(g))
            pe.wait_ge(sm["csil_done"], 1)
            ada(Place(G_ADA), Place(G_ADA))
            ada(Place(G_ADA + 1), Place(G_ADA + 1),
                lambda s: mod_columns(Place(G_ADA), Place(0)) if s == 1 else None)
            with pe.Fori(0, N_ADA_HEAD // 2 - 1) as i:
                for m in range(2):
                    g = Place(G_ADA + 2 + m, i, 2)
                    ada(g, g, lambda s: mod_columns(g.plus(-1), Place(1 + m, i, 2)) if s == 1 else None)
            for n in range(4):
                g = Place(G_OAB + n)
                for s in range(SLOTS):
                    chunk_ready(g, s)
                    if s == 0:
                        use(g)
                        if n == 0:
                            pe.wait_ge(x_lo, 4 * E_OAB + 4)
                        if n == 1:
                            pe.wait_ge(sm["mod_done"], N_ADA_HEAD)
                        if n >= 2:
                            pe.wait_ge(sm["b_free"], n - 1)
                    out = acc_ws(g.slot) if s < 2 else ctx_ws(n)
                    for kk in range(FT):
                        k = 4 * s + kk
                        ins = ws(out, k, s, XH[:, k, :], XL[:, k, :], k % 8 == 0, k % 8 == 7, kk)
                    ins.then_inc(pe_chunk, 1)
                    if n == 0 and s == 1:
                        mod_columns(Place(G_OAB - 1), Place(N_ADA_HEAD - 1))
            for n in range(4):
                wide(Place(G_OUT1 + n), Place(G_OUT1 + n), e=E_OUT1 if n == 0 else None)
            norm_sum(N_FF1, 4, KC)

            def ff1_step(j):
                g, q, a = ff1_place(j)
                ada(g, q)
                wide(g.plus(1), q.plus(1), after=lambda s: mod_columns(q, a) if s == 1 else None)
                down(g.plus(2), q.plus(2), j)

            wide(Place(G_FF1), Place(Q_FF1), e=E_NORM2)
            ff1_step(Place(0))
            ff1_step(Place(1))
            with pe.Fori(0, FF1_ITERS) as i:
                ff1_step(Place(2, i, 2))
                ff1_step(Place(3, i, 2))
            wide(Place(G_FF1_TAIL), Place(Q_FF1_TAIL))
            down(Place(G_FF1_TAIL + 1), Place(Q_FF1_TAIL + 1), Place(STEPS1 - 2))
            down(Place(G_FF1_TAIL + 2), Place(Q_FF1_TAIL + 5), Place(STEPS1 - 1))

            norm_sum(N_CTX, 8, KC)
            norm_sum(N_MIX_IN, 12, KC)
            pe.wait_ge(sm["mod_done"], N_MOD * KC // FT)
            pe.wait_ge(sm["norm_rt"], N_MIX_IN + 1)
            pe.wait_ge(x_lo, 4 * E_CTX + 4)
            for n in range(10):
                if 2 <= n < 4:
                    pe.wait_ge(sm["ctx_free"], n - 1)
                wide(Place(G_IN2 + n), Place(Q_IN2 + n), token=n in (2, 3, 6), e=E_NORM3 if n == 0 else None,
                     ctx_n=n if n < 4 else None)
            pe.wait_ge(sm["ctx_free"], 4)
            pe.wait_ge(sm["brow_in"], 16)
            pe.wait_ge(sm["bsel_in"], 16)
            for n in range(8):
                if n >= 4:
                    pe.wait_ge(sm["bias_done"], n - 3)
                for c in range(8):
                    ins = MM(bank(4 + n % 4)[:, c * 64:(c + 1) * 64], bsel[:, 8 * n + c, :], brow[:, :],
                             start=True, stop=True)
                ins.then_inc(sm["bias_ps"], 1)

            def scores2(u):
                b, h, t = u % 2, u // 2, u % 2
                if u >= 2:
                    pe.wait_ge(sm["sm_done"], u - 1)
                qs = q2[:, h, t * P:(t + 1) * P]
                MM(bank(4 + b)[:, 0:T], qs, k2[:, h, :], start=True, stop=True)
                MM(bank(4 + b)[:, T:2 * T], qs, kc2[:, h, :], start=True, stop=True).then_inc(sm["sc_done"], 1)

            pe.wait_ge(sm["q2_done"], 1)
            pe.wait_ge(sm["bias_done"], 8)
            scores2(0)
            scores2(1)
            for u in range(2 * HEADS):
                b, h = u % 2, u // 2
                pe.wait_ge(sm["pn_done"], u + 1)
                if u >= 2:
                    pe.wait_ge(sm["pt_done"], u - 1)
                for k in range(4):
                    ins = nc.tensor.transpose(bank(6 + b)[:, k * P:(k + 1) * P], P2[:, b, k * P:(k + 1) * P], ident)
                ins.then_inc(sm["tp_done"], 1)
                if u + 2 < 2 * HEADS:
                    scores2(u + 2)
                if b == 1:
                    pe.wait_ge(sm["pt_done"], u + 1)
                    if h >= 2:
                        pe.wait_ge(sm["a2_done"], h - 1)
                    c = slice(h * DH, (h + 1) * DH)
                    for k in range(4):
                        ins = MM(bank(2 * (h % 2))[:, 0:T], (v2 if k < 2 else vc2)[:, k % 2, c], PT[:, h % 2, k, :],
                                 start=k == 0, stop=k == 3)
                    ins.then_inc(sm["pv2_done"], 1)
            pe.wait_ge(sm["four_in"], 32)
            for n in range(FNG):
                if n >= 2:
                    pe.wait_ge(sm["fu_done"], n - 1)
                for t in range(TT):
                    ins = MM(bank(4 + n % 2), fX[:, t, n * P:(n + 1) * P], fcl[:, t, :], start=t == 0, stop=t == 1)
                ins.then_inc(sm["fu_ps"], 1)
            for n in range(FNG):
                pe.wait_ge(sm["fu_done"], n + 1)
                if n >= 2:
                    pe.wait_ge(sm["fy_done"], n - 1)
                for m in range(2):
                    ins = MM(bank(6 + n % 2)[:, 0:T], fcd[:, m, :], fU[:, n, m * T:(m + 1) * T],
                             start=m == 0, stop=m == 1)
                ins.then_inc(sm["fy_ps"], 1)
            pe.wait_ge(sm["mlp_in"], 48)
            pe.wait_ge(sm["fu_done"], FNG)
            MM(bank(4)[0:64, 0:T], w1h[:, :], pz[:, :], start=True, stop=True).then_inc(sm["mlp_ps"], 1)
            pe.wait_ge(sm["mlp_sin"], 1)
            MM(bank(5)[0:64, 0:T], w2h[:, :], hdn[:, 0, :], start=True, stop=True).then_inc(sm["mlp_ps"], 1)
            pe.wait_ge(sm["mlp_sin"], 2)
            pe.wait_ge(sm["mlp3_in"], 16)
            pe.wait_ge(sm["fy_done"], FNG)
            for n in range(4):
                o, t = n // 2, n % 2
                if n >= 2:
                    pe.wait_ge(sm["hf_done"], n - 1)
                for f in range(2):
                    c0 = o * 2 * HW + f * HW
                    ins = MM(bank(4 + 2 * (n % 2) + f), hdn[:, 1, t * P:(t + 1) * P], w3h[:, c0:c0 + HW],
                             start=True, stop=True)
                ins.then_inc(sm["hf_ps"], 1)
            pe.wait_ge(sm["hf_done"], 4)
            pe.wait_ge(sm["e_in"], 32)
            for n in range(10):
                o, m = n // 5, n % 5
                if n >= 2:
                    pe.wait_ge(sm["ks_done"], n - 1)
                e0 = (0, P, 2 * P, 3 * P, 5 * P)[m]
                for t in range(TT):
                    ins = MM(bank(6 + n % 2), Ef[:, t, e0:e0 + P], hSD[:, o, 1 if m in (2, 3) else 0, t, :],
                             start=t == 0, stop=t == 1)
                ins.then_inc(sm["ks_ps"], 1)
            pe.wait_ge(sm["hyc_done"], 1)
            pe.wait_ge(sm["gi_in"], 16)
            pe.wait_ge(sm["ks_done"], 10)
            for o in range(2):
                if o:
                    pe.wait_ge(sm["hz_done"], 1)
                src = hyC if o == 0 else zT2
                for t in range(TT):
                    for k in range(HT):
                        ins = nc.tensor.transpose(bank(4 + t)[:, k * P:(k + 1) * P], src[:, k, t * P:(t + 1) * P],
                                                  ident)
                    ins.then_inc(sm["zt_ps"], 1)
                pe.wait_ge(sm["zt_done"], TT * (o + 1))
                for w, e0 in enumerate((0, P, 4 * P, 3 * P)):
                    for t in range(TT):
                        ins = MM(bank(w), Ef[:, t, e0:e0 + P], zt[:, t, :], start=t == 0, stop=t == 1)
                ins.then_inc(sm["zf_ps"], 1)
                pe.wait_ge(sm["ys_done"], o + 1)
                for k in range(HT):
                    for w in range(4):
                        ins = MM(bank(6 + k // 2)[:, (k % 2) * T:(k % 2 + 1) * T], YS[:, w, k * P:(k + 1) * P],
                                 Gi[:, w, :], start=w == 0, stop=w == 3)
                ins.then_inc(sm["yi_ps"], 1)
            norm_sum(N_A, 16, 8)
            norm_sum(N_F, 18, 4)
            norm_sum(N_H, 19, 4)
            for n in range(4):
                wide(Place(G_OUT2 + n), Place(Q_OUT2 + n), e=E_OUT2 if n == 0 else None)
            norm_sum(N_FF2, 20, KC)

            def ff2_step(j):
                g, q = ff2_place(j)
                wide(g, q)
                wide(g.plus(1), q.plus(1))
                down(g.plus(2), q.plus(2), j, STEPS1)

            wide(Place(G_FF2), Place(Q_FF2), e=E_NORM4)
            wide(Place(G_FF2 + 1), Place(Q_FF2 + 1))
            ff2_step(Place(0))
            ff2_step(Place(1))
            with pe.Fori(0, FF2_ITERS) as i:
                ff2_step(Place(2, i, 2))
                ff2_step(Place(3, i, 2))
            down(Place(G_END - 1), Place(Q_END - 4), Place(STEPS2 - 1), STEPS1)
            norm_sum(N_LAST, 24, KC)


def shape_constants():
    f = np.float32
    out = {}
    r = np.arange(P)
    out["mats"] = np.stack([np.ones((P, P)), np.eye(P), r[:, None] > r[None, :], r[:, None] < r[None, :]], 1).astype(f)
    out["sel"] = np.array([[1, 0], [0, 1], [1, 0], [0, 1]], f)
    s = np.zeros((2, 32, GRID_W, 2, GRID_W), f)
    for c in range(GRID_W):
        c0 = min(max(c - NA_KW // 2, 0), GRID_W - NA_KW)
        for k in range(GRID_W):
            row = k - c + NA_KW - 1 if c0 <= k < c0 + NA_KW else 31
            for half in range(2):
                s[half, row, k, half, c] = 1
    out["bsel"] = s.reshape(64, GRID_W, P)
    tok = 2 * np.pi * np.outer(np.arange(T), np.arange(T)) / T
    cl = np.concatenate([np.cos(tok), np.sin(tok)], 1) / np.sqrt(T)
    out["fcl"] = cl.reshape(TT, P, 2 * T).transpose(1, 0, 2).astype(f)
    ch = 2 * np.pi * np.outer(r, r) / P
    out["fcd"] = (np.stack([np.cos(ch), -np.sin(ch)], 1) / np.sqrt(P)).astype(f)
    t = np.arange(T)
    ang = 2 * np.pi * np.outer(t, np.arange(T)) / L2
    cos, sin = np.cos(ang), -np.sin(ang)
    alt = (-1.0) ** t
    im0, re0 = sin[:, :P].copy(), cos[:, :P].copy()
    im0[:, 0] = alt
    re0[:, 0] = alt
    ef = np.concatenate([cos, sin, im0, re0], 1)
    out["ef"] = ef.reshape(TT, P, 6 * P).transpose(1, 0, 2).astype(f)
    g = np.concatenate([cos.T * 2, sin.T * 2], 0) / L2
    g[0] /= 2
    g[T] = alt / L2
    out["gi"] = g.reshape(4, P, T).transpose(1, 0, 2).astype(f)
    pos = np.arange(T, dtype=f)[:, None]
    tn = pos / f(T - 1)
    bands = np.linspace(1e-4, 15, 16, dtype=f)
    a = (bands * f(2.0 * math.pi / T)).astype(f) * pos
    out["pz"] = np.ascontiguousarray(np.concatenate([tn, np.cos(a), -np.sin(a)], 1).T.astype(f))
    deltas = np.linspace(math.log(1e-2) / 1.5, math.log(1e-2) / 0.3, HW, dtype=f)
    decay = np.exp(-tn * np.abs(deltas)).astype(f)
    back = decay.copy()
    back[0] = 0
    out["dec"] = np.stack([decay, back]).reshape(2, TT, P, HW).transpose(2, 0, 1, 3)
    return out


def lay_out(v):
    def columns(a):
        return np.asarray(a).reshape(-1, P).T

    def padded(a):
        return np.concatenate([a, np.zeros((P - a.shape[0], a.shape[1]), a.dtype)], 0)

    a = {k: v[k][0] for k in ("w_in", "w_oa", "w_ob", "w_out", "w_ff1", "w_ff2", "w_in_2", "w_out_2")}
    a["ada_w"], a["w_up"], a["w_down"] = v["ada_w_2"][0], v["ffn_w_up_2"][0], v["ffn_w_down_2"][0]
    a["hy_w1"], a["hy_w2"], a["hy_w3"] = v["hy_w1_2"][0], v["hy_w2_2"][0], v["hy_w3_2"][0]
    a["x"], a["ctx"] = v["x"][0].T, v["ctx_2"][0].T
    ffw = np.concatenate([v["ffn_conv_w_2"][0], v["ffn_conv_b_2"]], 0)
    ffw = ffw.reshape(4, STEPS2, FT, P).transpose(3, 1, 2, 0).reshape(P, -1)
    parts = dict(g_mix=columns(v["g_mix"]), g_q=columns(v["g_q"]), g_k=columns(v["g_k"]), g_ff=columns(v["g_ff"]),
                 norm1=columns(v["norm1_g_2"]), norm2=columns(v["norm2_g_2"]), mix=columns(v["mix_norm_g_2"]),
                 final=columns(v["final_norm_g_2"]), ada_b=columns(v["ada_b_2"]), hy_w=columns(v["hy_conv_w_2"]),
                 hy_b=columns(v["hy_conv_b_2"]), hy_bias=columns(v["hy_bias_2"]), ff_w=ffw,
                 c=np.concatenate([columns(v["c_2"]), columns(v["c_ctx_2"])], 1),
                 mlp=padded(np.stack([v["hy_b1_2"][0], v["hy_b2_2"][0], v["hy_freq_2"][0]], 1)))
    assert all(parts[n].shape[1] == w for n, (_, w) in COLS.items())
    a["cols"] = np.concatenate([parts[n] for n in COLS], 1)
    a["ln_g"] = np.broadcast_to(v["sgu_ln_g"], (P, 1024))
    a["ln_b"] = np.broadcast_to(v["sgu_ln_b"], (P, 1024))
    a["b_sp"] = np.broadcast_to(v["b_spatial"], (P, 8, P))
    a["w_sp"] = v["w_spatial"][0].transpose(2, 0, 1)
    rpb = v["na_rpb_2"][0]
    rows = [[[NA_KH - 1 + r - (2 * t + half) for r in range(ROWS)] for t in range(TT)] for half in range(2)]
    b = rpb[:, np.array(rows), :].transpose(1, 4, 2, 0, 3)
    neg = np.full((2, 1) + b.shape[2:], NEG, b.dtype)
    a["brow"] = np.concatenate([b, neg], 1).reshape(64, 64)
    a.update(shape_constants())
    return {k: np.ascontiguousarray(x) for k, x in a.items()}


def kernel(**inputs):
    import concourse.bacc as bacc
    from concourse.bass_utils import run_bass_kernel_spmd

    nc = bacc.Bacc("TRN2", target_bir_lowering=False, num_devices=1)
    arrays = lay_out({k: np.asarray(x) for k, x in inputs.items()})
    d = {k: nc.dram_tensor("in_" + k, a.shape, mybir.dt.from_np(a.dtype), kind="ExternalInput").ap()
         for k, a in arrays.items()}
    out = nc.dram_tensor("out", (D, T), mybir.dt.float32, kind="ExternalOutput").ap()
    build_program(nc, d, out)
    r = run_bass_kernel_spmd(nc, [{"in_" + k: a for k, a in arrays.items()}], core_ids=[0])
    return np.ascontiguousarray(r.results[0]["out"].T)[None]
```

```python
import math
import numpy as np
import concourse.bass as bass
from concourse import mybir
from contextlib import ExitStack

P = 128
T = 256
TT = T // P
D = 2048
KC = D // P
NB = 512
FT = NB // P
SLOTS = 4
HEADS = 8
DH = 128
CHUNK = 64
GRID_W, NA_KH, NA_KW = 64, 8, 16
ROWS = T // GRID_W
FNG = 4
HW = 512
HT = HW // P
D_FF1, D_FF2 = 8192, 5632
STEPS1, STEPS2 = D_FF1 // NB, D_FF2 // NB
N_MOD = 6
EPS = 1e-6
NEG = -1e30
SCALE = DH ** -0.5
L2 = 2 * T

COLS = {}
_n = 0
for _name, _w in [("g_mix", KC), ("g_q", HEADS), ("g_k", HEADS), ("g_ff", KC), ("norm1", KC), ("norm2", KC),
                  ("mix", KC), ("final", KC), ("ada_b", N_MOD * KC), ("hy_w", 3 * 12), ("hy_b", 12),
                  ("hy_bias", 2 * HT), ("ff_w", STEPS2 * 4 * FT), ("c", 2 * KC), ("mlp", 3)]:
    COLS[_name] = (_n, _w)
    _n += _w
NCOLS = _n

STEP1, STEP2 = 2 * SLOTS, 3 * SLOTS
C_VG, C_U, C_Q, C_K, C_V = 0, 8, 16, 24, 32
C_GATE = 40
C_OAB = C_GATE + 2 * 8 * SLOTS
C_OUT1 = C_OAB + 4 * SLOTS
C_FF1 = C_OUT1 + 4 * SLOTS
C_FF1_STEPS = C_FF1 + SLOTS
FF1_ITERS = (STEPS1 - 4) // 2
C_FF1_TAIL = C_FF1_STEPS + STEP1 * (STEPS1 - 2)
C_IN2 = C_FF1_TAIL + 3 * SLOTS
C_OUT2 = C_IN2 + 10 * SLOTS
C_FF2 = C_OUT2 + 4 * SLOTS
C_FF2_STEPS = C_FF2 + 2 * SLOTS
FF2_ITERS = (STEPS2 - 3) // 2
C_END = C_FF2 + STEP2 * STEPS2
Q_GATE, Q_OAB, Q_OUT1, Q_FF1 = 10, 18, 22, 26
Q_FF1_TAIL = Q_FF1 + 1 + 5 * (STEPS1 - 2)
Q_IN2 = Q_FF1_TAIL + 9
Q_OUT2 = Q_IN2 + 10
Q_FF2 = Q_OUT2 + 4
Q_END = Q_FF2 + 6 * STEPS2
ADA_GATE = 8
ADA_GROUPS = N_MOD * KC // FT
ADA_TAIL = [n * 11 // 16 for n in range(16)]
IN1_COLS = [4096, 4608, 3072, 3584, 0, 512, 1024, 1536, 2048, 2560]
GATE_COL = 5120
IN2_COLS = [1024, 1536, 2048, 2560, 0, 512, 3072, 3584, 4096, 4608]
T_LN, T_SGU, T_QK, T_ATT, S_ATT = 10, 20, 22, 39, 8
T_BIAS, T_ATT2 = 17, 24
E_NORM1, E_OAB, E_OUT1, E_NORM2, E_CTX, E_NORM3, E_OUT2, E_NORM4 = range(8)


class Place:

    def __init__(self, base, i=None, per=0):
        self.base, self.i, self.per = base, i, per

    def plus(self, n):
        return Place(self.base + n, self.i, self.per)

    def value(self, mul=1, plus=0):
        v = self.base * mul + plus
        return v if self.i is None else self.i * (self.per * mul) + v

    def turns(self, n, plus=0, mul=1):
        v = (self.base // n + plus) * mul
        return v if self.i is None else self.i * (self.per // n * mul) + v

    def since(self, n):
        return self.i is not None or self.base >= n

    @property
    def slot(self):
        return self.base % 2


class Chain:

    def __init__(self, eng, sem):
        self.eng, self.sem, self.n = eng, sem, 0

    def did(self, ins):
        ins.then_inc(self.sem, 1)
        self.n += 1

    def settle(self):
        self.eng.wait_ge(self.sem, self.n)


N_IN, N_FF1, N_CTX, N_MIX_IN, N_A, N_F, N_H, N_FF2, N_LAST = range(9)
QUARTERS = [0, 4, 8, 12, 16, 18, 19, 20, 24]
PARTS = [(0, 3), (0, 3), (0,), (0, 2, 3), (0,), (2,), (3,), (0, 3), (0, 2, 3)]
PARTS_BEFORE = [sum(len(p) for p in PARTS[:n]) for n in range(9)]
SUM_BANK = [4, 4, 4, 7, 0, 1, 4, 4, 4]


def ff1_place(j):
    return (Place(C_FF1_STEPS + STEP1 * j.base, j.i, STEP1 * j.per), Place(Q_FF1 + 1 + 5 * j.base, j.i, 5 * j.per),
            Place(ADA_GATE + j.base, j.i, j.per))


def ff2_place(j):
    return (Place(C_FF2_STEPS + STEP2 * j.base, j.i, STEP2 * j.per), Place(Q_FF2 + 2 + 6 * j.base, j.i, 6 * j.per))


def build_program(nc, d, out):
    f32, f32r = mybir.dt.float32, mybir.dt.float32r
    ALU = mybir.AluOpType
    ACT = mybir.ActivationFunctionType
    AX = mybir.AxisListType
    base = 16512

    with ExitStack() as ctx:
        def at(name, shape, offset, dt=f32):
            return nc.alloc_sbuf_tensor_at(name, shape, dt, offset=base + offset)

        def sem(name):
            return ctx.enter_context(nc.semaphore(name))

        K = 1024
        RAW = at("RAW", [P, SLOTS, FT, NB], 0)
        WH = at("WH", [P, 2, FT, NB], 32 * K, f32r)
        WL = at("WL", [P, 2, FT, NB], 48 * K, f32r)
        X = at("X", [P, KC, T], 64 * K)
        XH = at("XH", [P, KC, T], 80 * K, f32r)
        XL = at("XL", [P, KC, T], 96 * K, f32r)
        HH = at("HH", [P, 2, FT, T], 112 * K, f32r)
        HL = at("HL", [P, 2, FT, T], 120 * K, f32r)
        NT = at("NT", [P, KC, T], 112 * K)
        CON = 128 * K
        cols = at("cols", [P, NCOLS], CON)
        small = CON + 2176
        mats = at("mats", [P, 4, P], small)
        mod = at("mod", [P, N_MOD * KC, 2], small + 2048)
        rt = at("rt", [P, 2 * T], small + 2816)
        MR = at("MR", [4, NB], small + 2816)
        csil = at("csil", [P, KC, 4], small + 4864, f32r)
        brow = at("brow", [64, 64], small + 5120)
        ctmp = at("ctmp", [P, 2, KC], small + 5120)
        csig = at("csig", [P, 2, KC], small + 5248)
        gmod = at("gmod", [P, KC], small + 5376)
        lnst = at("lnst", [P, 16], small + 5440)
        cw = at("cw", [P, 4 * FT], small + 5504)
        smx = at("smx", [P, 2, 4], small + 5568)
        sel = at("sel", [4, 2], small + 5600)
        epsc = at("epsc", [P, 1], small + 5632)
        AR = small + 5664
        assert 4 * NCOLS <= 2176
        ones, ident, lower, past = (mats[:, n, :] for n in range(4))

        def col(name, n=0, w=1):
            s = COLS[name][0] + n
            return cols[:, s:s + w]

        qT = at("qT", [P, HEADS, T], AR)
        kT = at("kT", [P, HEADS, T], AR + 8 * K)
        v1 = at("v1", [P, TT, 1024], AR + 16 * K)
        uT = at("uT", [P, 8, T], AR + 24 * K)
        vg = at("vg", [P, TT, 1024], AR + 32 * K)
        ga = at("ga", [P, KC, T], AR + 40 * K)
        gb = at("gb", [P, KC, T], AR + 56 * K)
        lng = at("lng", [P, 1024], AR + 40 * K)
        lnb = at("lnb", [P, 1024], AR + 44 * K)
        bsp = at("bsp", [P, 8, P], AR + 48 * K)
        wsp = at("wsp", [P, 8, P], AR + 52 * K)
        t1 = 112 * K
        sgt = at("sgt", [P, 2, 2, T], t1 + 8 * K)
        qk_sq = at("qk_sq", [P, FT, T], t1)
        zs = at("zs", [P, 2, 384], t1)
        zneg = at("zneg", [P, 2, 384], t1 + 3 * K)
        lk = at("lk", [P, 2, 384], t1 + 6 * K)
        lsg = at("lsg", [P, 2, 384], t1 + 9 * K)
        aw = at("aw", [P, 2, 384], t1 + 12 * K)
        MH = at("MH", [P, KC, T], AR, f32r)
        ML = at("ML", [P, KC, T], AR + 16 * K, f32r)
        FR = at("FR", [P, FT, T], AR + 32 * K)
        FQ = at("FQ", [P, FT, T], AR + 36 * K)
        GS = at("GS", [P, FT, T], AR + 40 * K)
        CV = at("CV", [P, FT, T], AR + 44 * K)
        SQ = at("SQ", [P, KC, T], AR)
        adab = at("adab", [P, 2, 2, NB], AR + 16 * K)
        adac = at("adac", [P, 2, 2, NB], AR + 24 * K)
        CX = at("CX", [P, KC, T], AR)
        CSQ = at("CSQ", [P, KC, T], AR + 56 * K)
        q2 = at("q2", [P, HEADS, T], AR)
        k2 = at("k2", [P, HEADS, T], AR + 8 * K)
        v2 = at("v2", [P, TT, 1024], AR + 16 * K)
        kc2 = at("kc2", [P, HEADS, T], AR + 24 * K)
        vc2 = at("vc2", [P, TT, 1024], AR + 32 * K)
        CH = at("CH", [P, KC, T], AR + 40 * K, f32r)
        CL = at("CL", [P, KC, T], AR + 56 * K, f32r)
        bia = at("bia", [P, TT, HEADS * ROWS, GRID_W], AR + 40 * K)
        bsel = at("bsel", [64, 2, 16, P], AR + 56 * K)
        hyC = at("hyC", [P, 12, T], AR + 56 * K)
        fX = at("fX", [P, TT, 512], AR + 68 * K)
        fY = at("fY", [P, FNG, T], AR + 68 * K)
        S2 = at("S2", [P, 2, 2 * T], t1)
        P2 = at("P2", [P, 2, 2 * T], t1 + 4 * K)
        PT = at("PT", [P, 2, 4, T], t1 + 8 * K)
        SM = at("SM", [P, KC, T], AR + 8 * K)
        fcl = at("fcl", [P, TT, 2 * T], 80 * K)
        fcd = at("fcd", [P, 2, P], 84 * K)
        fU = at("fU", [P, FNG, 2 * T], 88 * K)
        KS = at("KS", [P, 2, 5, HW], AR + 24 * K)
        zt = at("zt", [P, TT, HW], AR + 44 * K)
        YS = at("YS", [P, 4, HW], AR + 48 * K)
        hSD = at("hSD", [P, 2, 2, TT, HW], 80 * K)
        dec = at("dec", [P, 2, TT, HW], 96 * K)
        Ef = at("Ef", [P, TT, 6 * P], 104 * K)
        pz = at("pz", [33, T], 110 * K)
        w1h = at("w1h", [33, 64], 111 * K)
        w2h = at("w2h", [64, 64], 111 * K + 512)
        w3h = at("w3h", [64, 2048], t1)
        hdn = at("hdn", [64, 2, T], AR + 52 * K)
        sr = at("sr", [64, 2, T], AR + 54 * K)
        hfb = at("hfb", [P, 2, HW], AR + 48 * K)
        pp = at("pp", [P, 2, 2, HW], t1)
        zT2 = at("zT2", [P, HT, T], t1 + 8 * K)
        Gi = at("Gi", [P, 4, T], t1 + 12 * K)

        PS = ctx.enter_context(nc.psum_tensor("PS", [P, 8, 512], f32))

        def acc_ws(s):
            return PS[:, 2 * s:2 * s + 2, :].rearrange("p b (h t) -> p (b h) t", t=T)

        def acc_as(s):
            return PS[:, 2 * s:2 * s + 2, :]

        def bank(n):
            return PS[:, n, :]

        def ctx_as(n):
            return PS[:, 4 + 2 * (n % 2):6 + 2 * (n % 2), :]

        def ctx_ws(n):
            return ctx_as(n).rearrange("p b (h t) -> p (b h) t", t=T)

        def chunks(w):
            return w.rearrange("(s k p) n -> s p k n", p=P, k=FT)

        w_in, w_out, w_ff1, w_ff2 = map(chunks, (d["w_in"], d["w_out"], d["w_ff1"], d["w_ff2"]))
        w_oa, w_ob, ada_w = map(chunks, (d["w_oa"], d["w_ob"], d["ada_w"]))
        w_in2, w_out2, w_up, w_down = map(chunks, (d["w_in_2"], d["w_out_2"], d["w_up"], d["w_down"]))

        raw_in = [sem(f"raw_in{s}") for s in range(SLOTS)]
        hi_done = sem("hi_done")
        lo_done = sem("lo_done")
        pe_half = sem("pe_half")
        acc_free = [sem("acc_free0"), sem("acc_free1")]
        x_hi = sem("x_hi")
        x_lo = sem("x_lo")
        x_in = [sem(f"x_in{n}") for n in range(4)]
        bsel_in = [sem("bsel_in0"), sem("bsel_in1")]
        ada_in = [sem("ada_in0"), sem("ada_in1")]
        ada_acc = sem("ada_acc")
        act_own = sem("act_own")
        dve_own = sem("dve_own")
        names = (
            "cols_in mats_in eps_set ln_in cx_in brow_in four_in e_in mlp_in mlp3_in gi_in outs "
            "norm_sq norm_sum norm_rt norm_h ctx_sq qk_sqd qk_sum qk_rt q_done z_done zs_done zneg_done l_done "
            "lk_done cum_done la_done a_done am_done pv_done o_done ln_var ln_root mix_done sgu_ps s_done b_free "
            "merged csig_done csil_f csil_hi csil_done row_done mt_done mod_done relu_sq hid_hi hid_lo ctx_free "
            "bias_ps bias_done sc_done sm_done exp_done pn_done tp_done pt_done pv2_done a2_done fu_ps fu_done "
            "fy_ps fy_done hyc_done mlp_ps mlp_arg mlp_sin hf_ps hf_done ks_ps ks_done zt_ps zt_done zf_ps "
            "ys_done yi_ps hz_done mix_sq cw_done conv_a conv_b conv_done gelu_done").split()
        sm = {n: sem(n) for n in names}
        HF = FT // 2

        block = ctx.enter_context(nc.Block())

        @block.sync
        def _(sp):
            def load(c, src):
                if c.since(SLOTS):
                    sp.wait_ge(hi_done, c.value(2, -6))
                    sp.wait_ge(lo_done, c.value(2, -6))
                sp.dma_start(RAW[:, c.base % SLOTS], src).then_inc(raw_in[c.base % SLOTS], 16)

            def cut(view, s, n0):
                return view[s][:, :, n0:n0 + NB] if isinstance(n0, int) else view[s][:, :, bass.ds(n0, NB)]

            def down(c, view, j):
                for s in range(SLOTS):
                    load(c.plus(s), view[j.value()][:, :, s * NB:(s + 1) * NB])

            def wide(c, view, n0):
                for s in range(SLOTS):
                    load(c.plus(s), cut(view, s, n0))

            def beside_ada(c, view, n0, a):
                for s in range(SLOTS):
                    load(c.plus(2 * s), cut(view, s, n0))
                    load(c.plus(2 * s + 1), cut(ada_w, s, a.value(NB)))

            xq = d["x"].rearrange("(n k p) t -> n p k t", p=P, k=FT)
            for n in range(4):
                sp.dma_start(X[:, 4 * n:4 * n + 4, :], xq[n]).then_inc(x_in[n], 16)
            sp.dma_start(mats[:, :, :], d["mats"]).then_inc(sm["mats_in"], 16)
            sp.dma_start(sel[:, :], d["sel"]).then_inc(sm["mats_in"], 16)
            sp.dma_start(cols[:, :], d["cols"]).then_inc(sm["cols_in"], 16)
            for g, n0 in enumerate(IN1_COLS):
                wide(Place(4 * g), w_in, n0)
                if g == 0:
                    for dst, name in ((lng[:, :], "ln_g"), (lnb[:, :], "ln_b"),
                                      (bsp[:, :, :], "b_sp"), (wsp[:, :, :], "w_sp")):
                        sp.dma_start(dst, d[name]).then_inc(sm["ln_in"], 16)
            for g in range(8):
                beside_ada(Place(C_GATE + 8 * g), w_in, GATE_COL + g * NB, Place(g))
            for g in range(4):
                for s in range(SLOTS):
                    load(Place(C_OAB + 4 * g + s), cut(w_oa if s < 2 else w_ob, s % 2, g * NB))
            for g in range(4):
                wide(Place(C_OUT1 + 4 * g), w_out, g * NB)

            def load_piece(a, n, order):
                if order.since(2):
                    sp.wait_ge(ada_acc, order.value(2, -2))
                sp.dma_start(adab[:, order.base % 2], cut(ada_w, n // 2, a.value(NB))[:, 2 * (n % 2):2 * (n % 2) + 2, :])\
                    .then_inc(ada_in[order.base % 2], 16)

            def ff1_step(j, first=False):
                c, _, a = ff1_place(j)
                order = Place(8 * j.base, j.i, 8 * j.per)
                for s in range(STEP1):
                    if s < SLOTS:
                        load(c.plus(s), cut(w_ff1, s, j.value(NB, NB)))
                    else:
                        load(c.plus(s), w_ff2[j.value()][:, :, (s - 4) * NB:(s - 3) * NB])
                    if s >= 2:
                        load_piece(a, s - 2, order.plus(s - 2))
                    elif not first:
                        load_piece(a.plus(-1), s + 6, order.plus(s - 2))

            wide(Place(C_FF1), w_ff1, 0)
            sp.wait_ge(pe_half, 2 * C_FF1)
            sp.dma_start(CX[:, :, :], d["ctx"].rearrange("(k p) t -> p k t", p=P)).then_inc(sm["cx_in"], 16)
            ff1_step(Place(0), True)
            ff1_step(Place(1))
            with sp.Fori(0, FF1_ITERS) as i:
                ff1_step(Place(2, i, 2))
                ff1_step(Place(3, i, 2))
            for s in range(3 * SLOTS):
                g, r = divmod(s, SLOTS)
                load(Place(C_FF1_TAIL + s), cut(w_ff1, r, (STEPS1 - 1) * NB) if g == 0 else
                     w_ff2[STEPS1 - 3 + g][:, :, r * NB:(r + 1) * NB])
                if s < 2:
                    load_piece(Place(ADA_GROUPS - 3), s + 6, Place(8 * (STEPS1 - 2) + s - 2))
                for n in range(16):
                    if ADA_TAIL[n] == s - 1:
                        load_piece(Place(ADA_GROUPS - 2 + n // 8), n % 8, Place(8 * (STEPS1 - 2) + n))
            for n, n0 in enumerate(IN2_COLS):
                wide(Place(C_IN2 + 4 * n), w_in2, n0)
            wide(Place(C_OUT2), w_out2, 0)
            sp.wait_ge(pe_half, 2 * C_OUT2)
            sp.dma_start(pz[:, :], d["pz"]).then_inc(sm["mlp_in"], 16)
            sp.dma_start(w1h[:, :], d["hy_w1"]).then_inc(sm["mlp_in"], 16)
            sp.dma_start(w2h[:, :], d["hy_w2"]).then_inc(sm["mlp_in"], 16)
            sp.dma_start(fcl[:, :, :], d["fcl"]).then_inc(sm["four_in"], 16)
            sp.dma_start(fcd[:, :, :], d["fcd"]).then_inc(sm["four_in"], 16)
            sp.dma_start(dec[:, :, :, :], d["dec"]).then_inc(sm["e_in"], 16)
            sp.dma_start(Ef[:, :, :], d["ef"]).then_inc(sm["e_in"], 16)
            sp.wait_ge(sm["tp_done"], 2 * HEADS)
            sp.dma_start(w3h[:, :], d["hy_w3"]).then_inc(sm["mlp3_in"], 16)
            sp.wait_ge(sm["pv2_done"], HEADS)
            sp.dma_start(Gi[:, :, :], d["gi"]).then_inc(sm["gi_in"], 16)
            for g in range(1, 4):
                wide(Place(C_OUT2 + 4 * g), w_out2, g * NB)

            def ff2_step(j):
                c, _ = ff2_place(j)
                wide(c, w_up, j.value(NB, NB))
                wide(c.plus(SLOTS), w_up, j.value(NB, D_FF2 + NB))
                down(c.plus(2 * SLOTS), w_down, j)

            wide(Place(C_FF2), w_up, 0)
            wide(Place(C_FF2 + SLOTS), w_up, D_FF2)
            ff2_step(Place(0))
            ff2_step(Place(1))
            with sp.Fori(0, FF2_ITERS) as i:
                ff2_step(Place(2, i, 2))
                ff2_step(Place(3, i, 2))
            down(Place(C_END - SLOTS), w_down, Place(STEPS2 - 1))
            for n in range(4):
                sp.wait_ge(sm["norm_h"], QUARTERS[N_LAST] + n + 1)
                sp.dma_start(out.rearrange("(k p) t -> p k t", p=P)[:, 4 * n:4 * n + 4, :],
                             NT[:, 4 * n:4 * n + 4, :]).then_inc(sm["outs"], 16)
            sp.wait_ge(sm["outs"], 64)

        @block.scalar
        def _(act):
            own = Chain(act, act_own)
            A = nc.scalar.activation

            def high_half(c, h):
                if h == 0:
                    act.wait_ge(raw_in[c.base % SLOTS], c.turns(SLOTS, 1, 16))
                if c.since(2):
                    act.wait_ge(pe_half, c.value(2, h - 3))
                hs = slice(HF * h, HF * h + HF)
                A(WH[:, c.base % 2, hs], RAW[:, c.base % SLOTS, hs], ACT.Copy).then_inc(hi_done, 1)

            def high(c):
                high_half(c, 0)
                high_half(c, 1)

            def done(c):
                act.wait_ge(pe_half, c.value(2, 2))

            def evac(c, q, dst, fn, ws=True, scale=1.0):
                done(c)
                A(dst, acc_ws(q.slot) if ws else acc_as(q.slot), fn, scale=scale).then_inc(acc_free[q.slot], 1)

            def root(n, total):
                act.wait_ge(sm["norm_sum"], n + 1)
                if n:
                    act.wait_ge(sm["norm_h"], QUARTERS[n])
                A(rt[:, 0:T], bank(SUM_BANK[n])[:, 0:T], ACT.Sqrt, bias=epsc[:, 0:1],
                  scale=1.0 / total).then_inc(sm["norm_rt"], 1)

            def split_high(dst, src, n):
                A(dst[:, 4 * n:4 * n + 4, :], src, ACT.Copy).then_inc(x_hi, 1)

            def shifted_high(dst, src, shift, norm, n):
                act.wait_ge(sm["norm_h"], QUARTERS[norm] + n + 1)
                for k in range(4 * n, 4 * n + 4):
                    ins = A(dst[:, k, :], src[:, k, :], ACT.Identity, bias=shift(k))
                ins.then_inc(x_hi, 1)

            def norm_window(norm, c, shift=None):
                def quarter_high(n):
                    if shift is None:
                        act.wait_ge(sm["norm_h"], QUARTERS[norm] + n + 1)
                        split_high(XH, NT[:, 4 * n:4 * n + 4, :], n)
                    else:
                        shifted_high(XH, NT, shift, norm, n)

                high(c)
                high(c.plus(1))
                root(norm, D)
                quarter_high(0)
                quarter_high(1)
                high(c.plus(2))
                quarter_high(2)
                high(c.plus(3))
                quarter_high(3)

            def ada_row(c, a):
                done(c)
                if a.since(1):
                    act.wait_ge(sm["mt_done"], a.value())
                A(MR[:, :], bank(7)[0:4, :], ACT.Copy).then_inc(sm["row_done"], 1)

            act.wait_ge(sm["cols_in"], 16)
            act.wait_ge(sm["eps_set"], 1)
            norm_window(N_IN, Place(0))

            def project_out(g):
                n = g % 2
                t4 = slice(4 * n, 4 * n + 4)
                c5 = slice(n * NB, (n + 1) * NB)
                c, q = Place(4 * g + 3), Place(g)
                if g < 2:
                    evac(c, q, vg[:, :, c5], ACT.Gelu, ws=False)
                elif g < 4:
                    evac(c, q, uT[:, t4, :], ACT.Gelu)
                elif g < 6:
                    evac(c, q, qT[:, t4, :], ACT.Copy)
                elif g < 8:
                    evac(c, q, kT[:, t4, :], ACT.Copy)
                else:
                    evac(c, q, v1[:, :, c5], ACT.Copy, ws=False)

            def gate_out(g):
                dst = (ga if g < 4 else gb)[:, 4 * (g % 4):4 * (g % 4) + 4, :]
                evac(Place(C_GATE + 8 * g + 6), Place(Q_GATE + g), dst, ACT.Sigmoid)

            def attention_step(h, t):
                if t == 1:
                    act.wait_ge(sm["z_done"], h + 1)
                    if h:
                        act.wait_ge(sm["lk_done"], h)
                    A(zs[:, 0, :], bank(4)[:, 0:384], ACT.Copy, scale=SCALE).then_inc(sm["zs_done"], 1)
                if t == 2:
                    act.wait_ge(sm["zneg_done"], h + 1)
                    own.did(A(zneg[:, 0, :], zneg[:, 0, :], ACT.Exp))
                    own.settle()
                    A(zneg[:, 0, :], zneg[:, 0, :], ACT.Ln, bias=1.0).then_inc(sm["l_done"], 1)
                if t == 4:
                    act.wait_ge(sm["la_done"], h + 1)
                    if h:
                        act.wait_ge(sm["pv_done"], h)
                    A(aw[:, 0, :], lsg[:, 0, :], ACT.Exp).then_inc(sm["a_done"], 1)
                if t == 7:
                    act.wait_ge(sm["pv_done"], h + 1)
                    A(qT[:, h, :], bank(5)[:, 0:T], ACT.Copy).then_inc(sm["o_done"], 1)

            for c in range(4, C_OAB):
                high(Place(c))
                if c % 4 == 1 and c < C_GATE + 4:
                    project_out((c - 5) // 4)
                if c in (T_LN + 1, T_LN + 5):
                    t = (c - T_LN - 1) // 4
                    act.wait_ge(sm["ln_var"], t + 1)
                    A(lnst[:, 14 + t:15 + t], lnst[:, 12 + t:13 + t], ACT.Sqrt, bias=epsc[:, 0:1])\
                        .then_inc(sm["ln_root"], 1)
                if T_QK + 2 <= c < T_QK + 18 and (c - T_QK) % 4 in (2, 3):
                    n = 2 * ((c - T_QK - 2) // 4) + (c - T_QK) % 4 - 2
                    act.wait_ge(sm["qk_sum"], n + 1)
                    act.wait_ge(sm["q_done"], n)
                    if n == 0:
                        act.wait_ge(sm["norm_h"], 4)
                    A(rt[:, :], bank(4 + n % 2), ACT.Sqrt, bias=epsc[:, 0:1], scale=1.0 / DH)\
                        .then_inc(sm["qk_rt"], 1)
                if c == T_QK - 4:
                    A(csig[:, :, :], col("c", 0, 2 * KC).rearrange("p (a k) -> p a k", a=2), ACT.Sigmoid)\
                        .then_inc(sm["csig_done"], 1)
                if c == T_QK - 2:
                    act.wait_ge(sm["csil_f"], 1)
                    A(csil[:, :, 0:2], ctmp[:, :, :].rearrange("p a k -> p k a"), ACT.Copy)\
                        .then_inc(sm["csil_hi"], 1)
                if T_ATT <= c < T_ATT + S_ATT * HEADS:
                    attention_step(*divmod(c - T_ATT, S_ATT))
                if c >= C_GATE + 8 and c % 8 == 0:
                    gate_out((c - C_GATE - 8) // 8)
                if c >= C_GATE + 9 and c % 8 == 1:
                    ada_row(Place(c - 2), Place((c - C_GATE - 9) // 8))
            for c in range(C_OAB, C_OUT1):
                t = c - C_OAB
                high(Place(c))
                if t < 4:
                    done(Place(C_OAB - 2))
                    if t == 0:
                        act.wait_ge(sm["o_done"], HEADS)
                    split_high(XH, (qT if t < 2 else uT)[:, 4 * (t % 2):4 * (t % 2) + 4, :], t)
                if t == 0:
                    gate_out(7)
                if t == 1:
                    ada_row(Place(C_OAB - 1), Place(7))
                if t >= 6 and t % 4 == 2:
                    n = (t - 6) // 4
                    act.wait_ge(sm["merged"], n + 1)
                    split_high(MH, ga[:, 4 * n:4 * n + 4, :], n)
            for c in range(C_OUT1, C_FF1):
                high(Place(c))
                if c == C_OUT1 + 2:
                    act.wait_ge(sm["merged"], 4)
                    split_high(MH, ga[:, 12:16, :], 3)
            act.wait_ge(sm["mt_done"], ADA_GATE)
            norm_window(N_FF1, Place(C_FF1))

            def relu(c, q, j):
                done(c)
                if j.since(1):
                    act.wait_ge(sm["relu_sq"], j.value())
                A(FR[:, :, :], acc_ws(q.slot), ACT.Relu).then_inc(acc_free[q.slot], 1)

            def hidden_high(j):
                act.wait_ge(sm["relu_sq"], j.value(1, 1))
                if j.since(1):
                    act.wait_ge(sm["hid_lo"], j.value())
                A(HH[:, j.base % 2], FQ[:, :, :], ACT.Copy).then_inc(sm["hid_hi"], 1)

            def context_norm(step, s):
                if step == 0 and 1 <= s < 5:
                    n = s - 1
                    if n == 0:
                        act.wait_ge(sm["cx_in"], 16)
                    A(CSQ[:, 4 * n:4 * n + 4, :], CX[:, 4 * n:4 * n + 4, :], ACT.Square).then_inc(sm["ctx_sq"], 1)
                if step == 1 and s == 0:
                    root(N_CTX, D)
                if step == 1 and s in (2, 3, 5, 6):
                    shifted_high(CH, CX, lambda k: mod[:, k, 1:2], N_CTX, (2, 3, 5, 6).index(s))

            def ff1_step(j, beside=None):
                c, q, _ = ff1_place(j)
                for s in range(STEP1):
                    high(c.plus(s))
                    if beside == 0 and s == 1:
                        relu(c.plus(-1), Place(Q_FF1), Place(0))
                    if beside == 0 and s == 2:
                        hidden_high(Place(0))
                    if s == 5:
                        relu(c.plus(3), q, j.plus(1))
                    if s == 6:
                        hidden_high(j.plus(1))
                    if beside is not None:
                        context_norm(beside, s)

            ff1_step(Place(0), 0)
            ff1_step(Place(1), 1)
            with act.Fori(0, FF1_ITERS) as i:
                ff1_step(Place(2, i, 2))
                ff1_step(Place(3, i, 2))
            c = Place(C_FF1_TAIL)
            for s in range(3 * SLOTS):
                high(c.plus(s))
                if s == 5:
                    relu(c.plus(3), Place(Q_FF1_TAIL), Place(STEPS1 - 1))
                if s == 6:
                    hidden_high(Place(STEPS1 - 1))

            norm_window(N_MIX_IN, Place(C_IN2), lambda k: mod[:, k, 0:1])

            def project2_out(n):
                c, q = Place(C_IN2 + 4 * n + 3), Place(Q_IN2 + n)
                t4 = slice(4 * (n % 2), 4 * (n % 2) + 4)
                c5 = slice((n % 2) * NB, (n % 2 + 1) * NB)
                if n < 2:
                    evac(c, q, k2[:, t4, :], ACT.Copy)
                    A(kc2[:, t4, :], ctx_ws(n), ACT.Copy).then_inc(sm["ctx_free"], 1)
                elif n < 4:
                    evac(c, q, v2[:, :, c5], ACT.Copy, ws=False)
                    A(vc2[:, :, c5], ctx_as(n), ACT.Copy).then_inc(sm["ctx_free"], 1)
                elif n < 6:
                    evac(c, q, q2[:, t4, :], ACT.Copy, scale=SCALE)
                elif n == 6:
                    evac(c, q, fX[:, :, :], ACT.Copy, ws=False)

            def load_selector(part):
                act.dma_start(bsel[:, part % 2], d["bsel"][:, 16 * part:16 * part + 16, :])\
                    .then_inc(bsel_in[part % 2], 16)

            def bias_out(n):
                act.wait_ge(sm["bias_ps"], n + 1)
                A(bia[:, :, :, 8 * n:8 * n + 8], bank(4 + n % 4).rearrange("p (c t h) -> p t h c", t=TT, c=8),
                  ACT.Copy).then_inc(sm["bias_done"], 1)

            def attention2_step(t):
                u = t - T_ATT2 - 2
                if 0 <= u < 2 * HEADS:
                    b = u % 2
                    act.wait_ge(sm["sm_done"], u + 1)
                    if u >= 2:
                        act.wait_ge(sm["tp_done"], u - 1)
                    A(P2[:, b, :], S2[:, b, :], ACT.Exp, bias=smx[:, b, 0:1],
                      accum_out=smx[:, b, 1:2]).then_inc(sm["exp_done"], 1)
                u = t - T_ATT2 - 6
                if 0 <= u < 2 * HEADS and u % 2:
                    h = u // 2
                    act.wait_ge(sm["pv2_done"], h + 1)
                    A(q2[:, h, :], bank(7)[:, 0:T], ACT.Copy).then_inc(sm["a2_done"], 1)

            for t in range(4, 10 * SLOTS):
                high(Place(C_IN2 + t))
                if t % 4 == 1 and t < 33:
                    project2_out((t - 5) // 4)
                if t == T_BIAS:
                    done(Place(C_IN2 + 15))
                    act.dma_start(brow[:, :], d["brow"]).then_inc(sm["brow_in"], 16)
                    load_selector(0)
                    load_selector(1)
                if t == T_BIAS + 4:
                    act.wait_ge(sm["bias_ps"], 2)
                    load_selector(2)
                if t == T_BIAS + 5:
                    act.wait_ge(sm["bias_ps"], 4)
                    load_selector(3)
                if t in (T_BIAS + 4, T_BIAS + 5, T_BIAS + 7, T_BIAS + 8):
                    n = 2 * (T_BIAS + 4, T_BIAS + 5, T_BIAS + 7, T_BIAS + 8).index(t)
                    bias_out(n)
                    bias_out(n + 1)
                attention2_step(t)

            def fourier_tokens(n):
                act.wait_ge(sm["fu_ps"], n + 1)
                A(fU[:, n, :], bank(n % 2), ACT.Copy).then_inc(sm["fu_done"], 1)

            def sine(n):
                act.wait_ge(sm["mlp_arg"], n + 1)
                A(hdn[:, n, :], sr[:, 0, :], ACT.Sin).then_inc(sm["mlp_sin"], 1)

            high(Place(C_OUT2))
            attention2_step(40)
            high(Place(C_OUT2 + 1))
            for t in range(41, 44):
                attention2_step(t)
            fourier_tokens(0)
            attention2_step(44)
            attention2_step(45)
            fourier_tokens(1)
            sine(0)
            fourier_tokens(2)
            fourier_tokens(3)
            sine(1)
            for n in range(FNG):
                act.wait_ge(sm["fy_ps"], n + 1)
                A(fY[:, n, :], bank((2, 6)[n % 2])[:, 0:T], ACT.Copy).then_inc(sm["fy_done"], 1)
            act.wait_ge(sm["a2_done"], HEADS)
            for n in range(2):
                A(SM[:, 4 * n:4 * n + 4, :], q2[:, 4 * n:4 * n + 4, :], ACT.Square).then_inc(sm["mix_sq"], 1)

            def spectrum(n):
                act.wait_ge(sm["ks_ps"], n + 1)
                A(KS[:, n // 5, n % 5, :], bank(n % 2), ACT.Copy).then_inc(sm["ks_done"], 1)

            def to_tokens(o):
                for t in range(TT):
                    act.wait_ge(sm["zt_ps"], TT * o + t + 1)
                    A(zt[:, t, :], bank(2 + t), ACT.Copy).then_inc(sm["zt_done"], 1)

            for n in range(5):
                spectrum(n)
            to_tokens(0)
            for n in range(5, 10):
                spectrum(n)
            root(N_A, 1024)
            to_tokens(1)
            act.wait_ge(sm["ks_ps"], 10)
            for n in range(2):
                act.wait_ge(sm["norm_h"], QUARTERS[N_A] + n + 1)
                split_high(XH, SM[:, 4 * n:4 * n + 4, :], n)
            root(N_F, 512)
            act.wait_ge(sm["norm_h"], QUARTERS[N_F] + 1)
            split_high(XH, SM[:, 8:12, :], 2)
            high(Place(C_OUT2 + 2))
            root(N_H, 512)
            act.wait_ge(sm["norm_h"], QUARTERS[N_H] + 1)
            split_high(XH, SM[:, 12:16, :], 3)
            for c in range(C_OUT2 + 3, C_FF2):
                high(Place(c))
            norm_window(N_FF2, Place(C_FF2), lambda k: mod[:, 3 * KC + k, 0:1])

            def hidden_gate(c, q, j):
                done(c)
                if j.since(1):
                    act.wait_ge(sm["conv_done"], j.value())
                A(GS[:, :, :], acc_ws(q.slot), ACT.Copy).then_inc(acc_free[q.slot], 1)

            def gate_gelu(j):
                act.wait_ge(sm["conv_done"], j.value(1, 1))
                A(CV[:, :, :], CV[:, :, :], ACT.Gelu_apprx_tanh).then_inc(sm["gelu_done"], 1)

            def hidden_high2(q, j):
                act.wait_ge(acc_free[q.slot], q.turns(2, 1))
                A(HH[:, j.base % 2], FQ[:, :, :], ACT.Copy).then_inc(sm["hid_hi"], 1)

            def ff2_step(j, first=False):
                c, q = ff2_place(j)
                for s in range(STEP2):
                    high(c.plus(s))
                    if first and s == 0:
                        gate_gelu(Place(0))
                    if first and s == 2:
                        hidden_high2(q.plus(-1), Place(0))
                    if s == 5:
                        hidden_gate(c.plus(3), q, j.plus(1))
                    if s == 8:
                        gate_gelu(j.plus(1))
                    if s == 10:
                        hidden_high2(q.plus(1), j.plus(1))

            for s in range(4, 8):
                high(Place(C_FF2 + s))
                if s == 5:
                    hidden_gate(Place(C_FF2 + 3), Place(Q_FF2), Place(0))
            ff2_step(Place(0), first=True)
            ff2_step(Place(1))
            with act.Fori(0, FF2_ITERS) as i:
                ff2_step(Place(2, i, 2))
                ff2_step(Place(3, i, 2))
            for s in range(4):
                high(Place(C_END - 4 + s))
            root(N_LAST, D)

        @block.vector
        def _(dve):
            own = Chain(dve, dve_own)
            V = nc.vector
            stt, tt, ts = V.scalar_tensor_tensor, V.tensor_tensor, V.tensor_scalar

            def low_half(c, h):
                dve.wait_ge(hi_done, c.value(2, h + 1))
                if c.since(2):
                    dve.wait_ge(pe_half, c.value(2, h - 3))
                hs = slice(HF * h, HF * h + HF)
                b = c.base % 2
                tt(WL[:, b, hs], RAW[:, c.base % SLOTS, hs], WH[:, b, hs].bitcast(f32), ALU.subtract)\
                    .then_inc(lo_done, 1)

            def low(c):
                low_half(c, 0)
                low_half(c, 1)

            def done(c):
                dve.wait_ge(pe_half, c.value(2, 2))

            def settled(ins):
                own.did(ins)
                own.settle()

            def quarter(x, n):
                return x[:, 4 * n:4 * n + 4, :]

            def squares(dst, src, n, part):
                ins = tt(quarter(dst, n), quarter(src, n), quarter(src, n), ALU.mult)
                if part:
                    ins.then_inc(sm["norm_sq"], 1)
                else:
                    settled(ins)

            def add_squares(dst, n, part):
                ins = tt(quarter(dst, 0), quarter(dst, 0), quarter(dst, n), ALU.add)
                if part:
                    ins.then_inc(sm["norm_sq"], 1)
                else:
                    settled(ins)

            def inverse_root(n):
                dve.wait_ge(sm["norm_rt"], n + 1)
                settled(V.reciprocal(rt[:, 0:T], rt[:, 0:T]))

            def scaled(dst, src, gain, n):
                for k in range(4):
                    ins = stt(dst[:, 4 * n + k, :], src[:, k, :], gain(4 * n + k), rt[:, 0:T],
                              ALU.mult, ALU.mult)
                ins.then_inc(sm["norm_h"], 1)

            def split_low(e, hi, lo, src, n):
                dve.wait_ge(x_hi, 4 * e + n + 1)
                tt(quarter(lo, n), src, quarter(hi, n).bitcast(f32), ALU.subtract).then_inc(x_lo, 1)

            def shifted_low(e, hi, lo, src, shift, n):
                dve.wait_ge(x_hi, 4 * e + n + 1)
                for k in range(4 * n, 4 * n + 4):
                    ins = stt(lo[:, k, :], src[:, k, :], shift(k), hi[:, k, :].bitcast(f32), ALU.add, ALU.subtract)
                ins.then_inc(x_lo, 1)

            def norm_window(norm, e, c, gain, finish, shift=None):
                def quarter_low(n):
                    if shift is None:
                        split_low(e, XH, XL, quarter(NT, n), n)
                    else:
                        shifted_low(e, XH, XL, NT, shift, n)

                low(c)
                low_half(c.plus(1), 0)
                finish()
                low_half(c.plus(1), 1)
                inverse_root(norm)
                scaled(NT, quarter(X, 0), gain, 0)
                scaled(NT, quarter(X, 1), gain, 1)
                quarter_low(0)
                scaled(NT, quarter(X, 2), gain, 2)
                quarter_low(1)
                low(c.plus(2))
                scaled(NT, quarter(X, 3), gain, 3)
                quarter_low(2)
                low(c.plus(3))
                quarter_low(3)

            V.memset(epsc[:, :], EPS).then_inc(sm["eps_set"], 1)
            for n in range(4):
                dve.wait_ge(x_in[n], 16)
                squares(NT, X, n, n == 3)
                if n in (1, 2):
                    add_squares(NT, n, n == 2)
            dve.wait_ge(sm["cols_in"], 16)
            norm_window(N_IN, E_NORM1, Place(0), lambda k: col("g_mix", k), lambda: None)

            def layer_norm(t, step):
                if step == 0:
                    dve.wait_ge(acc_free[0], 1)
                    dve.wait_ge(acc_free[1], 1)
                    for n in range(2):
                        own.did(V.bn_stats(lnst[:, 6 * n:6 * n + 6], vg[:, t, n * 512:(n + 1) * 512]))
                    own.settle()
                    settled(V.bn_aggr(smx[:, t, 0:2], lnst[:, 0:12]))
                    V.tensor_copy(lnst[:, 12 + t:13 + t], smx[:, t, 1:2]).then_inc(sm["ln_var"], 1)
                if step == 2:
                    dve.wait_ge(sm["ln_root"], t + 1)
                    settled(V.reciprocal(smx[:, t, 2:3], lnst[:, 14 + t:15 + t]))
                    settled(ts(vg[:, t, :], vg[:, t, :], smx[:, t, 0:1], smx[:, t, 2:3], ALU.subtract, ALU.mult))
                if step == 3:
                    dve.wait_ge(sm["ln_in"], 64)
                    settled(tt(vg[:, t, :], vg[:, t, :], lng[:, :], ALU.mult))
                if step == 4:
                    tt(vg[:, t, :], vg[:, t, :], lnb[:, :], ALU.add).then_inc(sm["mix_done"], 1)

            def spatial_gating(n):
                dve.wait_ge(sm["sgu_ps"], n + 1)
                dve.wait_ge(acc_free[0], 2)
                dve.wait_ge(acc_free[1], 2)
                if n >= 2:
                    dve.wait_ge(sm["s_done"], n - 1)
                for g in range(2):
                    for c in range(TT):
                        own.did(tt(sgt[:, n % 2, g, c * P:(c + 1) * P],
                                   bank(6 + n % 2)[:, (TT * g + c) * P:(TT * g + c + 1) * P],
                                   bsp[:, 2 * n + g, :], ALU.add))
                own.settle()
                tt(uT[:, 2 * n:2 * n + 2, :], uT[:, 2 * n:2 * n + 2, :], sgt[:, n % 2], ALU.mult)\
                    .then_inc(sm["s_done"], 1)

            def head_norm(n, step):
                src = quarter(qT if n < 2 else kT, n % 2)
                gname = "g_q" if n < 2 else "g_k"
                if step == 0:
                    q = Place(4 + n)
                    dve.wait_ge(acc_free[q.slot], q.turns(2, 1))
                    if n:
                        dve.wait_ge(sm["qk_sum"], 2 * n)
                    tt(qk_sq[:, :, :], src, src, ALU.mult).then_inc(sm["qk_sqd"], 1)
                else:
                    half = step - 2
                    dve.wait_ge(sm["qk_rt"], 2 * n + half + 1)
                    settled(V.reciprocal(rt[:, :], rt[:, :]))
                    for m in range(2):
                        h = 2 * half + m
                        ins = stt(src[:, h, :], src[:, h, :], col(gname, 4 * (n % 2) + h),
                                  rt[:, m * T:(m + 1) * T], ALU.mult, ALU.mult)
                    ins.then_inc(sm["q_done"], 1)

            def attention_step(h, t):
                if t == 1:
                    dve.wait_ge(sm["zs_done"], h + 1)
                    if h:
                        dve.wait_ge(sm["lk_done"], h)
                    stt(zneg[:, 0, :], zs[:, 0, :], -1.0, zs[:, 0, :], ALU.mult, ALU.min)\
                        .then_inc(sm["zneg_done"], 1)
                if t == 2:
                    dve.wait_ge(sm["l_done"], h + 1)
                    if h:
                        dve.wait_ge(sm["a_done"], h)
                        dve.wait_ge(sm["cum_done"], h)
                    settled(stt(lsg[:, 0, :], zs[:, 0, :], 0.0, zneg[:, 0, :], ALU.min, ALU.subtract))
                    settled(tt(lk[:, 0, :], lsg[:, 0, :], zs[:, 0, :], ALU.subtract))
                    own.did(tt(lk[:, 0, 0:P], lk[:, 0, 0:P], past, ALU.mult))
                    tt(lk[:, 0, T:384], lk[:, 0, T:384], past, ALU.mult).then_inc(sm["lk_done"], 1)
                if t == 4:
                    dve.wait_ge(sm["cum_done"], h + 1)
                    tt(lsg[:, 0, :], bank(5)[:, 0:384], lsg[:, 0, :], ALU.add).then_inc(sm["la_done"], 1)
                if t == 5:
                    dve.wait_ge(sm["a_done"], h + 1)
                    own.did(tt(aw[:, 0, 0:P], aw[:, 0, 0:P], past, ALU.mult))
                    tt(aw[:, 0, T:384], aw[:, 0, T:384], past, ALU.mult).then_inc(sm["am_done"], 1)
                    own.settle()

            def mod_out(a):
                dve.wait_ge(sm["mt_done"], a.value(1, 1))
                n = a.value(FT)
                dst = mod[:, n:n + FT, :] if a.i is None else mod[:, bass.ds(n, FT), :]
                V.tensor_copy(dst, bank(6)[:, 0:2 * FT].rearrange("p (f c) -> p f c", c=2))\
                    .then_inc(sm["mod_done"], 1)

            for c in range(4, C_OAB):
                low(Place(c))
                if c == T_LN:
                    dve.wait_ge(sm["ln_in"], 64)
                    V.memset(wsp[CHUNK:P, :, 0:CHUNK], 0.0).then_inc(sm["mix_done"], 1)
                for t in range(TT):
                    if 0 <= c - T_LN - 4 * t < 5:
                        layer_norm(t, c - T_LN - 4 * t)
                if T_SGU < c <= T_SGU + 8 and (c - T_SGU) % 2:
                    spatial_gating((c - T_SGU) // 2)
                if T_QK <= c < T_QK + 16 and (c - T_QK) % 4 != 1:
                    head_norm((c - T_QK) // 4, (c - T_QK) % 4)
                if c == T_QK - 3:
                    dve.wait_ge(sm["csig_done"], 1)
                    tt(ctmp[:, :, :], col("c", 0, 2 * KC).rearrange("p (a k) -> p a k", a=2), csig[:, :, :],
                       ALU.mult).then_inc(sm["csil_f"], 1)
                if c == T_QK - 1:
                    dve.wait_ge(sm["csil_hi"], 1)
                    tt(csil[:, :, 2:4], ctmp[:, :, :].rearrange("p a k -> p k a"),
                       csil[:, :, 0:2].bitcast(f32), ALU.subtract).then_inc(sm["csil_done"], 1)
                if c == T_ATT:
                    dve.wait_ge(sm["mats_in"], 32)
                if T_ATT <= c < T_ATT + S_ATT * HEADS:
                    attention_step(*divmod(c - T_ATT, S_ATT))
                if c >= C_GATE + 12 and c % 8 == 4:
                    mod_out(Place((c - C_GATE - 12) // 8))

            def merge(g):
                q = Place(Q_OAB + g)
                done(Place(C_OAB + 4 * g + 3))
                if g == 0:
                    for n in range(2):
                        dve.wait_ge(acc_free[n], (Q_GATE + 8) // 2)
                tt(quarter(ga, g), acc_ws(q.slot), quarter(ga, g), ALU.mult).then_inc(acc_free[q.slot], 1)
                tt(quarter(gb, g), ctx_ws(g), quarter(gb, g), ALU.mult).then_inc(sm["b_free"], 1)
                dve.wait_ge(acc_free[q.slot], q.turns(2, 1))
                dve.wait_ge(sm["b_free"], g + 1)
                tt(quarter(ga, g), quarter(ga, g), quarter(gb, g), ALU.add).then_inc(sm["merged"], 1)

            for c in range(C_OAB, C_OUT1):
                t = c - C_OAB
                low(Place(c))
                if t < 4:
                    split_low(E_OAB, XH, XL, quarter(qT if t < 2 else uT, t % 2), t)
                if t == 4:
                    mod_out(Place(7))
                if t >= 5 and t % 4 == 1:
                    merge((t - 5) // 4)
                if t >= 6 and t % 4 == 2:
                    n = (t - 6) // 4
                    split_low(E_OUT1, MH, ML, quarter(ga, n), n)

            def residual(g):
                q = Place(Q_OUT1 + g)
                done(Place(C_OUT1 + 4 * g + 3))
                tt(quarter(X, g), acc_ws(q.slot), quarter(X, g), ALU.add).then_inc(acc_free[q.slot], 1)

            def residual_squares(c0, q0, g, residual):
                residual(g)
                q = Place(q0 + g)
                dve.wait_ge(acc_free[q.slot], q.turns(2, 1))
                squares(NT, X, g, g == 3)

            for t in range(4 * SLOTS):
                low(Place(C_OUT1 + t))
                if t == 1:
                    merge(3)
                if t == 2:
                    split_low(E_OUT1, MH, ML, quarter(ga, 3), 3)
                if t in (5, 9, 13):
                    residual_squares(C_OUT1, Q_OUT1, (t - 5) // 4, residual)
                if t in (10, 14):
                    add_squares(NT, (t - 6) // 4, t == 14)
            norm_window(N_FF1, E_NORM2, Place(C_FF1), lambda k: col("g_ff", k),
                        lambda: residual_squares(C_OUT1, Q_OUT1, 3, residual))

            def relu_squared(q, j):
                dve.wait_ge(acc_free[q.slot], q.turns(2, 1))
                if j.since(1):
                    dve.wait_ge(sm["hid_lo"], j.value())
                tt(FQ[:, :, :], FR[:, :, :], FR[:, :, :], ALU.mult).then_inc(sm["relu_sq"], 1)

            def hidden_low(j, before=0):
                dve.wait_ge(sm["hid_hi"], j.value(1, before + 1))
                tt(HL[:, j.base % 2], FQ[:, :, :], HH[:, j.base % 2].bitcast(f32), ALU.subtract)\
                    .then_inc(sm["hid_lo"], 1)

            def down_out(q, c, s):
                done(c)
                tt(quarter(X, s), acc_ws(q.slot), quarter(X, s), ALU.add).then_inc(acc_free[q.slot], 1)

            def gain_of(a, scale_at, name):
                settled(stt(gmod[:, :], mod[:, scale_at:scale_at + KC, a], 1.0, col(name, 0, KC),
                            ALU.add, ALU.mult))

            def add_ada_bias(n0, n1):
                dve.wait_ge(sm["mod_done"], n1 // FT)
                for a in range(2):
                    own.did(tt(mod[:, n0:n1, a], mod[:, n0:n1, a], col("ada_b", n0, n1 - n0), ALU.add))
                own.settle()

            def context_norm(step, s):
                if step == 0 and s == 2:
                    add_ada_bias(0, 2 * KC)
                    gain_of(1, KC, "norm1")
                if step == 0 and s in (3, 4, 5):
                    dve.wait_ge(sm["ctx_sq"], s - 1)
                    add_squares(CSQ, s - 2, s == 5)
                if step == 1 and s == 0:
                    inverse_root(N_CTX)
                if step == 1 and s in (1, 2, 4, 5):
                    n = (1, 2, 4, 5).index(s)
                    scaled(CX, quarter(CX, n), lambda k: gmod[:, k:k + 1], n)
                if step == 1 and s in (3, 4, 6, 7):
                    shifted_low(E_CTX, CH, CL, CX, lambda k: mod[:, k, 1:2], (3, 4, 6, 7).index(s))

            def add_piece(a, n, order):
                dve.wait_ge(ada_in[order.base % 2], order.turns(2, 1, 16))
                if n == 0:
                    dve.wait_ge(sm["mt_done"], a.value(1, -1))
                for m in range(2):
                    if order.base or m or order.i is not None:
                        dve.wait_ge(ada_acc, order.value(2, m - 1) if order.since(1) else m)
                    acc = adac[:, a.base % 2, m, :]
                    w, x = adab[:, order.base % 2, m, :], ctmp[:, 0, 2 * n + m:2 * n + m + 1]
                    ins = ts(acc, w, x, None, ALU.mult) if n == 0 else stt(acc, w, x, acc, ALU.mult, ALU.add)
                    ins.then_inc(ada_acc, 1)

            def ff1_step(j, beside=None):
                c, q, a = ff1_place(j)
                for s in range(STEP1):
                    low(c.plus(s))
                    add_piece(a, s, Place(8 * j.base + s, j.i, 8 * j.per))
                    if s < 2 and beside != 0:
                        down_out(q.plus(s - 2), c.plus(s - 2), s + 2)
                    if beside == 0 and s == 1:
                        relu_squared(Place(Q_FF1), Place(0))
                    if s == 2:
                        hidden_low(j)
                    if s == 5:
                        relu_squared(q, j.plus(1))
                    if s == 5 and beside != 0:
                        mod_out(a.plus(-1))
                    if s >= 6:
                        down_out(q.plus(s - 5), c.plus(s - 2), s - 6)
                    if beside is not None:
                        context_norm(beside, s)

            ff1_step(Place(0), 0)
            ff1_step(Place(1), 1)
            with dve.Fori(0, FF1_ITERS) as i:
                ff1_step(Place(2, i, 2))
                ff1_step(Place(3, i, 2))

            def complete(q, n, part):
                dve.wait_ge(acc_free[q.slot], q.turns(2, 1))
                squares(SQ, X, n, part)

            c, q = Place(C_FF1_TAIL), Place(Q_FF1_TAIL)
            for s in range(3 * SLOTS):
                low(c.plus(s))
                for n in range(16):
                    if ADA_TAIL[n] == s:
                        add_piece(Place(ADA_GROUPS - 2 + n // 8), n % 8, Place(8 * (STEPS1 - 2) + n))
                if s < 2:
                    down_out(q.plus(s - 2), c.plus(s - 2), s + 2)
                if s == 2:
                    hidden_low(Place(STEPS1 - 2))
                if s == 4:
                    mod_out(Place(ADA_GROUPS - 3))
                if s == 5:
                    relu_squared(q, Place(STEPS1 - 1))
                if s == 7:
                    hidden_low(Place(STEPS1 - 1))
                if s == 10:
                    mod_out(Place(ADA_GROUPS - 2))
                if s >= 6:
                    down_out(q.plus(s - 5), c.plus(s - 2), (s - 6) % 4)
                if s >= 10:
                    complete(q.plus(s - 5), s - 10, False)
            add_squares(SQ, 1, True)

            def ff1_finish():
                for n in (2, 3):
                    down_out(q.plus(5 + n), c.plus(8 + n), n)
                    complete(q.plus(5 + n), n, True)

            dve.wait_ge(x_lo, 4 * E_CTX + 4)
            gain_of(0, KC, "norm1")
            norm_window(N_MIX_IN, E_NORM3, Place(C_IN2), lambda k: gmod[:, k:k + 1], ff1_finish,
                        lambda k: mod[:, k, 0:1])

            def attention2_step(t):
                u = t - T_ATT2 - 1
                if 0 <= u < 2 * HEADS:
                    b, h, tile = u % 2, u // 2, u % 2
                    dve.wait_ge(sm["sc_done"], u + 1)
                    if u >= 2:
                        dve.wait_ge(sm["exp_done"], u - 1)
                    if u == 0:
                        dve.wait_ge(sm["bias_done"], 8)
                    own.did(tt(S2[:, b, 0:T].rearrange("p (r c) -> p r c", c=GRID_W),
                               bank(4 + b)[:, 0:T].rearrange("p (r c) -> p r c", c=GRID_W),
                               bia[:, tile, ROWS * h:ROWS * h + ROWS, :], ALU.add))
                    own.did(V.tensor_copy(S2[:, b, T:2 * T], bank(4 + b)[:, T:2 * T]))
                    own.settle()
                    settled(V.reduce_max(smx[:, b, 3:4], S2[:, b, :], AX.X))
                    ts(smx[:, b, 0:1], smx[:, b, 3:4], -1.0, None, ALU.mult).then_inc(sm["sm_done"], 1)
                u = t - T_ATT2 - 2
                if 0 <= u < 2 * HEADS:
                    b = u % 2
                    dve.wait_ge(sm["exp_done"], u + 1)
                    settled(V.reciprocal(smx[:, b, 2:3], smx[:, b, 1:2]))
                    ts(P2[:, b, :], P2[:, b, :], smx[:, b, 2:3], None, ALU.mult).then_inc(sm["pn_done"], 1)
                u = t - T_ATT2 - 4
                if 0 <= u < 2 * HEADS:
                    h, tile = u // 2, u % 2
                    dve.wait_ge(sm["tp_done"], u + 1)
                    if h >= 2:
                        dve.wait_ge(sm["pv2_done"], h - 1)
                    V.tensor_copy(PT[:, h % 2, :, tile * P:(tile + 1) * P],
                                  bank(6).rearrange("p (k q) -> p k q", q=P)).then_inc(sm["pt_done"], 1)

            def short_conv(m, tap):
                q = Place(Q_IN2 + 7 + m)
                src = acc_ws(q.slot)
                done(Place(C_IN2 + 4 * (7 + m) + 3))
                for k in range(4):
                    n = 4 * m + k
                    w = col("hy_w", 12 * (1, 0, 2)[tap] + n)
                    if tap == 0:
                        ins = ts(hyC[:, n, :], src[:, k, :], w, col("hy_b", n), ALU.mult, ALU.add)
                    elif tap == 1:
                        ins = stt(hyC[:, n, 1:T], src[:, k, 0:T - 1], w, hyC[:, n, 1:T], ALU.mult, ALU.add)
                    else:
                        ins = stt(hyC[:, n, 0:T - 1], src[:, k, 1:T], w, hyC[:, n, 0:T - 1], ALU.mult, ALU.add)
                if tap < 2:
                    settled(ins)
                else:
                    ins.then_inc(acc_free[q.slot], 1)

            for t in range(4, 10 * SLOTS):
                low(Place(C_IN2 + t))
                if t == 4:
                    mod_out(Place(ADA_GROUPS - 1))
                    add_ada_bias(2 * KC, N_MOD * KC)
                attention2_step(t)
                if t >= 33 and (t - 33) % 4 < 3:
                    short_conv((t - 33) // 4, (t - 33) % 4)

            C1, C2 = 6.28125, 0.0019340515136718750
            C3 = 2 * math.pi - C1 - C2
            ROUND = 1.5 * 2 ** 23

            def sine_argument(n):
                dve.wait_ge(sm["mlp_ps"], n + 1)
                if n:
                    dve.wait_ge(sm["mlp_sin"], 1)
                else:
                    dve.wait_ge(sm["sm_done"], 2 * HEADS)
                a, r = sr[:, 0, :], sr[:, 1, :]
                settled(ts(a, bank(4)[0:64, 0:T], cols[0:64, COLS["mlp"][0] + n:COLS["mlp"][0] + n + 1],
                           cols[0:64, COLS["mlp"][0] + 2:COLS["mlp"][0] + 3], ALU.add, ALU.mult))
                settled(ts(r, a, 1 / (2 * math.pi), ROUND, ALU.mult, ALU.add))
                settled(ts(r, r, ROUND, None, ALU.subtract))
                for c in (C1, C2, C3):
                    settled(stt(a, r, -c, a, ALU.mult, ALU.add))
                ts(a, a, 3.1415925, -3.1415925, ALU.min, ALU.max).then_inc(sm["mlp_arg"], 1)

            low(Place(C_OUT2))
            attention2_step(40)
            low(Place(C_OUT2 + 1))
            for t in range(41, 44):
                attention2_step(t)
                short_conv(2, t - 41)
            sine_argument(0)
            sine_argument(1)
            dve.wait_ge(sm["e_in"], 32)
            dve.wait_ge(sm["fy_ps"], FNG)
            dve.wait_ge(sm["fu_done"], FNG)
            for n in range(4):
                o, t = n // 2, n % 2
                dve.wait_ge(sm["hf_ps"], n + 1)
                if n:
                    dve.wait_ge(sm["hf_done"], n)
                for f in range(2):
                    own.did(tt(hfb[:, f, :], bank(4 + 2 * (n % 2) + f), dec[:, f, t, :], ALU.mult))
                own.settle()
                own.did(tt(hSD[:, o, 0, t, :], hfb[:, 0, :], hfb[:, 1, :], ALU.add))
                tt(hSD[:, o, 1, t, :], hfb[:, 0, :], hfb[:, 1, :], ALU.subtract).then_inc(sm["hf_done"], 1)
            own.settle()

            def products(o):
                dve.wait_ge(sm["zf_ps"], o + 1)
                dve.wait_ge(sm["ks_done"], 5 * o + 5)
                dve.wait_ge(sm["hf_done"], 4)
                if o:
                    dve.wait_ge(sm["ys_done"], o)
                    dve.wait_ge(sm["hz_done"], o)
                re, im = PS[:, 4:6, :], PS[:, 6:8, :]
                own.did(tt(pp[:, 0], re, KS[:, o, 0:2, :], ALU.mult))
                own.did(tt(pp[:, 1], im, KS[:, o, 2:4, :], ALU.mult))
                own.settle()
                settled(tt(YS[:, 0:2, :], pp[:, 0], pp[:, 1], ALU.subtract))
                own.did(tt(pp[:, 0], re, KS[:, o, 2:4, :], ALU.mult))
                own.did(tt(pp[:, 1, 0, :], bank(6), KS[:, o, 4, :], ALU.mult))
                own.did(tt(pp[:, 1, 1, :], bank(7), KS[:, o, 1, :], ALU.mult))
                own.settle()
                tt(YS[:, 2:4, :], pp[:, 0], pp[:, 1], ALU.add).then_inc(sm["ys_done"], 1)

            def gated_output(o):
                dve.wait_ge(sm["yi_ps"], o + 1)
                dve.wait_ge(sm["ys_done"], o + 1)
                dve.wait_ge(acc_free[1], Q_OUT2 // 2)
                src = hyC[:, 0:HT, :] if o == 0 else zT2
                gate = hyC[:, HT * (o + 1):HT * (o + 2), :]
                dst = zT2 if o == 0 else gate
                tmp = pp[:, 0].rearrange("p a (b t) -> p (a b) t", t=T)
                for k in range(HT):
                    own.did(stt(tmp[:, k, :], src[:, k, :], col("hy_bias", HT * o + k),
                                bank(2 + k // 2)[:, (k % 2) * T:(k % 2 + 1) * T], ALU.mult, ALU.add))
                own.settle()
                tt(dst[:, 0:HT, :], tmp, gate, ALU.mult).then_inc(sm["hz_done"], 1)

            products(0)
            dve.wait_ge(sm["mix_sq"], 2)
            add_squares(SM, 1, True)
            dve.wait_ge(sm["fy_done"], FNG)
            tt(quarter(SM, 2), fY[:, :, :], fY[:, :, :], ALU.mult).then_inc(sm["norm_sq"], 1)
            gated_output(0)
            inverse_root(N_A)
            for n in range(2):
                scaled(SM, quarter(q2, n), lambda k: col("mix", k), n)
            for n in range(2):
                split_low(E_OUT2, XH, XL, quarter(SM, n), n)
            products(1)
            inverse_root(N_F)
            scaled(SM, fY[:, :, :], lambda k: col("mix", k), 2)
            split_low(E_OUT2, XH, XL, quarter(SM, 2), 2)
            gated_output(1)
            dve.wait_ge(sm["hz_done"], 2)
            tt(quarter(SM, 3), quarter(hyC, 2), quarter(hyC, 2), ALU.mult).then_inc(sm["norm_sq"], 1)
            low(Place(C_OUT2 + 2))
            inverse_root(N_H)
            scaled(SM, quarter(hyC, 2), lambda k: col("mix", k), 3)
            split_low(E_OUT2, XH, XL, quarter(SM, 3), 3)

            def residual2(g):
                q = Place(Q_OUT2 + g)
                done(Place(C_OUT2 + 4 * g + 3))
                for k in range(4):
                    ins = stt(X[:, 4 * g + k, :], acc_ws(q.slot)[:, k, :], mod[:, 2 * KC + 4 * g + k, 0:1],
                              X[:, 4 * g + k, :], ALU.mult, ALU.add)
                ins.then_inc(acc_free[q.slot], 1)

            for t in range(3, 4 * SLOTS):
                low(Place(C_OUT2 + t))
                if t == 4:
                    gain_of(0, 4 * KC, "norm2")
                if t in (5, 9, 13):
                    residual_squares(C_OUT2, Q_OUT2, (t - 5) // 4, residual2)
                if t in (10, 14):
                    add_squares(NT, (t - 6) // 4, t == 14)
            norm_window(N_FF2, E_NORM4, Place(C_FF2), lambda k: gmod[:, k:k + 1],
                        lambda: residual_squares(C_OUT2, Q_OUT2, 3, residual2), lambda k: mod[:, 3 * KC + k, 0:1])

            def gate_conv(q, j, s):
                w = lambda n, k: cw[:, 4 * k + n:4 * k + n + 1]
                if s == 0:
                    c0 = j.value(4 * FT, COLS["ff_w"][0])
                    src = cols[:, c0:c0 + 4 * FT] if j.i is None else cols[:, bass.ds(c0, 4 * FT)]
                    V.tensor_copy(cw[:, :], src).then_inc(sm["cw_done"], 1)
                    dve.wait_ge(acc_free[q.slot], q.turns(2, 1))
                    dve.wait_ge(sm["cw_done"], j.value(1, 1))
                    for k in range(FT):
                        ins = ts(CV[:, k, :], GS[:, k, :], w(1, k), w(3, k), ALU.mult, ALU.add)
                    ins.then_inc(sm["conv_a"], 1)
                if s == 1:
                    dve.wait_ge(sm["conv_a"], j.value(1, 1))
                    for k in range(FT):
                        ins = stt(CV[:, k, 1:T], GS[:, k, 0:T - 1], w(0, k), CV[:, k, 1:T], ALU.mult, ALU.add)
                    ins.then_inc(sm["conv_b"], 1)
                if s == 2:
                    dve.wait_ge(sm["conv_b"], j.value(1, 1))
                    for k in range(FT):
                        ins = stt(CV[:, k, 0:T - 1], GS[:, k, 1:T], w(2, k), CV[:, k, 0:T - 1], ALU.mult, ALU.add)
                    ins.then_inc(sm["conv_done"], 1)

            def gated(q, c, j):
                done(c)
                dve.wait_ge(sm["gelu_done"], j.value(1, 1))
                dve.wait_ge(sm["hid_lo"], j.value(1, STEPS1))
                tt(FQ[:, :, :], acc_ws(q.slot), CV[:, :, :], ALU.mult).then_inc(acc_free[q.slot], 1)

            def down_out2(q, c, s):
                done(c)
                for k in range(4):
                    ins = stt(X[:, 4 * s + k, :], acc_ws(q.slot)[:, k, :], mod[:, 5 * KC + 4 * s + k, 0:1],
                              X[:, 4 * s + k, :], ALU.mult, ALU.add)
                ins.then_inc(acc_free[q.slot], 1)

            def ff2_step(j, first=False):
                c, q = ff2_place(j)
                for s in range(STEP2):
                    low(c.plus(s))
                    if first:
                        if s == 1:
                            gated(q.plus(-1), c.plus(-1), Place(0))
                        if s == 3:
                            hidden_low(Place(0), STEPS1)
                    elif s < 2:
                        down_out2(q.plus(s - 2), c.plus(s - 2), s + 2)
                    if 5 <= s < 8:
                        gate_conv(q, j.plus(1), s - 5)
                    if s == 9:
                        gated(q.plus(1), c.plus(7), j.plus(1))
                    if s >= 10:
                        down_out2(q.plus(s - 8), c.plus(s - 2), s - 10)
                    if s == 11:
                        hidden_low(j.plus(1), STEPS1)

            for s in range(4, 8):
                low(Place(C_FF2 + s))
                if s >= 5:
                    gate_conv(Place(Q_FF2), Place(0), s - 5)
            ff2_step(Place(0), first=True)
            ff2_step(Place(1))
            with dve.Fori(0, FF2_ITERS) as i:
                ff2_step(Place(2, i, 2))
                ff2_step(Place(3, i, 2))
            c, q = Place(C_END - 4), Place(Q_END - 4)
            for s in range(4):
                low(c.plus(s))
                if s < 2:
                    down_out2(q.plus(s - 2), c.plus(s - 2), s + 2)
                else:
                    down_out2(q.plus(s - 2), c.plus(s - 2), s - 2)
                    complete(q.plus(s - 2), s - 2, False)
            add_squares(SQ, 1, True)
            for n in (2, 3):
                down_out2(q.plus(n), c.plus(n), n)
                complete(q.plus(n), n, True)
            inverse_root(N_LAST)
            for n in range(4):
                scaled(NT, quarter(X, n), lambda k: col("final", k), n)

        @block.tensor
        def _(pe):
            MM = nc.tensor.matmul

            def half_ready(c, h):
                pe.wait_ge(lo_done, c.value(2, h + 1))

            def use(q):
                if q.since(2):
                    pe.wait_ge(acc_free[q.slot], q.turns(2))

            def ws(out, c, xh, xl, first, last, kk):
                b = c.base % 2
                for f in range(FT):
                    cs = slice(f * P, (f + 1) * P)
                    wh, wl = WH[:, b, kk, cs], WL[:, b, kk, cs]
                    MM(out[:, f, :], wh, xh, start=first and f % 2 == 0, stop=False, skip_group_check=True)
                    MM(out[:, f, :], wh, xl, start=False, stop=False, skip_group_check=True)
                    ins = MM(out[:, f, :], wl, xh, start=False, stop=last, skip_group_check=True)
                return ins

            def tok(out, c, xh, xl, first, last, kk):
                b = c.base % 2
                wh, wl = WH[:, b, kk, :], WL[:, b, kk, :]
                for t in range(TT):
                    h, l = xh[:, t * P:(t + 1) * P], xl[:, t * P:(t + 1) * P]
                    MM(out[:, t, :], h, wh, start=first, stop=False)
                    MM(out[:, t, :], h, wl, start=False, stop=False)
                    ins = MM(out[:, t, :], l, wh, start=False, stop=last)
                return ins

            def product(c, q, s, xh, xl, k0=0, first=True, last=True, fn=ws, out=None, e=None):
                if q is not None and first:
                    use(q)
                if e is not None:
                    pe.wait_ge(x_lo, 4 * e + s + 1)
                if out is None:
                    out = (acc_ws if fn is ws else acc_as)(q.slot)
                for h in range(2):
                    half_ready(c, h)
                    for kk in range(HF * h, HF * h + HF):
                        ins = fn(out, c, xh[:, k0 + kk, :], xl[:, k0 + kk, :], first and kk == 0,
                                 last and kk == FT - 1, kk)
                    ins.then_inc(pe_half, 1)

            def wide(c, q, s, fn=ws, e=None, xh=XH, xl=XL):
                product(c, q, s, xh, xl, 4 * s, s == 0, s == SLOTS - 1, fn, e=e)

            def down(c, q, j, s, before=0):
                if s == 0:
                    pe.wait_ge(sm["hid_lo"], j.value(1, before + 1))
                product(c, q, s, HH[:, j.base % 2], HL[:, j.base % 2])

            def ada(c, a, s):
                if s == 0 and a.since(1):
                    pe.wait_ge(sm["row_done"], a.value())
                out = bank(7)[0:4, :]
                for h in range(2):
                    half_ready(c, h)
                    for kk in range(HF * h, HF * h + HF):
                        k = 4 * s + kk
                        MM(out, csil[:, k, :], WH[:, c.base % 2, kk, :], start=k == 0, stop=False)
                        ins = MM(out, csil[:, k, :], WL[:, c.base % 2, kk, :], start=False, stop=k == KC - 1)
                    ins.then_inc(pe_half, 1)

            def mod_columns(a):
                pe.wait_ge(sm["row_done"], a.value(1, 1))
                if a.since(1):
                    pe.wait_ge(sm["mod_done"], a.value())
                for f in range(FT):
                    ins = MM(bank(6)[:, 2 * f:2 * f + 2], MR[:, f * P:(f + 1) * P], sel[:, :], start=True, stop=True)
                ins.then_inc(sm["mt_done"], 1)

            def norm_sum(norm, sq, parts=None):
                every = PARTS[norm]
                for n in range(len(every)) if parts is None else parts:
                    if n == 0 and norm:
                        pe.wait_ge(sm["norm_rt"], norm)
                    pe.wait_ge(sm["norm_sq"], PARTS_BEFORE[norm] + n + 1)
                    for k in range(4):
                        ins = MM(bank(SUM_BANK[norm])[:, 0:T], ones, sq[:, 4 * every[n] + k, :],
                                 start=n == 0 and k == 0, stop=n == len(every) - 1 and k == 3)
                    if n == len(every) - 1:
                        ins.then_inc(sm["norm_sum"], 1)

            def spatial_gating(n):
                pe.wait_ge(sm["mix_done"], TT + 1)
                if n >= 2:
                    pe.wait_ge(sm["s_done"], n - 1)
                for g in range(2):
                    for c in range(TT):
                        ins = MM(bank(6 + n % 2)[:, (TT * g + c) * P:(TT * g + c + 1) * P],
                                 vg[:, c, (2 * n + g) * P:(2 * n + g + 1) * P], wsp[:, 2 * n + g, :],
                                 start=True, stop=True)
                ins.then_inc(sm["sgu_ps"], 1)

            def head_sums(n):
                pe.wait_ge(sm["qk_sqd"], n + 1)
                for half in range(2):
                    if n:
                        pe.wait_ge(sm["qk_rt"], 2 * n + half - 1)
                    MM(bank(4 + half), ones, qk_sq[:, 2 * half:2 * half + 2, :], start=True, stop=True)\
                        .then_inc(sm["qk_sum"], 1)

            def attention_step(h, t):
                if t == 0:
                    if h == 0:
                        pe.wait_ge(sm["q_done"], 8)
                    else:
                        pe.wait_ge(sm["zs_done"], h)
                    MM(bank(4)[:, 0:T], kT[:, h, 0:P], qT[:, h, :], start=True, stop=True)
                    MM(bank(4)[:, T:384], kT[:, h, P:T], qT[:, h, P:T], start=True, stop=True)\
                        .then_inc(sm["z_done"], 1)
                if t == 3:
                    pe.wait_ge(sm["lk_done"], h + 1)
                    if h:
                        pe.wait_ge(sm["o_done"], h)
                    MM(bank(5)[:, 0:384], lower, lk[:, 0, :], start=True, stop=False)
                    MM(bank(5)[:, P:T], ones, lk[:, 0, T:384], start=False, stop=True).then_inc(sm["cum_done"], 1)
                if t == 6:
                    pe.wait_ge(sm["am_done"], h + 1)
                    if h == 0:
                        for n in range(2):
                            pe.wait_ge(acc_free[n], Q_GATE // 2)
                    c = slice(h * DH, (h + 1) * DH)
                    MM(bank(5)[:, 0:T], v1[:, 0, c], aw[:, 0, 0:T], start=True, stop=False)
                    MM(bank(5)[:, P:T], v1[:, 1, c], aw[:, 0, T:384], start=False, stop=True)\
                        .then_inc(sm["pv_done"], 1)

            pe.wait_ge(sm["mats_in"], 32)
            norm_sum(N_IN, NT)
            for c in range(C_OAB):
                if T_SGU <= c < T_SGU + 8 and (c - T_SGU) % 2 == 0:
                    spatial_gating((c - T_SGU) // 2)
                if T_QK < c < T_QK + 16 and (c - T_QK) % 4 == 1:
                    head_sums((c - T_QK) // 4)
                if T_ATT <= c < T_ATT + S_ATT * HEADS:
                    attention_step(*divmod(c - T_ATT, S_ATT))
                if c >= C_GATE + 11 and c % 8 == 3:
                    mod_columns(Place((c - C_GATE - 11) // 8))
                if c < C_GATE:
                    g, s = divmod(c, 4)
                    wide(Place(c), Place(g), s, tok if g in (0, 1, 8, 9) else ws, E_NORM1 if g == 0 else None)
                elif c % 2 == 0:
                    g, s = divmod((c - C_GATE) // 2, 4)
                    wide(Place(c), Place(Q_GATE + g), s)
                else:
                    if c == C_GATE + 1:
                        pe.wait_ge(sm["csil_done"], 1)
                        pe.wait_ge(sm["s_done"], 4)
                    a, s = divmod((c - C_GATE) // 2, 4)
                    ada(Place(c), Place(a), s)
            for n in range(4):
                for s in range(SLOTS):
                    c = Place(C_OAB + 4 * n + s)
                    if n == 0 and s == 3:
                        mod_columns(Place(7))
                    if n == 1 and s == 2:
                        pe.wait_ge(sm["mod_done"], 8)
                    if s == 2 and n >= 2:
                        pe.wait_ge(sm["b_free"], n - 1)
                    product(c, Place(Q_OAB + n) if s < 2 else None, s, XH, XL, 4 * s, s % 2 == 0, s % 2 == 1,
                            out=acc_ws((Q_OAB + n) % 2) if s < 2 else ctx_ws(n), e=E_OAB)
            for t in range(4 * SLOTS):
                if t == 15:
                    norm_sum(N_FF1, NT, [0])
                wide(Place(C_OUT1 + t), Place(Q_OUT1 + t // 4), t % 4, e=E_OUT1, xh=MH, xl=ML)
            norm_sum(N_FF1, NT, [1])

            def sum_columns(a):
                pe.wait_ge(ada_acc, a.value(16, 16 - 16 * ADA_GATE))
                pe.wait_ge(sm["mod_done"], a.value())
                for f in range(FT):
                    for m in range(2):
                        ins = MM(bank(6)[:, 2 * f:2 * f + 2], adac[:, a.base % 2, m, f * P:(f + 1) * P],
                                 ones[:, 0:2], start=m == 0, stop=m == 1)
                ins.then_inc(sm["mt_done"], 1)

            def ff1_step(j, first=False):
                c, q, a = ff1_place(j)
                for s in range(SLOTS):
                    if s == 3 and not first:
                        sum_columns(a.plus(-1))
                    wide(c.plus(s), q, s)
                for s in range(SLOTS):
                    if first and s == 3:
                        norm_sum(N_CTX, CSQ)
                    down(c.plus(4 + s), q.plus(1 + s), j, s)

            for s in range(SLOTS):
                wide(Place(C_FF1 + s), Place(Q_FF1), s, e=E_NORM2)
            ff1_step(Place(0), True)
            ff1_step(Place(1))
            with pe.Fori(0, FF1_ITERS) as i:
                ff1_step(Place(2, i, 2))
                ff1_step(Place(3, i, 2))
            c, q = Place(C_FF1_TAIL), Place(Q_FF1_TAIL)
            for s in range(SLOTS):
                if s == 3:
                    sum_columns(Place(ADA_GROUPS - 3))
                wide(c.plus(s), q, s)
            for s in range(2 * SLOTS):
                if s == 4:
                    sum_columns(Place(ADA_GROUPS - 2))
                down(c.plus(4 + s), q.plus(1 + s), Place(STEPS1 - 2 + s // 4), s % 4)
            norm_sum(N_MIX_IN, SQ)

            def beside_context(n, s):
                if s == 0 and n >= 2:
                    pe.wait_ge(sm["ctx_free"], n - 1)
                if s == 0 and n == 1:
                    pe.wait_ge(sm["norm_rt"], N_MIX_IN + 1)
                    pe.wait_ge(sm["mod_done"], ADA_GROUPS)
                c = Place(C_IN2 + 4 * n + s)
                fn, out = (ws, ctx_ws(n)) if n < 2 else (tok, ctx_as(n))
                for h in range(2):
                    half_ready(c, h)
                    for kk in range(HF * h, HF * h + HF):
                        k = 4 * s + kk
                        fn(out, c, CH[:, k, :], CL[:, k, :], k == 0, k == KC - 1, kk)

            def bias_columns(n):
                if n >= 4:
                    pe.wait_ge(sm["bias_done"], n - 3)
                for c in range(8):
                    ins = MM(bank(4 + n % 4)[:, c * 64:(c + 1) * 64], bsel[:, n // 2 % 2, 8 * (n % 2) + c, :],
                             brow[:, :], start=True, stop=True)
                ins.then_inc(sm["bias_ps"], 1)

            def attention2_step(t):
                u = t - T_ATT2 - 3
                if 0 <= u < 2 * HEADS:
                    b = u % 2
                    pe.wait_ge(sm["pn_done"], u + 1)
                    if u >= 1:
                        pe.wait_ge(sm["pt_done"], u)
                    for k in range(4):
                        ins = nc.tensor.transpose(bank(6)[:, k * P:(k + 1) * P], P2[:, b, k * P:(k + 1) * P], ident)
                    ins.then_inc(sm["tp_done"], 1)
                u = t - T_ATT2 - 5
                if 0 <= u < 2 * HEADS and u % 2:
                    h = u // 2
                    pe.wait_ge(sm["pt_done"], u + 1)
                    if h:
                        pe.wait_ge(sm["a2_done"], h)
                    c = slice(h * DH, (h + 1) * DH)
                    for k in range(4):
                        ins = MM(bank(7)[:, 0:T], (v2 if k < 2 else vc2)[:, k % 2, c], PT[:, h % 2, k, :],
                                 start=k == 0, stop=k == 3)
                    ins.then_inc(sm["pv2_done"], 1)
                u = t - T_ATT2
                if 0 <= u < 2 * HEADS:
                    b, h, tile = u % 2, u // 2, u % 2
                    if u >= 2:
                        pe.wait_ge(sm["sm_done"], u - 1)
                    else:
                        pe.wait_ge(sm["bias_done"], 5 + u)
                    if u % 8 == 0:
                        q = Place(Q_IN2 + 4 + u // 8)
                        pe.wait_ge(acc_free[q.slot], q.turns(2, 1))
                    qs = q2[:, h, tile * P:(tile + 1) * P]
                    MM(bank(4 + b)[:, 0:T], qs, k2[:, h, :], start=True, stop=True)
                    MM(bank(4 + b)[:, T:2 * T], qs, kc2[:, h, :], start=True, stop=True).then_inc(sm["sc_done"], 1)

            pe.wait_ge(x_lo, 4 * E_CTX + 4)
            for s in range(2):
                beside_context(0, s)
            for t in range(10 * SLOTS):
                n, s = divmod(t, SLOTS)
                if t == 2:
                    sum_columns(Place(ADA_GROUPS - 1))
                if 2 <= t < 4 * SLOTS:
                    beside_context(n, s)
                if t == T_BIAS + 3:
                    pe.wait_ge(sm["ctx_free"], 4)
                    pe.wait_ge(sm["brow_in"], 16)
                if t in (T_BIAS + 3, T_BIAS + 4, T_BIAS + 6, T_BIAS + 7):
                    m = (T_BIAS + 3, T_BIAS + 4, T_BIAS + 6, T_BIAS + 7).index(t)
                    pe.wait_ge(bsel_in[m % 2], 16 * (m // 2 + 1))
                    bias_columns(2 * m)
                    bias_columns(2 * m + 1)
                attention2_step(t)
                wide(Place(C_IN2 + t), Place(Q_IN2 + n), s, tok if n in (2, 3, 6) else ws,
                     E_NORM3 if n == 0 else None)

            def fourier_tokens(n):
                if n >= 2:
                    pe.wait_ge(sm["fu_done"], n - 1)
                for t in range(TT):
                    ins = MM(bank(n % 2), fX[:, t, n * P:(n + 1) * P], fcl[:, t, :], start=t == 0, stop=t == 1)
                ins.then_inc(sm["fu_ps"], 1)

            for t in (40, 41, 42):
                attention2_step(t)
            pe.wait_ge(sm["mlp_in"], 48)
            pe.wait_ge(sm["sm_done"], 2 * HEADS)
            MM(bank(4)[0:64, 0:T], w1h[:, :], pz[:, :], start=True, stop=True).then_inc(sm["mlp_ps"], 1)
            pe.wait_ge(sm["four_in"], 32)
            pe.wait_ge(acc_free[0], Q_OUT2 // 2)
            fourier_tokens(0)
            attention2_step(43)
            attention2_step(44)
            fourier_tokens(1)
            fourier_tokens(2)
            fourier_tokens(3)
            pe.wait_ge(sm["mlp_sin"], 1)
            MM(bank(4)[0:64, 0:T], w2h[:, :], hdn[:, 0, :], start=True, stop=True).then_inc(sm["mlp_ps"], 1)
            pe.wait_ge(acc_free[1], Q_OUT2 // 2)
            pe.wait_ge(sm["pt_done"], 2 * HEADS)
            for n in range(FNG):
                pe.wait_ge(sm["fu_done"], n + 1)
                if n >= 2:
                    pe.wait_ge(sm["fy_done"], n - 1)
                for m in range(2):
                    ins = MM(bank((2, 6)[n % 2])[:, 0:T], fcd[:, m, :], fU[:, n, m * T:(m + 1) * T],
                             start=m == 0, stop=m == 1)
                ins.then_inc(sm["fy_ps"], 1)
            pe.wait_ge(sm["mlp_sin"], 2)
            pe.wait_ge(sm["mlp3_in"], 16)
            for n in range(4):
                o, t = n // 2, n % 2
                if n == 1:
                    pe.wait_ge(sm["fy_done"], FNG)
                    pe.wait_ge(sm["a2_done"], HEADS)
                if n >= 2:
                    pe.wait_ge(sm["hf_done"], n - 1)
                for f in range(2):
                    c0 = o * 2 * HW + f * HW
                    ins = MM(bank(4 + 2 * (n % 2) + f), hdn[:, 1, t * P:(t + 1) * P], w3h[:, c0:c0 + HW],
                             start=True, stop=True)
                ins.then_inc(sm["hf_ps"], 1)

            def spectrum(n):
                o, m = n // 5, n % 5
                pe.wait_ge(sm["hf_done"], 2 * o + 2)
                if n >= 2:
                    pe.wait_ge(sm["ks_done"], n - 1)
                e0 = (0, P, 2 * P, 3 * P, 5 * P)[m]
                for t in range(TT):
                    ins = MM(bank(n % 2), Ef[:, t, e0:e0 + P], hSD[:, o, 1 if m in (2, 3) else 0, t, :],
                             start=t == 0, stop=t == 1)
                ins.then_inc(sm["ks_ps"], 1)

            def to_tokens(o):
                if o:
                    pe.wait_ge(sm["hz_done"], 1)
                src = hyC if o == 0 else zT2
                for t in range(TT):
                    for k in range(HT):
                        ins = nc.tensor.transpose(bank(2 + t)[:, k * P:(k + 1) * P], src[:, k, t * P:(t + 1) * P],
                                                  ident)
                    ins.then_inc(sm["zt_ps"], 1)

            def forward(o):
                pe.wait_ge(sm["zt_done"], TT * (o + 1))
                if o == 0:
                    pe.wait_ge(sm["hf_done"], 4)
                for w, e0 in enumerate((0, P, 4 * P, 3 * P)):
                    for t in range(TT):
                        ins = MM(bank(4 + w), Ef[:, t, e0:e0 + P], zt[:, t, :], start=t == 0, stop=t == 1)
                ins.then_inc(sm["zf_ps"], 1)

            def inverse(o):
                pe.wait_ge(sm["ys_done"], o + 1)
                for k in range(HT):
                    for w in range(4):
                        ins = MM(bank(2 + k // 2)[:, (k % 2) * T:(k % 2 + 1) * T], YS[:, w, k * P:(k + 1) * P],
                                 Gi[:, w, :], start=w == 0, stop=w == 3)
                ins.then_inc(sm["yi_ps"], 1)

            pe.wait_ge(sm["fu_done"], FNG)
            pe.wait_ge(sm["e_in"], 32)
            for n in range(5):
                spectrum(n)
            to_tokens(0)
            forward(0)
            for n in range(5, 10):
                spectrum(n)
            pe.wait_ge(sm["gi_in"], 16)
            inverse(0)
            pe.wait_ge(sm["ks_done"], 10)
            norm_sum(N_A, SM)
            to_tokens(1)
            forward(1)
            norm_sum(N_F, SM)
            pe.wait_ge(sm["norm_rt"], N_F + 1)
            wide(Place(C_OUT2), Place(Q_OUT2), 0, e=E_OUT2)
            inverse(1)
            wide(Place(C_OUT2 + 1), Place(Q_OUT2), 1, e=E_OUT2)
            norm_sum(N_H, SM)
            wide(Place(C_OUT2 + 2), Place(Q_OUT2), 2, e=E_OUT2)
            wide(Place(C_OUT2 + 3), Place(Q_OUT2), 3, e=E_OUT2)
            pe.wait_ge(sm["hz_done"], 2)
            for t in range(4, 4 * SLOTS):
                if t == 15:
                    norm_sum(N_FF2, NT, [0])
                wide(Place(C_OUT2 + t), Place(Q_OUT2 + t // 4), t % 4)
            norm_sum(N_FF2, NT, [1])

            def ff2_step(j):
                c, q = ff2_place(j)
                for s in range(SLOTS):
                    wide(c.plus(s), q, s)
                for s in range(SLOTS):
                    wide(c.plus(4 + s), q.plus(1), s)
                for s in range(SLOTS):
                    down(c.plus(8 + s), q.plus(2 + s), j, s, STEPS1)

            for s in range(SLOTS):
                wide(Place(C_FF2 + s), Place(Q_FF2), s, e=E_NORM4)
            for s in range(SLOTS):
                wide(Place(C_FF2 + 4 + s), Place(Q_FF2 + 1), s)
            ff2_step(Place(0))
            ff2_step(Place(1))
            with pe.Fori(0, FF2_ITERS) as i:
                ff2_step(Place(2, i, 2))
                ff2_step(Place(3, i, 2))
            for s in range(SLOTS):
                down(Place(C_END - 4 + s), Place(Q_END - 4 + s), Place(STEPS2 - 1), s, STEPS1)
            norm_sum(N_LAST, SQ)


def shape_constants():
    f = np.float32
    out = {}
    r = np.arange(P)
    out["mats"] = np.stack([np.ones((P, P)), np.eye(P), r[:, None] > r[None, :], r[:, None] < r[None, :]], 1).astype(f)
    out["sel"] = np.array([[1, 0], [0, 1], [1, 0], [0, 1]], f)
    s = np.zeros((2, 32, GRID_W, 2, GRID_W), f)
    for c in range(GRID_W):
        c0 = min(max(c - NA_KW // 2, 0), GRID_W - NA_KW)
        for k in range(GRID_W):
            row = k - c + NA_KW - 1 if c0 <= k < c0 + NA_KW else 31
            for half in range(2):
                s[half, row, k, half, c] = 1
    out["bsel"] = s.reshape(64, GRID_W, P)
    tok = 2 * np.pi * np.outer(np.arange(T), np.arange(T)) / T
    cl = np.concatenate([np.cos(tok), np.sin(tok)], 1) / np.sqrt(T)
    out["fcl"] = cl.reshape(TT, P, 2 * T).transpose(1, 0, 2).astype(f)
    ch = 2 * np.pi * np.outer(r, r) / P
    out["fcd"] = (np.stack([np.cos(ch), -np.sin(ch)], 1) / np.sqrt(P)).astype(f)
    t = np.arange(T)
    ang = 2 * np.pi * np.outer(t, np.arange(T)) / L2
    cos, sin = np.cos(ang), -np.sin(ang)
    alt = (-1.0) ** t
    im0, re0 = sin[:, :P].copy(), cos[:, :P].copy()
    im0[:, 0] = alt
    re0[:, 0] = alt
    ef = np.concatenate([cos, sin, im0, re0], 1)
    out["ef"] = ef.reshape(TT, P, 6 * P).transpose(1, 0, 2).astype(f)
    g = np.concatenate([cos.T * 2, sin.T * 2], 0) / L2
    g[0] /= 2
    g[T] = alt / L2
    out["gi"] = g.reshape(4, P, T).transpose(1, 0, 2).astype(f)
    pos = np.arange(T, dtype=f)[:, None]
    tn = pos / f(T - 1)
    bands = np.linspace(1e-4, 15, 16, dtype=f)
    a = (bands * f(2.0 * math.pi / T)).astype(f) * pos
    out["pz"] = np.ascontiguousarray(np.concatenate([tn, np.cos(a), -np.sin(a)], 1).T.astype(f))
    deltas = np.linspace(math.log(1e-2) / 1.5, math.log(1e-2) / 0.3, HW, dtype=f)
    decay = np.exp(-tn * np.abs(deltas)).astype(f)
    back = decay.copy()
    back[0] = 0
    out["dec"] = np.stack([decay, back]).reshape(2, TT, P, HW).transpose(2, 0, 1, 3)
    return out


def lay_out(v):
    def columns(a):
        return np.asarray(a).reshape(-1, P).T

    def padded(a):
        return np.concatenate([a, np.zeros((P - a.shape[0], a.shape[1]), a.dtype)], 0)

    a = {k: v[k][0] for k in ("w_in", "w_oa", "w_ob", "w_out", "w_ff1", "w_ff2", "w_in_2", "w_out_2")}
    a["ada_w"], a["w_up"], a["w_down"] = v["ada_w_2"][0], v["ffn_w_up_2"][0], v["ffn_w_down_2"][0]
    a["hy_w1"], a["hy_w2"], a["hy_w3"] = v["hy_w1_2"][0], v["hy_w2_2"][0], v["hy_w3_2"][0]
    a["x"], a["ctx"] = v["x"][0].T, v["ctx_2"][0].T
    ffw = np.concatenate([v["ffn_conv_w_2"][0], v["ffn_conv_b_2"]], 0)
    ffw = ffw.reshape(4, STEPS2, FT, P).transpose(3, 1, 2, 0).reshape(P, -1)
    parts = dict(g_mix=columns(v["g_mix"]), g_q=columns(v["g_q"]), g_k=columns(v["g_k"]), g_ff=columns(v["g_ff"]),
                 norm1=columns(v["norm1_g_2"]), norm2=columns(v["norm2_g_2"]), mix=columns(v["mix_norm_g_2"]),
                 final=columns(v["final_norm_g_2"]), ada_b=columns(v["ada_b_2"]), hy_w=columns(v["hy_conv_w_2"]),
                 hy_b=columns(v["hy_conv_b_2"]), hy_bias=columns(v["hy_bias_2"]), ff_w=ffw,
                 c=np.concatenate([columns(v["c_2"]), columns(v["c_ctx_2"])], 1),
                 mlp=padded(np.stack([v["hy_b1_2"][0], v["hy_b2_2"][0], v["hy_freq_2"][0]], 1)))
    assert all(parts[n].shape[1] == w for n, (_, w) in COLS.items())
    a["cols"] = np.concatenate([parts[n] for n in COLS], 1)
    a["ln_g"] = np.broadcast_to(v["sgu_ln_g"], (P, 1024))
    a["ln_b"] = np.broadcast_to(v["sgu_ln_b"], (P, 1024))
    a["b_sp"] = np.broadcast_to(v["b_spatial"], (P, 8, P))
    a["w_sp"] = v["w_spatial"][0].transpose(2, 0, 1)
    rpb = v["na_rpb_2"][0]
    rows = [[[NA_KH - 1 + r - (2 * t + half) for r in range(ROWS)] for t in range(TT)] for half in range(2)]
    b = rpb[:, np.array(rows), :].transpose(1, 4, 2, 0, 3)
    neg = np.full((2, 1) + b.shape[2:], NEG, b.dtype)
    a["brow"] = np.concatenate([b, neg], 1).reshape(64, 64)
    a.update(shape_constants())
    return {k: np.ascontiguousarray(x) for k, x in a.items()}


def kernel(**inputs):
    import concourse.bacc as bacc
    from concourse.bass_utils import run_bass_kernel_spmd

    nc = bacc.Bacc("TRN2", target_bir_lowering=False, num_devices=1)
    arrays = lay_out({k: np.asarray(x) for k, x in inputs.items()})
    d = {k: nc.dram_tensor("in_" + k, a.shape, mybir.dt.from_np(a.dtype), kind="ExternalInput").ap()
         for k, a in arrays.items()}
    out = nc.dram_tensor("out", (D, T), mybir.dt.float32, kind="ExternalOutput").ap()
    build_program(nc, d, out)
    r = run_bass_kernel_spmd(nc, [{"in_" + k: a for k, a in arrays.items()}], core_ids=[0])
    return np.ascontiguousarray(r.results[0]["out"].T)[None]
```

```python
import math
import numpy as np
import concourse.bass as bass
from concourse import mybir
from contextlib import ExitStack

P = 128
T = 256
TT = T // P
D = 2048
KC = D // P
NB = 512
FT = NB // P
SLOTS = 4
HEADS = 8
DH = 128
CHUNK = 64
GRID_W, NA_KH, NA_KW = 64, 8, 16
ROWS = T // GRID_W
FNG = 4
HW = 512
HT = HW // P
D_FF1, D_FF2 = 8192, 5632
STEPS1, STEPS2 = D_FF1 // NB, D_FF2 // NB
N_MOD = 6
EPS = 1e-6
NEG = -1e30
SCALE = DH ** -0.5
L2 = 2 * T

COLS = {}
_n = 0
for _name, _w in [("g_mix", KC), ("g_q", HEADS), ("g_k", HEADS), ("g_ff", KC), ("norm1", KC), ("norm2", KC),
                  ("mix", KC), ("final", KC), ("ada_b", N_MOD * KC), ("hy_w", 3 * 12), ("hy_b", 12),
                  ("hy_bias", 2 * HT), ("ff_w", STEPS2 * 4 * FT), ("c", 2 * KC), ("mlp", 3)]:
    COLS[_name] = (_n, _w)
    _n += _w
NCOLS = _n

STEP1, STEP2 = 2 * SLOTS, 3 * SLOTS
C_GATE = 10 * SLOTS
C_OAB = C_GATE + 8 * SLOTS
C_OUT1 = C_OAB + 4 * SLOTS
C_FF1 = C_OUT1 + 4 * SLOTS
C_FF1_STEPS = C_FF1 + SLOTS
FF1_ITERS = (STEPS1 - 4) // 2
C_FF1_TAIL = C_FF1_STEPS + STEP1 * (STEPS1 - 2)
C_IN2 = C_FF1_TAIL + 3 * SLOTS
C_OUT2 = C_IN2 + 10 * SLOTS
C_FF2 = C_OUT2 + 4 * SLOTS
C_FF2_STEPS = C_FF2 + 2 * SLOTS
FF2_ITERS = (STEPS2 - 3) // 2
C_END = C_FF2 + STEP2 * STEPS2
Q_GATE, Q_OAB, Q_OUT1, Q_FF1 = 10, 18, 22, 26
Q_FF1_TAIL = Q_FF1 + 1 + 5 * (STEPS1 - 2)
Q_IN2 = Q_FF1_TAIL + 9
Q_OUT2 = Q_IN2 + 10
Q_FF2 = Q_OUT2 + 4
Q_END = Q_FF2 + 6 * STEPS2
T_ADA, S_ADA, ADA_AT = 4, 12, [0, 1, 3, 4, 6, 7, 9, 10]
ADA_GATE = 8
ADA_GROUPS = N_MOD * KC // FT
ADA_TAIL = [n * 11 // 16 for n in range(16)]
IN1_COLS = [0, 512, 1024, 1536, 2048, 2560, 4096, 4608, 3072, 3584]
GATE_COL = 5120
IN2_COLS = [1024, 1536, 2048, 2560, 0, 512, 3072, 3584, 4096, 4608]
T_QK, T_ATT, S_ATT, T_LN, T_SGU = 6, 22, 5, 34, 44
T_BIAS, T_ATT2 = 17, 24
E_NORM1, E_OAB, E_OUT1, E_NORM2, E_CTX, E_NORM3, E_OUT2, E_NORM4 = range(8)
WINDOWS = [E_NORM1, E_NORM2, E_NORM3, E_NORM4]


def column_bank(a):
    return 4 if a.i is None and a.base == 6 else 6


class Place:

    def __init__(self, base, i=None, per=0):
        self.base, self.i, self.per = base, i, per

    def plus(self, n):
        return Place(self.base + n, self.i, self.per)

    def value(self, mul=1, plus=0):
        v = self.base * mul + plus
        return v if self.i is None else self.i * (self.per * mul) + v

    def turns(self, n, plus=0, mul=1):
        v = (self.base // n + plus) * mul
        return v if self.i is None else self.i * (self.per // n * mul) + v

    def since(self, n):
        return self.i is not None or self.base >= n

    @property
    def slot(self):
        return self.base % 2


class Chain:

    def __init__(self, eng, sem):
        self.eng, self.sem, self.n = eng, sem, 0

    def did(self, ins):
        ins.then_inc(self.sem, 1)
        self.n += 1

    def settle(self):
        self.eng.wait_ge(self.sem, self.n)


N_IN, N_FF1, N_CTX, N_MIX_IN, N_A, N_F, N_H, N_FF2, N_LAST = range(9)
QUARTERS = [0, 4, 8, 12, 16, 18, 19, 20, 24]
PARTS = [(0, 3), (0, 3), (0,), (0, 2, 3), (0,), (2,), (3,), (0, 3), (0, 2, 3)]
PARTS_BEFORE = [sum(len(p) for p in PARTS[:n]) for n in range(9)]
SUM_BANK = [4, 4, 4, 7, 0, 2, 4, 4, 4]


def ff1_place(j):
    return (Place(C_FF1_STEPS + STEP1 * j.base, j.i, STEP1 * j.per), Place(Q_FF1 + 1 + 5 * j.base, j.i, 5 * j.per),
            Place(ADA_GATE + j.base, j.i, j.per))


def ff2_place(j):
    return (Place(C_FF2_STEPS + STEP2 * j.base, j.i, STEP2 * j.per), Place(Q_FF2 + 2 + 6 * j.base, j.i, 6 * j.per))


def build_program(nc, d, out):
    f32, f32r = mybir.dt.float32, mybir.dt.float32r
    ALU = mybir.AluOpType
    ACT = mybir.ActivationFunctionType
    AX = mybir.AxisListType
    base = 16512

    with ExitStack() as ctx:
        def at(name, shape, offset, dt=f32):
            return nc.alloc_sbuf_tensor_at(name, shape, dt, offset=base + offset)

        def sem(name):
            return ctx.enter_context(nc.semaphore(name))

        K = 1024
        RAW = at("RAW", [P, SLOTS, FT, NB], 0)
        WH = at("WH", [P, 2, FT, NB], 32 * K, f32r)
        WL = at("WL", [P, 2, FT, NB], 48 * K, f32r)
        X = at("X", [P, KC, T], 64 * K)
        XH = at("XH", [P, KC, T], 80 * K, f32r)
        XL = at("XL", [P, KC, T], 96 * K, f32r)
        HH = at("HH", [P, 2, FT, T], 112 * K, f32r)
        HL = at("HL", [P, 2, FT, T], 120 * K, f32r)
        NT = at("NT", [P, KC, T], 112 * K)
        CON = 128 * K
        cols = at("cols", [P, NCOLS], CON)
        small = CON + 2176
        mats = at("mats", [P, 4, P], small)
        mod = at("mod", [P, N_MOD * KC, 2], small + 2048)
        rt = at("rt", [P, 2 * T], small + 2816)
        brow = at("brow", [64, 64], small + 5120)
        ctmp = at("ctmp", [P, 2, KC], small + 5120)
        csig = at("csig", [P, 2, KC], small + 5248)
        gmod = at("gmod", [P, KC], small + 5376)
        lnst = at("lnst", [P, 16], small + 5440)
        cw = at("cw", [P, 4 * FT], small + 5504)
        smx = at("smx", [P, 2, 4], small + 5568)
        epsc = at("epsc", [P, 1], small + 5632)
        AR = small + 5664
        assert 4 * NCOLS <= 2176
        ones, ident, lower, past = (mats[:, n, :] for n in range(4))

        def col(name, n=0, w=1):
            s = COLS[name][0] + n
            return cols[:, s:s + w]

        qT = at("qT", [P, HEADS, T], AR)
        kT = at("kT", [P, HEADS, T], AR + 8 * K)
        v1 = at("v1", [P, TT, 1024], AR + 16 * K)
        uT = at("uT", [P, 8, T], AR + 24 * K)
        vg = at("vg", [P, TT, 1024], AR + 32 * K)
        ga = at("ga", [P, KC, T], AR + 40 * K)
        gb = at("gb", [P, KC, T], AR + 56 * K)
        lng = at("lng", [P, 1024], AR + 40 * K)
        lnb = at("lnb", [P, 1024], AR + 44 * K)
        bsp = at("bsp", [P, 8, P], AR + 48 * K)
        wsp = at("wsp", [P, 8, P], AR + 52 * K)
        t1 = 112 * K
        sgt = at("sgt", [P, 2, 2, T], t1 + 8 * K)
        qk_sq = at("qk_sq", [P, FT, T], t1)
        zs, zneg, lk, lsg, aw = (at(n, [P, 384], t1 + 1536 * k)
                                 for k, n in enumerate(("zs", "zneg", "lk", "lsg", "aw")))
        ada1b = [at("ada1b0", [P, 2, 2, NB], AR + 64 * K),
                 at("ada1b1", [P, 2, 2, NB], AR + 32 * K)]
        ada1c = at("ada1c", [P, 2, NB], t1 + 12 * K)
        MH = at("MH", [P, KC, T], AR, f32r)
        ML = at("ML", [P, KC, T], AR + 16 * K, f32r)
        FR = at("FR", [P, FT, T], AR + 32 * K)
        FQ = at("FQ", [P, FT, T], AR + 36 * K)
        GS = at("GS", [P, FT, T], AR + 40 * K)
        CV = at("CV", [P, FT, T], AR + 44 * K)
        SQ = at("SQ", [P, KC, T], AR)
        adab = at("adab", [P, 2, 2, NB], AR + 16 * K)
        adac = at("adac", [P, 2, 2, NB], AR + 24 * K)
        CX = at("CX", [P, KC, T], AR)
        CSQ = at("CSQ", [P, KC, T], AR + 56 * K)
        q2 = at("q2", [P, HEADS, T], AR)
        k2 = at("k2", [P, HEADS, T], AR + 8 * K)
        v2 = at("v2", [P, TT, 1024], AR + 16 * K)
        kc2 = at("kc2", [P, HEADS, T], AR + 24 * K)
        vc2 = at("vc2", [P, TT, 1024], AR + 32 * K)
        CH = at("CH", [P, KC, T], AR + 40 * K, f32r)
        CL = at("CL", [P, KC, T], AR + 56 * K, f32r)
        bia = at("bia", [P, TT, HEADS * ROWS, GRID_W], AR + 40 * K)
        bsel = at("bsel", [64, 2, 16, P], AR + 56 * K)
        hyC = at("hyC", [P, 12, T], AR + 56 * K)
        fX = at("fX", [P, TT, 512], AR + 68 * K)
        fY = at("fY", [P, FNG, T], AR + 68 * K)
        S2 = at("S2", [P, 2, 2 * T], t1)
        P2 = at("P2", [P, 2, 2 * T], t1 + 4 * K)
        PT = at("PT", [P, 2, 4, T], t1 + 8 * K)
        SM = at("SM", [P, KC, T], AR + 8 * K)
        fcl = at("fcl", [P, TT, 2 * T], 80 * K)
        fcd = at("fcd", [P, 2, P], 84 * K)
        fU = at("fU", [P, FNG, 2 * T], 88 * K)
        KS = at("KS", [P, 2, 5, HW], AR + 24 * K)
        zt = at("zt", [P, TT, HW], AR + 44 * K)
        YS = at("YS", [P, 4, HW], AR + 48 * K)
        hSD = at("hSD", [P, 2, 2, TT, HW], 80 * K)
        dec = at("dec", [P, 2, TT, HW], 96 * K)
        Ef = at("Ef", [P, TT, 6 * P], 104 * K)
        pz = at("pz", [33, T], 110 * K)
        w1h = at("w1h", [33, 64], 111 * K)
        w2h = at("w2h", [64, 64], 111 * K + 512)
        w3h = at("w3h", [64, 2048], t1)
        hdn = at("hdn", [64, 2, T], AR + 52 * K)
        sr = at("sr", [64, 2, T], AR + 54 * K)
        hfb = at("hfb", [P, 2, HW], AR + 48 * K)
        pp = at("pp", [P, 2, 2, HW], t1)
        zT2 = at("zT2", [P, HT, T], t1 + 8 * K)
        Gi = at("Gi", [P, 4, T], t1 + 12 * K)

        PS = ctx.enter_context(nc.psum_tensor("PS", [P, 8, 512], f32))

        def acc_ws(s):
            return PS[:, 2 * s:2 * s + 2, :].rearrange("p b (h t) -> p (b h) t", t=T)

        def acc_as(s):
            return PS[:, 2 * s:2 * s + 2, :]

        def bank(n):
            return PS[:, n, :]

        def ctx_as(n):
            return PS[:, 4 + 2 * (n % 2):6 + 2 * (n % 2), :]

        def ctx_ws(n):
            return ctx_as(n).rearrange("p b (h t) -> p (b h) t", t=T)

        def chunks(w):
            return w.rearrange("(s k p) n -> s p k n", p=P, k=FT)

        w_in, w_out, w_ff1, w_ff2 = map(chunks, (d["w_in"], d["w_out"], d["w_ff1"], d["w_ff2"]))
        w_oa, w_ob, ada_w = map(chunks, (d["w_oa"], d["w_ob"], d["ada_w"]))
        w_in2, w_out2, w_up, w_down = map(chunks, (d["w_in_2"], d["w_out_2"], d["w_up"], d["w_down"]))

        raw_in = [sem(f"raw_in{s}") for s in range(SLOTS)]
        hi_done = sem("hi_done")
        lo_done = sem("lo_done")
        pe_half = sem("pe_half")
        acc_free = [sem("acc_free0"), sem("acc_free1")]
        x_hi = sem("x_hi")
        x_lo = sem("x_lo")
        first_h = sem("first_h")
        first_hi = sem("first_hi")
        first_lo = sem("first_lo")
        x_in = [sem(f"x_in{n}") for n in range(4)]
        bsel_in = [sem("bsel_in0"), sem("bsel_in1")]
        ada1_in = [sem("ada1_in0"), sem("ada1_in1")]
        ada1_acc = sem("ada1_acc")
        ada_in = [sem("ada_in0"), sem("ada_in1")]
        ada_acc = sem("ada_acc")
        ada_sum = sem("ada_sum")
        act_own = sem("act_own")
        dve_own = sem("dve_own")
        names = (
            "cols_in mats_in eps_set ln_in cx_in brow_in four_in e_in mlp_in mlp3_in gi_in outs norm_sq norm_sum "
            "norm_rt norm_h ctx_sq qk_sqd qk_sum qk_rt q_done z_done zs_done zneg_done l_done lk_done cum_done "
            "la_done a_done am_done pv_done o_done ln_var ln_root mix_done sgu_ps s_done b_free merged csig_done "
            "csil_done mt_done mod_done relu_sq hid_hi hid_lo ctx_free bias_ps bias_done sc_done sm_done exp_done "
            "pn_done tp_done pt_done pv2_done a2_done fu_ps fu_done fy_ps fy_done mlp_ps mlp_arg mlp_sin hf_ps "
            "hf_done ks_ps ks_done zt_ps zt_done zf_ps ys_done yi_ps hz_done mix_sq cw_done conv_a conv_b "
            "conv_done gelu_done").split()
        sm = {n: sem(n) for n in names}
        HF = FT // 2

        block = ctx.enter_context(nc.Block())

        @block.sync
        def _(sp):
            def load(c, src):
                if c.since(SLOTS):
                    sp.wait_ge(hi_done, c.value(2, -6))
                    sp.wait_ge(lo_done, c.value(2, -6))
                sp.dma_start(RAW[:, c.base % SLOTS], src).then_inc(raw_in[c.base % SLOTS], 16)

            def cut(view, s, n0):
                return view[s][:, :, n0:n0 + NB] if isinstance(n0, int) else view[s][:, :, bass.ds(n0, NB)]

            def down(c, view, j):
                for s in range(SLOTS):
                    load(c.plus(s), view[j.value()][:, :, s * NB:(s + 1) * NB])

            def wide(c, view, n0):
                for s in range(SLOTS):
                    load(c.plus(s), cut(view, s, n0))

            xq = d["x"].rearrange("(n k p) t -> n p k t", p=P, k=FT)
            for n in range(4):
                sp.dma_start(X[:, 4 * n:4 * n + 4, :], xq[n]).then_inc(x_in[n], 16)
            sp.dma_start(mats[:, :, :], d["mats"]).then_inc(sm["mats_in"], 16)
            sp.dma_start(cols[:, :], d["cols"]).then_inc(sm["cols_in"], 16)

            def load_piece1(c):
                a, n = divmod(c - T_ADA, S_ADA)
                if 0 <= a < ADA_GATE and n in ADA_AT:
                    n = ADA_AT.index(n)
                    order = 8 * a + n
                    if order >= 2:
                        sp.wait_ge(ada1_acc, 4 * order - 4)
                    if a == 5:
                        sp.wait_ge(sm["s_done"], 4)
                    sp.dma_start(ada1b[a // 5][:, order % 2],
                                 cut(ada_w, n // 2, a * NB)[:, 2 * (n % 2):2 * (n % 2) + 2, :])\
                        .then_inc(ada1_in[order % 2], 16)

            for c in range(C_FF1):
                g, s = divmod(c, SLOTS)
                if c < C_GATE:
                    src = cut(w_in, s, IN1_COLS[g])
                elif c < C_OAB:
                    src = cut(w_in, s, GATE_COL + (g - 10) * NB)
                elif c < C_OUT1:
                    src = cut(w_oa if s < 2 else w_ob, s % 2, (g - C_OAB // SLOTS) * NB)
                else:
                    src = cut(w_out, s, (g - C_OUT1 // SLOTS) * NB)
                load(Place(c), src)
                if c == 7:
                    for dst, name in ((lng[:, :], "ln_g"), (lnb[:, :], "ln_b"),
                                      (bsp[:, :, :], "b_sp"), (wsp[:, :, :], "w_sp")):
                        sp.dma_start(dst, d[name]).then_inc(sm["ln_in"], 16)
                load_piece1(c - 2)

            def load_piece(a, n, order):
                if order.since(2):
                    sp.wait_ge(ada_acc, order.value(2, -2))
                sp.dma_start(adab[:, order.base % 2], cut(ada_w, n // 2, a.value(NB))[:, 2 * (n % 2):2 * (n % 2) + 2, :])\
                    .then_inc(ada_in[order.base % 2], 16)

            def ff1_step(j, first=False):
                c, _, a = ff1_place(j)
                order = Place(8 * j.base, j.i, 8 * j.per)
                for s in range(STEP1):
                    if s < SLOTS:
                        load(c.plus(s), cut(w_ff1, s, j.value(NB, NB)))
                    else:
                        load(c.plus(s), w_ff2[j.value()][:, :, (s - 4) * NB:(s - 3) * NB])
                    if s >= 2:
                        load_piece(a, s - 2, order.plus(s - 2))
                    elif not first:
                        load_piece(a.plus(-1), s + 6, order.plus(s - 2))

            wide(Place(C_FF1), w_ff1, 0)
            sp.wait_ge(pe_half, 2 * C_FF1)
            sp.dma_start(CX[:, :, :], d["ctx"].rearrange("(k p) t -> p k t", p=P)).then_inc(sm["cx_in"], 16)
            ff1_step(Place(0), True)
            ff1_step(Place(1))
            with sp.Fori(0, FF1_ITERS) as i:
                ff1_step(Place(2, i, 2))
                ff1_step(Place(3, i, 2))
            for s in range(3 * SLOTS):
                g, r = divmod(s, SLOTS)
                load(Place(C_FF1_TAIL + s), cut(w_ff1, r, (STEPS1 - 1) * NB) if g == 0 else
                     w_ff2[STEPS1 - 3 + g][:, :, r * NB:(r + 1) * NB])
                if s < 2:
                    load_piece(Place(ADA_GROUPS - 3), s + 6, Place(8 * (STEPS1 - 2) + s - 2))
                for n in range(16):
                    if ADA_TAIL[n] == s - 1:
                        load_piece(Place(ADA_GROUPS - 2 + n // 8), n % 8, Place(8 * (STEPS1 - 2) + n))
            for n, n0 in enumerate(IN2_COLS):
                wide(Place(C_IN2 + 4 * n), w_in2, n0)
            wide(Place(C_OUT2), w_out2, 0)
            sp.wait_ge(pe_half, 2 * C_OUT2)
            sp.dma_start(pz[:, :], d["pz"]).then_inc(sm["mlp_in"], 16)
            sp.dma_start(w1h[:, :], d["hy_w1"]).then_inc(sm["mlp_in"], 16)
            sp.dma_start(w2h[:, :], d["hy_w2"]).then_inc(sm["mlp_in"], 16)
            sp.dma_start(fcl[:, :, :], d["fcl"]).then_inc(sm["four_in"], 16)
            sp.dma_start(fcd[:, :, :], d["fcd"]).then_inc(sm["four_in"], 16)
            sp.dma_start(dec[:, :, :, :], d["dec"]).then_inc(sm["e_in"], 16)
            sp.dma_start(Ef[:, :, :], d["ef"]).then_inc(sm["e_in"], 16)
            sp.wait_ge(sm["tp_done"], 2 * HEADS)
            sp.dma_start(w3h[:, :], d["hy_w3"]).then_inc(sm["mlp3_in"], 16)
            sp.wait_ge(sm["pv2_done"], HEADS)
            sp.dma_start(Gi[:, :, :], d["gi"]).then_inc(sm["gi_in"], 16)
            for g in range(1, 4):
                wide(Place(C_OUT2 + 4 * g), w_out2, g * NB)

            def ff2_step(j):
                c, _ = ff2_place(j)
                wide(c, w_up, j.value(NB, NB))
                wide(c.plus(SLOTS), w_up, j.value(NB, D_FF2 + NB))
                down(c.plus(2 * SLOTS), w_down, j)

            wide(Place(C_FF2), w_up, 0)
            wide(Place(C_FF2 + SLOTS), w_up, D_FF2)
            ff2_step(Place(0))
            ff2_step(Place(1))
            with sp.Fori(0, FF2_ITERS) as i:
                ff2_step(Place(2, i, 2))
                ff2_step(Place(3, i, 2))
            down(Place(C_END - SLOTS), w_down, Place(STEPS2 - 1))
            for n in range(4):
                sp.wait_ge(sm["norm_h"], QUARTERS[N_LAST] + n + 1)
                sp.dma_start(out.rearrange("(k p) t -> p k t", p=P)[:, 4 * n:4 * n + 4, :],
                             NT[:, 4 * n:4 * n + 4, :]).then_inc(sm["outs"], 16)
            sp.wait_ge(sm["outs"], 64)

        @block.scalar
        def _(act):
            own = Chain(act, act_own)
            A = nc.scalar.activation

            def high_half(c, h):
                if h == 0:
                    act.wait_ge(raw_in[c.base % SLOTS], c.turns(SLOTS, 1, 16))
                if c.since(2):
                    act.wait_ge(pe_half, c.value(2, h - 3))
                hs = slice(HF * h, HF * h + HF)
                A(WH[:, c.base % 2, hs], RAW[:, c.base % SLOTS, hs], ACT.Copy).then_inc(hi_done, 1)

            def high(c):
                high_half(c, 0)
                high_half(c, 1)

            def done(c):
                act.wait_ge(pe_half, c.value(2, 2))

            def evac(c, q, dst, fn, ws=True, scale=1.0):
                done(c)
                A(dst, acc_ws(q.slot) if ws else acc_as(q.slot), fn, scale=scale).then_inc(acc_free[q.slot], 1)

            def root(n, total):
                act.wait_ge(sm["norm_sum"], n + 1)
                if n:
                    act.wait_ge(sm["norm_h"], QUARTERS[n])
                own.did(A(rt[:, 0:T], bank(SUM_BANK[n])[:, 0:T], ACT.Ln, bias=epsc[:, 0:1], scale=1.0 / total))
                own.settle()
                A(rt[:, 0:T], rt[:, 0:T], ACT.Exp, scale=-0.5).then_inc(sm["norm_rt"], 1)

            def split_high(dst, src, n):
                A(dst[:, 4 * n:4 * n + 4, :], src, ACT.Copy).then_inc(x_hi, 1)

            def shifted_high(dst, src, shift, norm, n):
                act.wait_ge(sm["norm_h"], QUARTERS[norm] + n + 1)
                for k in range(4 * n, 4 * n + 4):
                    ins = A(dst[:, k, :], src[:, k, :], ACT.Identity, bias=shift(k))
                ins.then_inc(x_hi, 1)

            def norm_window(norm, e, c, shift=None):
                def first_high():
                    for h in range(2):
                        if h == 0:
                            act.wait_ge(first_h, WINDOWS.index(e) + 1)
                        else:
                            act.wait_ge(sm["norm_h"], QUARTERS[norm] + 1)
                        if shift is None:
                            ins = A(XH[:, 2 * h:2 * h + 2, :], NT[:, 2 * h:2 * h + 2, :], ACT.Copy)
                        else:
                            for k in (2 * h, 2 * h + 1):
                                ins = A(XH[:, k, :], NT[:, k, :], ACT.Identity, bias=shift(k))
                        ins.then_inc(x_hi if h else first_hi, 1)

                def quarter_high(n):
                    if shift is None:
                        act.wait_ge(sm["norm_h"], QUARTERS[norm] + n + 1)
                        split_high(XH, NT[:, 4 * n:4 * n + 4, :], n)
                    else:
                        shifted_high(XH, NT, shift, norm, n)

                high(c)
                high(c.plus(1))
                root(norm, D)
                first_high()
                quarter_high(1)
                high(c.plus(2))
                quarter_high(2)
                high(c.plus(3))
                quarter_high(3)

            act.wait_ge(sm["cols_in"], 16)
            A(csig[:, :, :], col("c", 0, 2 * KC).rearrange("p (a k) -> p a k", a=2), ACT.Sigmoid)\
                .then_inc(sm["csig_done"], 1)
            act.wait_ge(sm["eps_set"], 1)
            norm_window(N_IN, E_NORM1, Place(0))

            def project_out(g):
                n = g % 2
                t4 = slice(4 * n, 4 * n + 4)
                c5 = slice(n * NB, (n + 1) * NB)
                c, q = Place(4 * g + 3), Place(g)
                if g < 2:
                    evac(c, q, qT[:, t4, :], ACT.Copy)
                elif g < 4:
                    evac(c, q, kT[:, t4, :], ACT.Copy)
                elif g < 6:
                    evac(c, q, v1[:, :, c5], ACT.Copy, ws=False)
                elif g < 8:
                    evac(c, q, vg[:, :, c5], ACT.Gelu, ws=False)
                else:
                    evac(c, q, uT[:, t4, :], ACT.Gelu)

            def gate_out(g):
                dst = (ga if g < 4 else gb)[:, 4 * (g % 4):4 * (g % 4) + 4, :]
                evac(Place(C_GATE + 4 * g + 3), Place(Q_GATE + g), dst, ACT.Sigmoid)

            def attention_step(h, t):
                if t == 1:
                    act.wait_ge(sm["z_done"], h + 1)
                    A(zs[:, :], bank(4)[:, 0:384], ACT.Copy, scale=SCALE).then_inc(sm["zs_done"], 1)
                    act.wait_ge(sm["zneg_done"], h + 1)
                    own.did(A(zneg[:, :], zneg[:, :], ACT.Exp))
                    own.settle()
                    A(zneg[:, :], zneg[:, :], ACT.Ln, bias=1.0).then_inc(sm["l_done"], 1)
                if t == 3:
                    act.wait_ge(sm["la_done"], h + 1)
                    A(aw[:, :], lsg[:, :], ACT.Exp).then_inc(sm["a_done"], 1)
                if t == 5:
                    act.wait_ge(sm["pv_done"], h + 1)
                    A(qT[:, h, :], bank(5)[:, 0:T], ACT.Copy).then_inc(sm["o_done"], 1)

            def branch_high(n):
                done(Place(C_OAB - 4 + n))
                if n == 0:
                    act.wait_ge(sm["o_done"], HEADS)
                    act.wait_ge(sm["s_done"], 4)
                split_high(XH, (qT if n < 2 else uT)[:, 4 * (n % 2):4 * (n % 2) + 4, :], n)

            for c in range(4, C_OAB):
                high(Place(c))
                if c % 4 == 1 and c < C_GATE + 2:
                    project_out((c - 5) // 4)
                if c in (T_LN + 1, T_LN + 5):
                    t = (c - T_LN - 1) // 4
                    act.wait_ge(sm["ln_var"], t + 1)
                    A(lnst[:, 14 + t:15 + t], lnst[:, 12 + t:13 + t], ACT.Sqrt, bias=epsc[:, 0:1])\
                        .then_inc(sm["ln_root"], 1)
                if T_QK + 2 <= c < T_QK + 18 and (c - T_QK) % 4 in (2, 3):
                    n = 2 * ((c - T_QK - 2) // 4) + (c - T_QK) % 4 - 2
                    act.wait_ge(sm["qk_sum"], n + 1)
                    act.wait_ge(sm["q_done"], n)
                    if n == 0:
                        act.wait_ge(sm["norm_h"], 4)
                    own.did(A(rt[:, :], bank(4 + n % 2), ACT.Ln, bias=epsc[:, 0:1], scale=1.0 / DH))
                    own.settle()
                    A(rt[:, :], rt[:, :], ACT.Exp, scale=-0.5).then_inc(sm["qk_rt"], 1)
                for h in range(HEADS):
                    attention_step(h, c - T_ATT - S_ATT * h)
                if c >= C_GATE + 5 and c % 4 == 1:
                    gate_out((c - C_GATE - 5) // 4)
                if c == C_OAB - 1:
                    branch_high(0)
            for c in range(C_OAB, C_OUT1):
                t = c - C_OAB
                high(Place(c))
                if t < 3:
                    branch_high(t + 1)
                if t == 1:
                    gate_out(7)
                if t >= 6 and t % 4 == 2:
                    n = (t - 6) // 4
                    act.wait_ge(sm["merged"], n + 1)
                    split_high(MH, ga[:, 4 * n:4 * n + 4, :], n)
            for c in range(C_OUT1, C_FF1):
                high(Place(c))
                if c == C_OUT1 + 2:
                    act.wait_ge(sm["merged"], 4)
                    split_high(MH, ga[:, 12:16, :], 3)
            norm_window(N_FF1, E_NORM2, Place(C_FF1))

            def relu(c, q, j):
                done(c)
                if j.since(1):
                    act.wait_ge(sm["relu_sq"], j.value())
                A(FR[:, :, :], acc_ws(q.slot), ACT.Relu).then_inc(acc_free[q.slot], 1)

            def hidden_high(j):
                act.wait_ge(sm["relu_sq"], j.value(1, 1))
                if j.since(1):
                    act.wait_ge(sm["hid_lo"], j.value())
                A(HH[:, j.base % 2], FQ[:, :, :], ACT.Copy).then_inc(sm["hid_hi"], 1)

            def context_norm(step, s):
                if step == 0 and 1 <= s < 5:
                    n = s - 1
                    if n == 0:
                        act.wait_ge(sm["cx_in"], 16)
                    A(CSQ[:, 4 * n:4 * n + 4, :], CX[:, 4 * n:4 * n + 4, :], ACT.Square).then_inc(sm["ctx_sq"], 1)
                if step == 1 and s == 0:
                    root(N_CTX, D)
                if step == 1 and s in (2, 3, 5, 6):
                    shifted_high(CH, CX, lambda k: mod[:, k, 1:2], N_CTX, (2, 3, 5, 6).index(s))

            def ff1_step(j, beside=None):
                c, q, _ = ff1_place(j)
                for s in range(STEP1):
                    high(c.plus(s))
                    if beside == 0 and s == 1:
                        relu(c.plus(-1), Place(Q_FF1), Place(0))
                    if beside == 0 and s == 2:
                        hidden_high(Place(0))
                    if s == 5:
                        relu(c.plus(3), q, j.plus(1))
                    if s == 6:
                        hidden_high(j.plus(1))
                    if beside is not None:
                        context_norm(beside, s)

            ff1_step(Place(0), 0)
            ff1_step(Place(1), 1)
            with act.Fori(0, FF1_ITERS) as i:
                ff1_step(Place(2, i, 2))
                ff1_step(Place(3, i, 2))
            c = Place(C_FF1_TAIL)
            for s in range(3 * SLOTS):
                high(c.plus(s))
                if s == 5:
                    relu(c.plus(3), Place(Q_FF1_TAIL), Place(STEPS1 - 1))
                if s == 6:
                    hidden_high(Place(STEPS1 - 1))

            norm_window(N_MIX_IN, E_NORM3, Place(C_IN2), lambda k: mod[:, k, 0:1])

            def project2_out(n):
                c, q = Place(C_IN2 + 4 * n + 3), Place(Q_IN2 + n)
                t4 = slice(4 * (n % 2), 4 * (n % 2) + 4)
                c5 = slice((n % 2) * NB, (n % 2 + 1) * NB)
                if n < 2:
                    evac(c, q, k2[:, t4, :], ACT.Copy)
                    A(kc2[:, t4, :], ctx_ws(n), ACT.Copy).then_inc(sm["ctx_free"], 1)
                elif n < 4:
                    evac(c, q, v2[:, :, c5], ACT.Copy, ws=False)
                    A(vc2[:, :, c5], ctx_as(n), ACT.Copy).then_inc(sm["ctx_free"], 1)
                elif n < 6:
                    evac(c, q, q2[:, t4, :], ACT.Copy, scale=SCALE)
                elif n == 6:
                    evac(c, q, fX[:, :, :], ACT.Copy, ws=False)

            def load_selector(part):
                act.dma_start(bsel[:, part % 2], d["bsel"][:, 16 * part:16 * part + 16, :])\
                    .then_inc(bsel_in[part % 2], 16)

            def bias_out(n):
                act.wait_ge(sm["bias_ps"], n + 1)
                A(bia[:, :, :, 8 * n:8 * n + 8], bank(4 + n % 4).rearrange("p (c t h) -> p t h c", t=TT, c=8),
                  ACT.Copy).then_inc(sm["bias_done"], 1)

            def attention2_step(t):
                u = t - T_ATT2 - 2
                if 0 <= u < 2 * HEADS:
                    b = u % 2
                    act.wait_ge(sm["sm_done"], u + 1)
                    if u >= 2:
                        act.wait_ge(sm["tp_done"], u - 1)
                    A(P2[:, b, :], S2[:, b, :], ACT.Exp, bias=smx[:, b, 0:1],
                      accum_out=smx[:, b, 1:2]).then_inc(sm["exp_done"], 1)
                u = t - T_ATT2 - 6
                if 0 <= u < 2 * HEADS and u % 2:
                    h = u // 2
                    act.wait_ge(sm["pv2_done"], h + 1)
                    A(q2[:, h, :], bank(7)[:, 0:T], ACT.Copy).then_inc(sm["a2_done"], 1)

            for t in range(4, 10 * SLOTS):
                high(Place(C_IN2 + t))
                if t % 4 == 1 and t < 33:
                    project2_out((t - 5) // 4)
                if t == T_BIAS:
                    done(Place(C_IN2 + 15))
                    act.dma_start(brow[:, :], d["brow"]).then_inc(sm["brow_in"], 16)
                    load_selector(0)
                    load_selector(1)
                if t == T_BIAS + 4:
                    act.wait_ge(sm["bias_ps"], 2)
                    load_selector(2)
                if t == T_BIAS + 5:
                    act.wait_ge(sm["bias_ps"], 4)
                    load_selector(3)
                if t in (T_BIAS + 4, T_BIAS + 5, T_BIAS + 7, T_BIAS + 8):
                    n = 2 * (T_BIAS + 4, T_BIAS + 5, T_BIAS + 7, T_BIAS + 8).index(t)
                    bias_out(n)
                    bias_out(n + 1)
                attention2_step(t)

            def fourier_tokens(n):
                act.wait_ge(sm["fu_ps"], n + 1)
                A(fU[:, n, :], bank(n % 2), ACT.Copy).then_inc(sm["fu_done"], 1)

            def sine(n):
                act.wait_ge(sm["mlp_arg"], n + 1)
                A(hdn[:, n, :], sr[:, 0, :], ACT.Sin).then_inc(sm["mlp_sin"], 1)

            high(Place(C_OUT2))
            attention2_step(40)
            high(Place(C_OUT2 + 1))
            for t in range(41, 44):
                attention2_step(t)
            fourier_tokens(0)
            attention2_step(44)
            attention2_step(45)
            fourier_tokens(1)
            sine(0)
            fourier_tokens(2)
            fourier_tokens(3)
            sine(1)
            for n in range(FNG):
                act.wait_ge(sm["fy_ps"], n + 1)
                A(fY[:, n, :], bank((2, 6)[n % 2])[:, 0:T], ACT.Copy).then_inc(sm["fy_done"], 1)
            act.wait_ge(sm["a2_done"], HEADS)
            for n in range(2):
                A(SM[:, 4 * n:4 * n + 4, :], q2[:, 4 * n:4 * n + 4, :], ACT.Square).then_inc(sm["mix_sq"], 1)

            def spectrum(n):
                act.wait_ge(sm["ks_ps"], n + 1)
                A(KS[:, n // 5, n % 5, :], bank(n % 2), ACT.Copy).then_inc(sm["ks_done"], 1)

            def to_tokens(o):
                for t in range(TT):
                    act.wait_ge(sm["zt_ps"], TT * o + t + 1)
                    A(zt[:, t, :], bank(2 + t), ACT.Copy).then_inc(sm["zt_done"], 1)

            to_tokens(0)
            for n in range(5):
                spectrum(n)
            for n in range(5, 10):
                spectrum(n)
            root(N_A, 1024)
            to_tokens(1)
            act.wait_ge(sm["ks_ps"], 10)
            for n in range(2):
                act.wait_ge(sm["norm_h"], QUARTERS[N_A] + n + 1)
                split_high(XH, SM[:, 4 * n:4 * n + 4, :], n)
            root(N_F, 512)
            act.wait_ge(sm["norm_h"], QUARTERS[N_F] + 1)
            split_high(XH, SM[:, 8:12, :], 2)
            high(Place(C_OUT2 + 2))
            high(Place(C_OUT2 + 3))
            root(N_H, 512)
            act.wait_ge(sm["norm_h"], QUARTERS[N_H] + 1)
            split_high(XH, SM[:, 12:16, :], 3)
            for c in range(C_OUT2 + 4, C_FF2):
                high(Place(c))
            norm_window(N_FF2, E_NORM4, Place(C_FF2), lambda k: mod[:, 3 * KC + k, 0:1])

            def hidden_gate(c, q, j):
                done(c)
                if j.since(1):
                    act.wait_ge(sm["conv_done"], j.value())
                A(GS[:, :, :], acc_ws(q.slot), ACT.Copy).then_inc(acc_free[q.slot], 1)

            def gate_gelu(j):
                act.wait_ge(sm["conv_done"], j.value(1, 1))
                A(CV[:, :, :], CV[:, :, :], ACT.Gelu_apprx_tanh).then_inc(sm["gelu_done"], 1)

            def hidden_high2(q, j):
                act.wait_ge(acc_free[q.slot], q.turns(2, 1))
                A(HH[:, j.base % 2], FQ[:, :, :], ACT.Copy).then_inc(sm["hid_hi"], 1)

            def ff2_step(j, first=False):
                c, q = ff2_place(j)
                for s in range(STEP2):
                    high(c.plus(s))
                    if first and s == 0:
                        gate_gelu(Place(0))
                    if first and s == 2:
                        hidden_high2(q.plus(-1), Place(0))
                    if s == 5:
                        hidden_gate(c.plus(3), q, j.plus(1))
                    if s == 8:
                        gate_gelu(j.plus(1))
                    if s == 10:
                        hidden_high2(q.plus(1), j.plus(1))

            for s in range(4, 8):
                high(Place(C_FF2 + s))
                if s == 5:
                    hidden_gate(Place(C_FF2 + 3), Place(Q_FF2), Place(0))
            ff2_step(Place(0), first=True)
            ff2_step(Place(1))
            with act.Fori(0, FF2_ITERS) as i:
                ff2_step(Place(2, i, 2))
                ff2_step(Place(3, i, 2))
            for s in range(4):
                high(Place(C_END - 4 + s))
            root(N_LAST, D)

        @block.vector
        def _(dve):
            own = Chain(dve, dve_own)
            V = nc.vector
            stt, tt, ts = V.scalar_tensor_tensor, V.tensor_tensor, V.tensor_scalar

            def low_half(c, h):
                dve.wait_ge(hi_done, c.value(2, h + 1))
                if c.since(2):
                    dve.wait_ge(pe_half, c.value(2, h - 3))
                hs = slice(HF * h, HF * h + HF)
                b = c.base % 2
                tt(WL[:, b, hs], RAW[:, c.base % SLOTS, hs], WH[:, b, hs].bitcast(f32), ALU.subtract)\
                    .then_inc(lo_done, 1)

            def low(c):
                low_half(c, 0)
                low_half(c, 1)

            def done(c):
                dve.wait_ge(pe_half, c.value(2, 2))

            def settled(ins):
                own.did(ins)
                own.settle()

            def quarter(x, n):
                return x[:, 4 * n:4 * n + 4, :]

            def squares(dst, src, n, part):
                ins = tt(quarter(dst, n), quarter(src, n), quarter(src, n), ALU.mult)
                if part:
                    ins.then_inc(sm["norm_sq"], 1)
                else:
                    settled(ins)

            def add_squares(dst, n, part):
                ins = tt(quarter(dst, 0), quarter(dst, 0), quarter(dst, n), ALU.add)
                if part:
                    ins.then_inc(sm["norm_sq"], 1)
                else:
                    settled(ins)

            def inverse_root(n):
                dve.wait_ge(sm["norm_rt"], n + 1)

            def scaled(dst, src, gain, n):
                for k in range(4):
                    ins = stt(dst[:, 4 * n + k, :], src[:, k, :], gain(4 * n + k), rt[:, 0:T],
                              ALU.mult, ALU.mult)
                ins.then_inc(sm["norm_h"], 1)

            def split_low(e, hi, lo, src, n):
                dve.wait_ge(x_hi, 4 * e + n + 1)
                tt(quarter(lo, n), src, quarter(hi, n).bitcast(f32), ALU.subtract).then_inc(x_lo, 1)

            def shifted_low(e, hi, lo, src, shift, n):
                dve.wait_ge(x_hi, 4 * e + n + 1)
                for k in range(4 * n, 4 * n + 4):
                    ins = stt(lo[:, k, :], src[:, k, :], shift(k), hi[:, k, :].bitcast(f32), ALU.add, ALU.subtract)
                ins.then_inc(x_lo, 1)

            def norm_window(norm, e, c, gain, finish, shift=None):
                def quarter_low(n):
                    if shift is None:
                        split_low(e, XH, XL, quarter(NT, n), n)
                    else:
                        shifted_low(e, XH, XL, NT, shift, n)

                def first_low(h):
                    if h == 0:
                        dve.wait_ge(first_hi, WINDOWS.index(e) + 1)
                    else:
                        dve.wait_ge(x_hi, 4 * e + 1)
                    t = slice(2 * h, 2 * h + 2)
                    if shift is None:
                        ins = tt(XL[:, t, :], NT[:, t, :], XH[:, t, :].bitcast(f32), ALU.subtract)
                    else:
                        for k in (2 * h, 2 * h + 1):
                            ins = stt(XL[:, k, :], NT[:, k, :], shift(k), XH[:, k, :].bitcast(f32),
                                      ALU.add, ALU.subtract)
                    ins.then_inc(x_lo if h else first_lo, 1)

                low(c)
                low_half(c.plus(1), 0)
                finish()
                low_half(c.plus(1), 1)
                inverse_root(norm)
                for k in range(4):
                    ins = stt(NT[:, k, :], X[:, k, :], gain(k), rt[:, 0:T], ALU.mult, ALU.mult)
                    if k % 2:
                        ins.then_inc(sm["norm_h"] if k == 3 else first_h, 1)
                first_low(0)
                first_low(1)
                scaled(NT, quarter(X, 1), gain, 1)
                scaled(NT, quarter(X, 2), gain, 2)
                quarter_low(1)
                low(c.plus(2))
                scaled(NT, quarter(X, 3), gain, 3)
                quarter_low(2)
                low(c.plus(3))
                quarter_low(3)

            V.memset(epsc[:, :], EPS).then_inc(sm["eps_set"], 1)
            for n in range(4):
                dve.wait_ge(x_in[n], 16)
                squares(NT, X, n, n == 3)
                if n in (1, 2):
                    add_squares(NT, n, n == 2)
            dve.wait_ge(sm["csig_done"], 1)
            tt(ctmp[:, :, :], col("c", 0, 2 * KC).rearrange("p (a k) -> p a k", a=2), csig[:, :, :], ALU.mult)\
                .then_inc(sm["csil_done"], 1)
            norm_window(N_IN, E_NORM1, Place(0), lambda k: col("g_mix", k), lambda: None)

            def layer_norm(t, step):
                if step == 0:
                    dve.wait_ge(acc_free[0], 4)
                    dve.wait_ge(acc_free[1], 4)
                    for n in range(2):
                        own.did(V.bn_stats(lnst[:, 6 * n:6 * n + 6], vg[:, t, n * 512:(n + 1) * 512]))
                    own.settle()
                    settled(V.bn_aggr(smx[:, t, 0:2], lnst[:, 0:12]))
                    V.tensor_copy(lnst[:, 12 + t:13 + t], smx[:, t, 1:2]).then_inc(sm["ln_var"], 1)
                if step == 2:
                    dve.wait_ge(sm["ln_root"], t + 1)
                    settled(V.reciprocal(smx[:, t, 2:3], lnst[:, 14 + t:15 + t]))
                    settled(ts(vg[:, t, :], vg[:, t, :], smx[:, t, 0:1], smx[:, t, 2:3], ALU.subtract, ALU.mult))
                if step == 3:
                    dve.wait_ge(sm["ln_in"], 64)
                    settled(tt(vg[:, t, :], vg[:, t, :], lng[:, :], ALU.mult))
                if step == 4:
                    tt(vg[:, t, :], vg[:, t, :], lnb[:, :], ALU.add).then_inc(sm["mix_done"], 1)

            def spatial_gating(n):
                dve.wait_ge(sm["sgu_ps"], n + 1)
                dve.wait_ge(acc_free[0], 5)
                dve.wait_ge(acc_free[1], 5)
                if n >= 2:
                    dve.wait_ge(sm["s_done"], n - 1)
                for g in range(2):
                    for c in range(TT):
                        own.did(tt(sgt[:, n % 2, g, c * P:(c + 1) * P],
                                   bank(6 + n % 2)[:, (TT * g + c) * P:(TT * g + c + 1) * P],
                                   bsp[:, 2 * n + g, :], ALU.add))
                own.settle()
                tt(uT[:, 2 * n:2 * n + 2, :], uT[:, 2 * n:2 * n + 2, :], sgt[:, n % 2], ALU.mult)\
                    .then_inc(sm["s_done"], 1)

            def head_norm(n, step):
                src = quarter(qT if n < 2 else kT, n % 2)
                gname = "g_q" if n < 2 else "g_k"
                if step == 0:
                    q = Place(n)
                    dve.wait_ge(acc_free[q.slot], q.turns(2, 1))
                    if n:
                        dve.wait_ge(sm["qk_sum"], 2 * n)
                    tt(qk_sq[:, :, :], src, src, ALU.mult).then_inc(sm["qk_sqd"], 1)
                else:
                    half = step - 2
                    dve.wait_ge(sm["qk_rt"], 2 * n + half + 1)
                    for m in range(2):
                        h = 2 * half + m
                        ins = stt(src[:, h, :], src[:, h, :], col(gname, 4 * (n % 2) + h),
                                  rt[:, m * T:(m + 1) * T], ALU.mult, ALU.mult)
                    ins.then_inc(sm["q_done"], 1)

            def attention_step(h, t):
                if t == 1:
                    dve.wait_ge(sm["zs_done"], h + 1)
                    stt(zneg[:, :], zs[:, :], -1.0, zs[:, :], ALU.mult, ALU.min).then_inc(sm["zneg_done"], 1)
                    dve.wait_ge(sm["l_done"], h + 1)
                    settled(stt(lsg[:, :], zs[:, :], 0.0, zneg[:, :], ALU.min, ALU.subtract))
                    settled(tt(lk[:, :], lsg[:, :], zs[:, :], ALU.subtract))
                    own.did(tt(lk[:, 0:P], lk[:, 0:P], past, ALU.mult))
                    tt(lk[:, T:384], lk[:, T:384], past, ALU.mult).then_inc(sm["lk_done"], 1)
                    dve.wait_ge(sm["lk_done"], h + 1)
                if t == 3:
                    dve.wait_ge(sm["cum_done"], h + 1)
                    tt(lsg[:, :], bank(5)[:, 0:384], lsg[:, :], ALU.add).then_inc(sm["la_done"], 1)
                    dve.wait_ge(sm["a_done"], h + 1)
                    own.did(tt(aw[:, 0:P], aw[:, 0:P], past, ALU.mult))
                    tt(aw[:, T:384], aw[:, T:384], past, ALU.mult).then_inc(sm["am_done"], 1)
                    own.settle()

            def mod_out(a):
                dve.wait_ge(sm["mt_done"], a.value(1, 1))
                n = a.value(FT)
                dst = mod[:, n:n + FT, :] if a.i is None else mod[:, bass.ds(n, FT), :]
                V.tensor_copy(dst, bank(column_bank(a))[:, 0:2 * FT].rearrange("p (f c) -> p f c", c=2))\
                    .then_inc(sm["mod_done"], 1)

            def beside_modulation(c):
                a, n = divmod(c - T_ADA, S_ADA)
                if n == 1 and 1 <= a <= ADA_GATE:
                    mod_out(Place(a - 1))
                if 0 <= a < ADA_GATE and n in ADA_AT:
                    n = ADA_AT.index(n)
                    order = 8 * a + n
                    dve.wait_ge(ada1_in[order % 2], 16 * (order // 2 + 1))
                    if order == 0:
                        dve.wait_ge(sm["csil_done"], 1)
                        dve.wait_ge(x_lo, 4)
                    if n == 0 and a:
                        dve.wait_ge(sm["mt_done"], a)
                    for m in range(4):
                        if order or m >= 2:
                            dve.wait_ge(ada1_acc, 4 * order + m - 1)
                        v = m % 2
                        acc, x = ada1c[:, v, :], ctmp[:, v, 2 * n + m // 2:2 * n + m // 2 + 1]
                        w = ada1b[a // 5][:, order % 2, m // 2, :]
                        ins = ts(acc, w, x, None, ALU.mult) if n == 0 and m < 2 else \
                            stt(acc, w, x, acc, ALU.mult, ALU.add)
                        ins.then_inc(ada1_acc, 1)

            def branch_low(n):
                split_low(E_OAB, XH, XL, quarter(qT if n < 2 else uT, n % 2), n)

            for c in range(4, C_OAB):
                low(Place(c))
                if c == T_LN:
                    dve.wait_ge(sm["ln_in"], 64)
                    V.memset(wsp[CHUNK:P, :, 0:CHUNK], 0.0).then_inc(sm["mix_done"], 1)
                for t in range(TT):
                    if 0 <= c - T_LN - 4 * t < 5:
                        layer_norm(t, c - T_LN - 4 * t)
                if T_SGU < c <= T_SGU + 8 and (c - T_SGU) % 2:
                    spatial_gating((c - T_SGU) // 2)
                if T_QK <= c < T_QK + 16 and (c - T_QK) % 4 != 1:
                    head_norm((c - T_QK) // 4, (c - T_QK) % 4)
                if c == T_ATT:
                    dve.wait_ge(sm["mats_in"], 16)
                for h in range(HEADS):
                    attention_step(h, c - T_ATT - S_ATT * h)
                if c == C_OAB - 1:
                    branch_low(0)
                beside_modulation(c)

            def merge(g):
                q = Place(Q_OAB + g)
                done(Place(C_OAB + 4 * g + 3))
                if g == 0:
                    for n in range(2):
                        dve.wait_ge(acc_free[n], (Q_GATE + 8) // 2)
                tt(quarter(ga, g), acc_ws(q.slot), quarter(ga, g), ALU.mult).then_inc(acc_free[q.slot], 1)
                tt(quarter(gb, g), ctx_ws(g), quarter(gb, g), ALU.mult).then_inc(sm["b_free"], 1)
                dve.wait_ge(acc_free[q.slot], q.turns(2, 1))
                dve.wait_ge(sm["b_free"], g + 1)
                tt(quarter(ga, g), quarter(ga, g), quarter(gb, g), ALU.add).then_inc(sm["merged"], 1)

            for c in range(C_OAB, C_OUT1):
                t = c - C_OAB
                low(Place(c))
                if t < 3:
                    branch_low(t + 1)
                if t >= 5 and t % 4 == 1:
                    merge((t - 5) // 4)
                if t >= 6 and t % 4 == 2:
                    n = (t - 6) // 4
                    split_low(E_OUT1, MH, ML, quarter(ga, n), n)
                beside_modulation(c)

            def residual(g):
                q = Place(Q_OUT1 + g)
                done(Place(C_OUT1 + 4 * g + 3))
                tt(quarter(X, g), acc_ws(q.slot), quarter(X, g), ALU.add).then_inc(acc_free[q.slot], 1)

            def residual_squares(c0, q0, g, residual):
                residual(g)
                q = Place(q0 + g)
                dve.wait_ge(acc_free[q.slot], q.turns(2, 1))
                squares(NT, X, g, g == 3)

            for t in range(4 * SLOTS):
                low(Place(C_OUT1 + t))
                if t == 1:
                    merge(3)
                if t == 2:
                    split_low(E_OUT1, MH, ML, quarter(ga, 3), 3)
                if t in (5, 9, 13):
                    residual_squares(C_OUT1, Q_OUT1, (t - 5) // 4, residual)
                if t in (10, 14):
                    add_squares(NT, (t - 6) // 4, t == 14)
                beside_modulation(C_OUT1 + t)
            norm_window(N_FF1, E_NORM2, Place(C_FF1), lambda k: col("g_ff", k),
                        lambda: residual_squares(C_OUT1, Q_OUT1, 3, residual))

            def relu_squared(q, j):
                dve.wait_ge(acc_free[q.slot], q.turns(2, 1))
                if j.since(1):
                    dve.wait_ge(sm["hid_lo"], j.value())
                tt(FQ[:, :, :], FR[:, :, :], FR[:, :, :], ALU.mult).then_inc(sm["relu_sq"], 1)

            def hidden_low(j, before=0):
                dve.wait_ge(sm["hid_hi"], j.value(1, before + 1))
                tt(HL[:, j.base % 2], FQ[:, :, :], HH[:, j.base % 2].bitcast(f32), ALU.subtract)\
                    .then_inc(sm["hid_lo"], 1)

            def down_out(q, c, s):
                done(c)
                tt(quarter(X, s), acc_ws(q.slot), quarter(X, s), ALU.add).then_inc(acc_free[q.slot], 1)

            def gain_of(a, scale_at, name):
                settled(stt(gmod[:, :], mod[:, scale_at:scale_at + KC, a], 1.0, col(name, 0, KC),
                            ALU.add, ALU.mult))

            def add_ada_bias(n0, n1):
                dve.wait_ge(sm["mod_done"], n1 // FT)
                for a in range(2):
                    own.did(tt(mod[:, n0:n1, a], mod[:, n0:n1, a], col("ada_b", n0, n1 - n0), ALU.add))
                own.settle()

            def context_norm(step, s):
                if step == 0 and s == 2:
                    add_ada_bias(0, 2 * KC)
                    gain_of(1, KC, "norm1")
                if step == 0 and s in (3, 4, 5):
                    dve.wait_ge(sm["ctx_sq"], s - 1)
                    add_squares(CSQ, s - 2, s == 5)
                if step == 1 and s == 0:
                    inverse_root(N_CTX)
                if step == 1 and s in (1, 2, 4, 5):
                    n = (1, 2, 4, 5).index(s)
                    scaled(CX, quarter(CX, n), lambda k: gmod[:, k:k + 1], n)
                if step == 1 and s in (3, 4, 6, 7):
                    shifted_low(E_CTX, CH, CL, CX, lambda k: mod[:, k, 1:2], (3, 4, 6, 7).index(s))

            def add_piece(a, n, order):
                dve.wait_ge(ada_in[order.base % 2], order.turns(2, 1, 16))
                if n == 0:
                    dve.wait_ge(sm["mt_done"], a.value(1, -1))
                for m in range(2):
                    if order.base or m or order.i is not None:
                        dve.wait_ge(ada_acc, order.value(2, m - 1) if order.since(1) else m)
                    acc = adac[:, a.base % 2, m, :]
                    w, x = adab[:, order.base % 2, m, :], ctmp[:, 0, 2 * n + m:2 * n + m + 1]
                    ins = ts(acc, w, x, None, ALU.mult) if n == 0 else stt(acc, w, x, acc, ALU.mult, ALU.add)
                    ins.then_inc(ada_acc, 1)
                if n == 7:
                    dve.wait_ge(ada_acc, order.value(2, 2))
                    acc = adac[:, a.base % 2, :, :]
                    tt(acc[:, 0, :], acc[:, 0, :], acc[:, 1, :], ALU.add).then_inc(ada_sum, 1)

            def ff1_step(j, beside=None):
                c, q, a = ff1_place(j)
                for s in range(STEP1):
                    low(c.plus(s))
                    if s < 2 and beside != 0:
                        down_out(q.plus(s - 2), c.plus(s - 2), s + 2)
                    if beside == 0 and s == 1:
                        relu_squared(Place(Q_FF1), Place(0))
                    if s == 2:
                        hidden_low(j)
                    if s == 5:
                        relu_squared(q, j.plus(1))
                    if s == 5 and beside != 0:
                        mod_out(a.plus(-1))
                    if s >= 6:
                        down_out(q.plus(s - 5), c.plus(s - 2), s - 6)
                    if beside is not None:
                        context_norm(beside, s)
                    add_piece(a, s, Place(8 * j.base + s, j.i, 8 * j.per))

            ff1_step(Place(0), 0)
            ff1_step(Place(1), 1)
            with dve.Fori(0, FF1_ITERS) as i:
                ff1_step(Place(2, i, 2))
                ff1_step(Place(3, i, 2))

            def complete(q, n, part):
                dve.wait_ge(acc_free[q.slot], q.turns(2, 1))
                squares(SQ, X, n, part)

            c, q = Place(C_FF1_TAIL), Place(Q_FF1_TAIL)
            for s in range(3 * SLOTS):
                low(c.plus(s))
                if s < 2:
                    down_out(q.plus(s - 2), c.plus(s - 2), s + 2)
                if s == 2:
                    hidden_low(Place(STEPS1 - 2))
                if s == 4:
                    mod_out(Place(ADA_GROUPS - 3))
                if s == 5:
                    relu_squared(q, Place(STEPS1 - 1))
                if s == 7:
                    hidden_low(Place(STEPS1 - 1))
                if s == 10:
                    mod_out(Place(ADA_GROUPS - 2))
                if s >= 6:
                    down_out(q.plus(s - 5), c.plus(s - 2), (s - 6) % 4)
                if s >= 10:
                    complete(q.plus(s - 5), s - 10, False)
                for n in range(16):
                    if ADA_TAIL[n] == s:
                        add_piece(Place(ADA_GROUPS - 2 + n // 8), n % 8, Place(8 * (STEPS1 - 2) + n))
            add_squares(SQ, 1, True)

            def ff1_finish():
                for n in (2, 3):
                    down_out(q.plus(5 + n), c.plus(8 + n), n)
                    complete(q.plus(5 + n), n, True)

            dve.wait_ge(x_lo, 4 * E_CTX + 4)
            gain_of(0, KC, "norm1")
            norm_window(N_MIX_IN, E_NORM3, Place(C_IN2), lambda k: gmod[:, k:k + 1], ff1_finish,
                        lambda k: mod[:, k, 0:1])

            def attention2_step(t):
                u = t - T_ATT2 - 1
                if 0 <= u < 2 * HEADS:
                    b, h, tile = u % 2, u // 2, u % 2
                    dve.wait_ge(sm["sc_done"], u + 1)
                    if u >= 2:
                        dve.wait_ge(sm["exp_done"], u - 1)
                    if u == 0:
                        dve.wait_ge(sm["bias_done"], 8)
                    own.did(tt(S2[:, b, 0:T].rearrange("p (r c) -> p r c", c=GRID_W),
                               bank(4 + b)[:, 0:T].rearrange("p (r c) -> p r c", c=GRID_W),
                               bia[:, tile, ROWS * h:ROWS * h + ROWS, :], ALU.add))
                    own.did(V.tensor_copy(S2[:, b, T:2 * T], bank(4 + b)[:, T:2 * T]))
                    own.settle()
                    settled(V.reduce_max(smx[:, b, 3:4], S2[:, b, :], AX.X))
                    ts(smx[:, b, 0:1], smx[:, b, 3:4], -1.0, None, ALU.mult).then_inc(sm["sm_done"], 1)
                u = t - T_ATT2 - 2
                if 0 <= u < 2 * HEADS:
                    b = u % 2
                    dve.wait_ge(sm["exp_done"], u + 1)
                    settled(V.reciprocal(smx[:, b, 2:3], smx[:, b, 1:2]))
                    ts(P2[:, b, :], P2[:, b, :], smx[:, b, 2:3], None, ALU.mult).then_inc(sm["pn_done"], 1)
                u = t - T_ATT2 - 4
                if 0 <= u < 2 * HEADS:
                    h, tile = u // 2, u % 2
                    dve.wait_ge(sm["tp_done"], u + 1)
                    if h >= 2:
                        dve.wait_ge(sm["pv2_done"], h - 1)
                    V.tensor_copy(PT[:, h % 2, :, tile * P:(tile + 1) * P],
                                  bank(6).rearrange("p (k q) -> p k q", q=P)).then_inc(sm["pt_done"], 1)

            def short_conv(m, tap):
                q = Place(Q_IN2 + 7 + m)
                src = acc_ws(q.slot)
                done(Place(C_IN2 + 4 * (7 + m) + 3))
                for k in range(4):
                    n = 4 * m + k
                    w = col("hy_w", 12 * (1, 0, 2)[tap] + n)
                    if tap == 0:
                        ins = ts(hyC[:, n, :], src[:, k, :], w, col("hy_b", n), ALU.mult, ALU.add)
                    elif tap == 1:
                        ins = stt(hyC[:, n, 1:T], src[:, k, 0:T - 1], w, hyC[:, n, 1:T], ALU.mult, ALU.add)
                    else:
                        ins = stt(hyC[:, n, 0:T - 1], src[:, k, 1:T], w, hyC[:, n, 0:T - 1], ALU.mult, ALU.add)
                if tap < 2:
                    settled(ins)
                else:
                    ins.then_inc(acc_free[q.slot], 1)

            for t in range(4, 10 * SLOTS):
                low(Place(C_IN2 + t))
                if t == 4:
                    mod_out(Place(ADA_GROUPS - 1))
                    add_ada_bias(2 * KC, N_MOD * KC)
                attention2_step(t)
                if t >= 33 and (t - 33) % 4 < 3:
                    short_conv((t - 33) // 4, (t - 33) % 4)

            C1, C2 = 6.28125, 0.0019340515136718750
            C3 = 2 * math.pi - C1 - C2
            ROUND = 1.5 * 2 ** 23

            def sine_argument(n):
                dve.wait_ge(sm["mlp_ps"], n + 1)
                if n:
                    dve.wait_ge(sm["mlp_sin"], 1)
                else:
                    dve.wait_ge(sm["sm_done"], 2 * HEADS)
                a, r = sr[:, 0, :], sr[:, 1, :]
                settled(ts(a, bank(4)[0:64, 0:T], cols[0:64, COLS["mlp"][0] + n:COLS["mlp"][0] + n + 1],
                           cols[0:64, COLS["mlp"][0] + 2:COLS["mlp"][0] + 3], ALU.add, ALU.mult))
                settled(ts(r, a, 1 / (2 * math.pi), ROUND, ALU.mult, ALU.add))
                settled(ts(r, r, ROUND, None, ALU.subtract))
                for c in (C1, C2, C3):
                    settled(stt(a, r, -c, a, ALU.mult, ALU.add))
                ts(a, a, 3.1415925, -3.1415925, ALU.min, ALU.max).then_inc(sm["mlp_arg"], 1)

            low(Place(C_OUT2))
            attention2_step(40)
            low(Place(C_OUT2 + 1))
            for t in range(41, 44):
                attention2_step(t)
                short_conv(2, t - 41)
            sine_argument(0)
            sine_argument(1)
            dve.wait_ge(sm["e_in"], 32)
            dve.wait_ge(sm["fy_ps"], FNG)
            dve.wait_ge(sm["fu_done"], FNG)
            for n in range(4):
                o, t = n // 2, n % 2
                dve.wait_ge(sm["hf_ps"], n + 1)
                if n:
                    dve.wait_ge(sm["hf_done"], n)
                for f in range(2):
                    own.did(tt(hfb[:, f, :], bank(4 + 2 * (n % 2) + f), dec[:, f, t, :], ALU.mult))
                own.settle()
                own.did(tt(hSD[:, o, 0, t, :], hfb[:, 0, :], hfb[:, 1, :], ALU.add))
                tt(hSD[:, o, 1, t, :], hfb[:, 0, :], hfb[:, 1, :], ALU.subtract).then_inc(sm["hf_done"], 1)
            own.settle()

            def products(o):
                dve.wait_ge(sm["zf_ps"], o + 1)
                dve.wait_ge(sm["ks_done"], 5 * o + 5)
                dve.wait_ge(sm["hf_done"], 4)
                if o:
                    dve.wait_ge(sm["ys_done"], o)
                    dve.wait_ge(sm["hz_done"], o)
                re, im = PS[:, 4:6, :], PS[:, 6:8, :]
                own.did(tt(pp[:, 0], re, KS[:, o, 0:2, :], ALU.mult))
                own.did(tt(pp[:, 1], im, KS[:, o, 2:4, :], ALU.mult))
                own.settle()
                settled(tt(YS[:, 0:2, :], pp[:, 0], pp[:, 1], ALU.subtract))
                own.did(tt(pp[:, 0], re, KS[:, o, 2:4, :], ALU.mult))
                own.did(tt(pp[:, 1, 0, :], bank(6), KS[:, o, 4, :], ALU.mult))
                own.did(tt(pp[:, 1, 1, :], bank(7), KS[:, o, 1, :], ALU.mult))
                own.settle()
                tt(YS[:, 2:4, :], pp[:, 0], pp[:, 1], ALU.add).then_inc(sm["ys_done"], 1)

            def gated_output(o):
                dve.wait_ge(sm["yi_ps"], o + 1)
                dve.wait_ge(sm["ys_done"], o + 1)
                dve.wait_ge(acc_free[1], Q_OUT2 // 2)
                src = hyC[:, 0:HT, :] if o == 0 else zT2
                gate = hyC[:, HT * (o + 1):HT * (o + 2), :]
                dst = zT2 if o == 0 else gate
                tmp = pp[:, 0].rearrange("p a (b t) -> p (a b) t", t=T)
                for k in range(HT):
                    own.did(stt(tmp[:, k, :], src[:, k, :], col("hy_bias", HT * o + k),
                                bank(2 + k // 2)[:, (k % 2) * T:(k % 2 + 1) * T], ALU.mult, ALU.add))
                own.settle()
                tt(dst[:, 0:HT, :], tmp, gate, ALU.mult).then_inc(sm["hz_done"], 1)

            products(0)
            dve.wait_ge(sm["mix_sq"], 2)
            add_squares(SM, 1, True)
            dve.wait_ge(sm["fy_done"], FNG)
            tt(quarter(SM, 2), fY[:, :, :], fY[:, :, :], ALU.mult).then_inc(sm["norm_sq"], 1)
            gated_output(0)
            inverse_root(N_A)
            for n in range(2):
                scaled(SM, quarter(q2, n), lambda k: col("mix", k), n)
            for n in range(2):
                split_low(E_OUT2, XH, XL, quarter(SM, n), n)
            products(1)
            inverse_root(N_F)
            scaled(SM, fY[:, :, :], lambda k: col("mix", k), 2)
            split_low(E_OUT2, XH, XL, quarter(SM, 2), 2)
            gated_output(1)
            dve.wait_ge(sm["hz_done"], 2)
            tt(quarter(SM, 3), quarter(hyC, 2), quarter(hyC, 2), ALU.mult).then_inc(sm["norm_sq"], 1)
            low(Place(C_OUT2 + 2))
            low(Place(C_OUT2 + 3))
            inverse_root(N_H)
            scaled(SM, quarter(hyC, 2), lambda k: col("mix", k), 3)
            split_low(E_OUT2, XH, XL, quarter(SM, 3), 3)

            def residual2(g):
                q = Place(Q_OUT2 + g)
                done(Place(C_OUT2 + 4 * g + 3))
                for k in range(4):
                    ins = stt(X[:, 4 * g + k, :], acc_ws(q.slot)[:, k, :], mod[:, 2 * KC + 4 * g + k, 0:1],
                              X[:, 4 * g + k, :], ALU.mult, ALU.add)
                ins.then_inc(acc_free[q.slot], 1)

            for t in range(4, 4 * SLOTS):
                low(Place(C_OUT2 + t))
                if t == 4:
                    gain_of(0, 4 * KC, "norm2")
                if t in (5, 9, 13):
                    residual_squares(C_OUT2, Q_OUT2, (t - 5) // 4, residual2)
                if t in (10, 14):
                    add_squares(NT, (t - 6) // 4, t == 14)
            norm_window(N_FF2, E_NORM4, Place(C_FF2), lambda k: gmod[:, k:k + 1],
                        lambda: residual_squares(C_OUT2, Q_OUT2, 3, residual2), lambda k: mod[:, 3 * KC + k, 0:1])

            def gate_conv(q, j, s):
                w = lambda n, k: cw[:, 4 * k + n:4 * k + n + 1]
                if s == 0:
                    c0 = j.value(4 * FT, COLS["ff_w"][0])
                    src = cols[:, c0:c0 + 4 * FT] if j.i is None else cols[:, bass.ds(c0, 4 * FT)]
                    V.tensor_copy(cw[:, :], src).then_inc(sm["cw_done"], 1)
                    dve.wait_ge(acc_free[q.slot], q.turns(2, 1))
                    dve.wait_ge(sm["cw_done"], j.value(1, 1))
                    for k in range(FT):
                        ins = ts(CV[:, k, :], GS[:, k, :], w(1, k), w(3, k), ALU.mult, ALU.add)
                    ins.then_inc(sm["conv_a"], 1)
                if s == 1:
                    dve.wait_ge(sm["conv_a"], j.value(1, 1))
                    for k in range(FT):
                        ins = stt(CV[:, k, 1:T], GS[:, k, 0:T - 1], w(0, k), CV[:, k, 1:T], ALU.mult, ALU.add)
                    ins.then_inc(sm["conv_b"], 1)
                if s == 2:
                    dve.wait_ge(sm["conv_b"], j.value(1, 1))
                    for k in range(FT):
                        ins = stt(CV[:, k, 0:T - 1], GS[:, k, 1:T], w(2, k), CV[:, k, 0:T - 1], ALU.mult, ALU.add)
                    ins.then_inc(sm["conv_done"], 1)

            def gated(q, c, j):
                done(c)
                dve.wait_ge(sm["gelu_done"], j.value(1, 1))
                dve.wait_ge(sm["hid_lo"], j.value(1, STEPS1))
                tt(FQ[:, :, :], acc_ws(q.slot), CV[:, :, :], ALU.mult).then_inc(acc_free[q.slot], 1)

            def down_out2(q, c, s):
                done(c)
                for k in range(4):
                    ins = stt(X[:, 4 * s + k, :], acc_ws(q.slot)[:, k, :], mod[:, 5 * KC + 4 * s + k, 0:1],
                              X[:, 4 * s + k, :], ALU.mult, ALU.add)
                ins.then_inc(acc_free[q.slot], 1)

            def ff2_step(j, first=False):
                c, q = ff2_place(j)
                for s in range(STEP2):
                    low(c.plus(s))
                    if first:
                        if s == 1:
                            gated(q.plus(-1), c.plus(-1), Place(0))
                        if s == 3:
                            hidden_low(Place(0), STEPS1)
                    elif s < 2:
                        down_out2(q.plus(s - 2), c.plus(s - 2), s + 2)
                    if 5 <= s < 8:
                        gate_conv(q, j.plus(1), s - 5)
                    if s == 9:
                        gated(q.plus(1), c.plus(7), j.plus(1))
                    if s >= 10:
                        down_out2(q.plus(s - 8), c.plus(s - 2), s - 10)
                    if s == 11:
                        hidden_low(j.plus(1), STEPS1)

            for s in range(4, 8):
                low(Place(C_FF2 + s))
                if s >= 5:
                    gate_conv(Place(Q_FF2), Place(0), s - 5)
            ff2_step(Place(0), first=True)
            ff2_step(Place(1))
            with dve.Fori(0, FF2_ITERS) as i:
                ff2_step(Place(2, i, 2))
                ff2_step(Place(3, i, 2))
            c, q = Place(C_END - 4), Place(Q_END - 4)
            for s in range(4):
                low(c.plus(s))
                if s < 2:
                    down_out2(q.plus(s - 2), c.plus(s - 2), s + 2)
                else:
                    down_out2(q.plus(s - 2), c.plus(s - 2), s - 2)
                    complete(q.plus(s - 2), s - 2, False)
            add_squares(SQ, 1, True)
            for n in (2, 3):
                down_out2(q.plus(n), c.plus(n), n)
                complete(q.plus(n), n, True)
            inverse_root(N_LAST)
            for n in range(4):
                scaled(NT, quarter(X, n), lambda k: col("final", k), n)

        @block.tensor
        def _(pe):
            MM = nc.tensor.matmul

            def half_ready(c, h):
                pe.wait_ge(lo_done, c.value(2, h + 1))

            def use(q):
                if q.since(2):
                    pe.wait_ge(acc_free[q.slot], q.turns(2))

            def ws(out, c, xh, xl, first, last, kk):
                b = c.base % 2
                for f in range(FT):
                    cs = slice(f * P, (f + 1) * P)
                    wh, wl = WH[:, b, kk, cs], WL[:, b, kk, cs]
                    MM(out[:, f, :], wh, xh, start=first and f % 2 == 0, stop=False, skip_group_check=True)
                    MM(out[:, f, :], wh, xl, start=False, stop=False, skip_group_check=True)
                    ins = MM(out[:, f, :], wl, xh, start=False, stop=last, skip_group_check=True)
                return ins

            def tok(out, c, xh, xl, first, last, kk):
                b = c.base % 2
                wh, wl = WH[:, b, kk, :], WL[:, b, kk, :]
                for t in range(TT):
                    h, l = xh[:, t * P:(t + 1) * P], xl[:, t * P:(t + 1) * P]
                    MM(out[:, t, :], h, wh, start=first, stop=False)
                    MM(out[:, t, :], h, wl, start=False, stop=False)
                    ins = MM(out[:, t, :], l, wh, start=False, stop=last)
                return ins

            def product(c, q, s, xh, xl, k0=0, first=True, last=True, fn=ws, out=None, e=None):
                if q is not None and first:
                    use(q)
                early = s == 0 and e in WINDOWS
                if early:
                    pe.wait_ge(first_lo, WINDOWS.index(e) + 1)
                elif e is not None:
                    pe.wait_ge(x_lo, 4 * e + s + 1)
                if out is None:
                    out = (acc_ws if fn is ws else acc_as)(q.slot)
                for h in range(2):
                    half_ready(c, h)
                    if h and early:
                        pe.wait_ge(x_lo, 4 * e + 1)
                    for kk in range(HF * h, HF * h + HF):
                        ins = fn(out, c, xh[:, k0 + kk, :], xl[:, k0 + kk, :], first and kk == 0,
                                 last and kk == FT - 1, kk)
                    ins.then_inc(pe_half, 1)

            def wide(c, q, s, fn=ws, e=None, xh=XH, xl=XL):
                product(c, q, s, xh, xl, 4 * s, s == 0, s == SLOTS - 1, fn, e=e)

            def down(c, q, j, s, before=0):
                if s == 0:
                    pe.wait_ge(sm["hid_lo"], j.value(1, before + 1))
                product(c, q, s, HH[:, j.base % 2], HL[:, j.base % 2])

            def first_columns(c):
                a, n = divmod(c - T_ADA, S_ADA)
                a -= 1
                if n == 0 and 0 <= a < ADA_GATE:
                    pe.wait_ge(ada1_acc, 32 * a + 32)
                    if a:
                        pe.wait_ge(sm["mod_done"], a)
                    if a == 6:
                        pe.wait_ge(sm["b_free"], 3)
                    if a == 7:
                        pe.wait_ge(sm["b_free"], 4)
                    for f in range(FT):
                        for v in range(2):
                            ins = MM(bank(column_bank(Place(a)))[:, 2 * f + v:2 * f + v + 1], ada1c[:, v, f * P:(f + 1) * P],
                                     ones[:, 0:1], start=True, stop=True)
                    ins.then_inc(sm["mt_done"], 1)

            def norm_sum(norm, sq, parts=None):
                every = PARTS[norm]
                for n in range(len(every)) if parts is None else parts:
                    if n == 0 and norm:
                        pe.wait_ge(sm["norm_rt"], norm)
                    pe.wait_ge(sm["norm_sq"], PARTS_BEFORE[norm] + n + 1)
                    for k in range(4):
                        ins = MM(bank(SUM_BANK[norm])[:, 0:T], ones, sq[:, 4 * every[n] + k, :],
                                 start=n == 0 and k == 0, stop=n == len(every) - 1 and k == 3)
                    if n == len(every) - 1:
                        ins.then_inc(sm["norm_sum"], 1)

            def spatial_gating(n):
                pe.wait_ge(sm["mix_done"], TT + 1)
                if n >= 2:
                    pe.wait_ge(sm["s_done"], n - 1)
                for g in range(2):
                    for c in range(TT):
                        ins = MM(bank(6 + n % 2)[:, (TT * g + c) * P:(TT * g + c + 1) * P],
                                 vg[:, c, (2 * n + g) * P:(2 * n + g + 1) * P], wsp[:, 2 * n + g, :],
                                 start=True, stop=True)
                ins.then_inc(sm["sgu_ps"], 1)

            def head_sums(n):
                pe.wait_ge(sm["qk_sqd"], n + 1)
                for half in range(2):
                    if n:
                        pe.wait_ge(sm["qk_rt"], 2 * n + half - 1)
                    MM(bank(4 + half), ones, qk_sq[:, 2 * half:2 * half + 2, :], start=True, stop=True)\
                        .then_inc(sm["qk_sum"], 1)

            def attention_step(h, t):
                if t == 0:
                    if h == 0:
                        pe.wait_ge(sm["q_done"], 8)
                    else:
                        pe.wait_ge(sm["zs_done"], h)
                    MM(bank(4)[:, 0:T], kT[:, h, 0:P], qT[:, h, :], start=True, stop=True)
                    MM(bank(4)[:, T:384], kT[:, h, P:T], qT[:, h, P:T], start=True, stop=True)\
                        .then_inc(sm["z_done"], 1)
                if t == 2:
                    pe.wait_ge(sm["lk_done"], h + 1)
                    if h:
                        pe.wait_ge(sm["o_done"], h)
                    MM(bank(5)[:, 0:384], lower, lk[:, :], start=True, stop=False)
                    MM(bank(5)[:, P:T], ones, lk[:, T:384], start=False, stop=True).then_inc(sm["cum_done"], 1)
                if t == 4:
                    pe.wait_ge(sm["am_done"], h + 1)
                    if h == 0:
                        for n in range(2):
                            pe.wait_ge(acc_free[n], 3)
                    c = slice(h * DH, (h + 1) * DH)
                    MM(bank(5)[:, 0:T], v1[:, 0, c], aw[:, 0:T], start=True, stop=False)
                    MM(bank(5)[:, P:T], v1[:, 1, c], aw[:, T:384], start=False, stop=True)\
                        .then_inc(sm["pv_done"], 1)

            pe.wait_ge(sm["mats_in"], 16)
            norm_sum(N_IN, NT)
            for c in range(C_OAB):
                if T_SGU <= c < T_SGU + 8 and (c - T_SGU) % 2 == 0:
                    spatial_gating((c - T_SGU) // 2)
                if T_QK < c < T_QK + 16 and (c - T_QK) % 4 == 1:
                    head_sums((c - T_QK) // 4)
                for h in range(HEADS):
                    attention_step(h, c - T_ATT - S_ATT * h)
                first_columns(c)
                g, s = divmod(c, SLOTS)
                wide(Place(c), Place(g), s, tok if 4 <= g < 8 else ws, E_NORM1 if g == 0 else None)
            for n in range(4):
                for s in range(SLOTS):
                    c = Place(C_OAB + 4 * n + s)
                    first_columns(c.base)
                    if n == 1 and s == 2:
                        pe.wait_ge(sm["mod_done"], 6)
                    if s == 2 and n >= 2:
                        pe.wait_ge(sm["b_free"], n - 1)
                    product(c, Place(Q_OAB + n) if s < 2 else None, s, XH, XL, 4 * s, s % 2 == 0, s % 2 == 1,
                            out=acc_ws((Q_OAB + n) % 2) if s < 2 else ctx_ws(n), e=E_OAB)
            for t in range(4 * SLOTS):
                first_columns(C_OUT1 + t)
                if t == 15:
                    norm_sum(N_FF1, NT, [0])
                wide(Place(C_OUT1 + t), Place(Q_OUT1 + t // 4), t % 4, e=E_OUT1, xh=MH, xl=ML)
            norm_sum(N_FF1, NT, [1])

            def sum_columns(a):
                pe.wait_ge(ada_sum, a.value(1, 1 - ADA_GATE))
                pe.wait_ge(sm["mod_done"], a.value())
                for f in range(FT):
                    ins = MM(bank(6)[:, 2 * f:2 * f + 2], adac[:, a.base % 2, 0, f * P:(f + 1) * P],
                             ones[:, 0:2], start=True, stop=True)
                ins.then_inc(sm["mt_done"], 1)

            def ff1_step(j, first=False):
                c, q, a = ff1_place(j)
                for s in range(SLOTS):
                    if s == 3 and not first:
                        sum_columns(a.plus(-1))
                    wide(c.plus(s), q, s)
                for s in range(SLOTS):
                    if first and s == 3:
                        norm_sum(N_CTX, CSQ)
                    down(c.plus(4 + s), q.plus(1 + s), j, s)

            for s in range(SLOTS):
                wide(Place(C_FF1 + s), Place(Q_FF1), s, e=E_NORM2)
            ff1_step(Place(0), True)
            ff1_step(Place(1))
            with pe.Fori(0, FF1_ITERS) as i:
                ff1_step(Place(2, i, 2))
                ff1_step(Place(3, i, 2))
            c, q = Place(C_FF1_TAIL), Place(Q_FF1_TAIL)
            for s in range(SLOTS):
                if s == 3:
                    sum_columns(Place(ADA_GROUPS - 3))
                wide(c.plus(s), q, s)
            for s in range(2 * SLOTS):
                if s == 4:
                    sum_columns(Place(ADA_GROUPS - 2))
                down(c.plus(4 + s), q.plus(1 + s), Place(STEPS1 - 2 + s // 4), s % 4)
            norm_sum(N_MIX_IN, SQ)

            def beside_context(n, s):
                if s == 0 and n >= 2:
                    pe.wait_ge(sm["ctx_free"], n - 1)
                if s == 0 and n == 1:
                    pe.wait_ge(sm["norm_rt"], N_MIX_IN + 1)
                    pe.wait_ge(sm["mod_done"], ADA_GROUPS)
                c = Place(C_IN2 + 4 * n + s)
                fn, out = (ws, ctx_ws(n)) if n < 2 else (tok, ctx_as(n))
                for h in range(2):
                    half_ready(c, h)
                    for kk in range(HF * h, HF * h + HF):
                        k = 4 * s + kk
                        fn(out, c, CH[:, k, :], CL[:, k, :], k == 0, k == KC - 1, kk)

            def bias_columns(n):
                if n >= 4:
                    pe.wait_ge(sm["bias_done"], n - 3)
                for c in range(8):
                    ins = MM(bank(4 + n % 4)[:, c * 64:(c + 1) * 64], bsel[:, n // 2 % 2, 8 * (n % 2) + c, :],
                             brow[:, :], start=True, stop=True)
                ins.then_inc(sm["bias_ps"], 1)

            def attention2_step(t):
                u = t - T_ATT2 - 3
                if 0 <= u < 2 * HEADS:
                    b = u % 2
                    pe.wait_ge(sm["pn_done"], u + 1)
                    if u >= 1:
                        pe.wait_ge(sm["pt_done"], u)
                    for k in range(4):
                        ins = nc.tensor.transpose(bank(6)[:, k * P:(k + 1) * P], P2[:, b, k * P:(k + 1) * P], ident)
                    ins.then_inc(sm["tp_done"], 1)
                u = t - T_ATT2 - 5
                if 0 <= u < 2 * HEADS and u % 2:
                    h = u // 2
                    pe.wait_ge(sm["pt_done"], u + 1)
                    if h:
                        pe.wait_ge(sm["a2_done"], h)
                    c = slice(h * DH, (h + 1) * DH)
                    for k in range(4):
                        ins = MM(bank(7)[:, 0:T], (v2 if k < 2 else vc2)[:, k % 2, c], PT[:, h % 2, k, :],
                                 start=k == 0, stop=k == 3)
                    ins.then_inc(sm["pv2_done"], 1)
                u = t - T_ATT2
                if 0 <= u < 2 * HEADS:
                    b, h, tile = u % 2, u // 2, u % 2
                    if u >= 2:
                        pe.wait_ge(sm["sm_done"], u - 1)
                    else:
                        pe.wait_ge(sm["bias_done"], 5 + u)
                    if u % 8 == 0:
                        q = Place(Q_IN2 + 4 + u // 8)
                        pe.wait_ge(acc_free[q.slot], q.turns(2, 1))
                    qs = q2[:, h, tile * P:(tile + 1) * P]
                    MM(bank(4 + b)[:, 0:T], qs, k2[:, h, :], start=True, stop=True)
                    MM(bank(4 + b)[:, T:2 * T], qs, kc2[:, h, :], start=True, stop=True).then_inc(sm["sc_done"], 1)

            pe.wait_ge(x_lo, 4 * E_CTX + 4)
            for s in range(2):
                beside_context(0, s)
            for t in range(10 * SLOTS):
                n, s = divmod(t, SLOTS)
                if t == 2:
                    sum_columns(Place(ADA_GROUPS - 1))
                if 2 <= t < 4 * SLOTS:
                    beside_context(n, s)
                if t == T_BIAS + 3:
                    pe.wait_ge(sm["ctx_free"], 4)
                    pe.wait_ge(sm["brow_in"], 16)
                if t in (T_BIAS + 3, T_BIAS + 4, T_BIAS + 6, T_BIAS + 7):
                    m = (T_BIAS + 3, T_BIAS + 4, T_BIAS + 6, T_BIAS + 7).index(t)
                    pe.wait_ge(bsel_in[m % 2], 16 * (m // 2 + 1))
                    bias_columns(2 * m)
                    bias_columns(2 * m + 1)
                attention2_step(t)
                wide(Place(C_IN2 + t), Place(Q_IN2 + n), s, tok if n in (2, 3, 6) else ws,
                     E_NORM3 if n == 0 else None)

            def fourier_tokens(n):
                if n >= 2:
                    pe.wait_ge(sm["fu_done"], n - 1)
                for t in range(TT):
                    ins = MM(bank(n % 2), fX[:, t, n * P:(n + 1) * P], fcl[:, t, :], start=t == 0, stop=t == 1)
                ins.then_inc(sm["fu_ps"], 1)

            for t in (40, 41, 42):
                attention2_step(t)
            pe.wait_ge(sm["mlp_in"], 48)
            pe.wait_ge(sm["sm_done"], 2 * HEADS)
            MM(bank(4)[0:64, 0:T], w1h[:, :], pz[:, :], start=True, stop=True).then_inc(sm["mlp_ps"], 1)
            pe.wait_ge(sm["four_in"], 32)
            pe.wait_ge(acc_free[0], Q_OUT2 // 2)
            fourier_tokens(0)
            attention2_step(43)
            attention2_step(44)
            fourier_tokens(1)
            fourier_tokens(2)
            fourier_tokens(3)
            pe.wait_ge(sm["mlp_sin"], 1)
            MM(bank(4)[0:64, 0:T], w2h[:, :], hdn[:, 0, :], start=True, stop=True).then_inc(sm["mlp_ps"], 1)
            pe.wait_ge(acc_free[1], Q_OUT2 // 2)
            pe.wait_ge(sm["pt_done"], 2 * HEADS)
            for n in range(FNG):
                pe.wait_ge(sm["fu_done"], n + 1)
                if n >= 2:
                    pe.wait_ge(sm["fy_done"], n - 1)
                for m in range(2):
                    ins = MM(bank((2, 6)[n % 2])[:, 0:T], fcd[:, m, :], fU[:, n, m * T:(m + 1) * T],
                             start=m == 0, stop=m == 1)
                ins.then_inc(sm["fy_ps"], 1)
            def to_tokens(o):
                if o:
                    pe.wait_ge(sm["hz_done"], 1)
                src = hyC if o == 0 else zT2
                for t in range(TT):
                    for k in range(HT):
                        ins = nc.tensor.transpose(bank(2 + t)[:, k * P:(k + 1) * P], src[:, k, t * P:(t + 1) * P],
                                                  ident)
                    ins.then_inc(sm["zt_ps"], 1)

            pe.wait_ge(sm["mlp_sin"], 2)
            pe.wait_ge(sm["mlp3_in"], 16)
            for n in range(4):
                o, t = n // 2, n % 2
                if n == 1:
                    pe.wait_ge(sm["fy_done"], FNG)
                    pe.wait_ge(sm["a2_done"], HEADS)
                if n >= 2:
                    pe.wait_ge(sm["hf_done"], n - 1)
                for f in range(2):
                    c0 = o * 2 * HW + f * HW
                    ins = MM(bank(4 + 2 * (n % 2) + f), hdn[:, 1, t * P:(t + 1) * P], w3h[:, c0:c0 + HW],
                             start=True, stop=True)
                ins.then_inc(sm["hf_ps"], 1)
                if n == 1:
                    to_tokens(0)

            def spectrum(n):
                o, m = n // 5, n % 5
                pe.wait_ge(sm["hf_done"], 2 * o + 2)
                if n >= 2:
                    pe.wait_ge(sm["ks_done"], n - 1)
                e0 = (0, P, 2 * P, 3 * P, 5 * P)[m]
                for t in range(TT):
                    ins = MM(bank(n % 2), Ef[:, t, e0:e0 + P], hSD[:, o, 1 if m in (2, 3) else 0, t, :],
                             start=t == 0, stop=t == 1)
                ins.then_inc(sm["ks_ps"], 1)

            def forward(o):
                pe.wait_ge(sm["zt_done"], TT * (o + 1))
                if o == 0:
                    pe.wait_ge(sm["hf_done"], 4)
                for w, e0 in enumerate((0, P, 4 * P, 3 * P)):
                    for t in range(TT):
                        ins = MM(bank(4 + w), Ef[:, t, e0:e0 + P], zt[:, t, :], start=t == 0, stop=t == 1)
                ins.then_inc(sm["zf_ps"], 1)

            def inverse(o):
                pe.wait_ge(sm["ys_done"], o + 1)
                for k in range(HT):
                    for w in range(4):
                        ins = MM(bank(2 + k // 2)[:, (k % 2) * T:(k % 2 + 1) * T], YS[:, w, k * P:(k + 1) * P],
                                 Gi[:, w, :], start=w == 0, stop=w == 3)
                ins.then_inc(sm["yi_ps"], 1)

            pe.wait_ge(sm["fu_done"], FNG)
            pe.wait_ge(sm["e_in"], 32)
            for n in range(5):
                spectrum(n)
            forward(0)
            for n in range(5, 10):
                spectrum(n)
            pe.wait_ge(sm["gi_in"], 16)
            inverse(0)
            pe.wait_ge(sm["ks_done"], 10)
            norm_sum(N_A, SM)
            to_tokens(1)
            forward(1)
            norm_sum(N_F, SM)
            pe.wait_ge(sm["norm_rt"], N_A + 1)
            wide(Place(C_OUT2), Place(Q_OUT2), 0, e=E_OUT2)
            pe.wait_ge(sm["norm_rt"], N_F + 1)
            inverse(1)
            wide(Place(C_OUT2 + 1), Place(Q_OUT2), 1, e=E_OUT2)
            norm_sum(N_H, SM)
            wide(Place(C_OUT2 + 2), Place(Q_OUT2), 2, e=E_OUT2)
            wide(Place(C_OUT2 + 3), Place(Q_OUT2), 3, e=E_OUT2)
            pe.wait_ge(sm["hz_done"], 2)
            for t in range(4, 4 * SLOTS):
                if t == 15:
                    norm_sum(N_FF2, NT, [0])
                wide(Place(C_OUT2 + t), Place(Q_OUT2 + t // 4), t % 4)
            norm_sum(N_FF2, NT, [1])

            def ff2_step(j):
                c, q = ff2_place(j)
                for s in range(SLOTS):
                    wide(c.plus(s), q, s)
                for s in range(SLOTS):
                    wide(c.plus(4 + s), q.plus(1), s)
                for s in range(SLOTS):
                    down(c.plus(8 + s), q.plus(2 + s), j, s, STEPS1)

            for s in range(SLOTS):
                wide(Place(C_FF2 + s), Place(Q_FF2), s, e=E_NORM4)
            for s in range(SLOTS):
                wide(Place(C_FF2 + 4 + s), Place(Q_FF2 + 1), s)
            ff2_step(Place(0))
            ff2_step(Place(1))
            with pe.Fori(0, FF2_ITERS) as i:
                ff2_step(Place(2, i, 2))
                ff2_step(Place(3, i, 2))
            for s in range(SLOTS):
                down(Place(C_END - 4 + s), Place(Q_END - 4 + s), Place(STEPS2 - 1), s, STEPS1)
            norm_sum(N_LAST, SQ)


def shape_constants():
    f = np.float32
    out = {}
    r = np.arange(P)
    out["mats"] = np.stack([np.ones((P, P)), np.eye(P), r[:, None] > r[None, :], r[:, None] < r[None, :]], 1).astype(f)
    s = np.zeros((2, 32, GRID_W, 2, GRID_W), f)
    for c in range(GRID_W):
        c0 = min(max(c - NA_KW // 2, 0), GRID_W - NA_KW)
        for k in range(GRID_W):
            row = k - c + NA_KW - 1 if c0 <= k < c0 + NA_KW else 31
            for half in range(2):
                s[half, row, k, half, c] = 1
    out["bsel"] = s.reshape(64, GRID_W, P)
    tok = 2 * np.pi * np.outer(np.arange(T), np.arange(T)) / T
    cl = np.concatenate([np.cos(tok), np.sin(tok)], 1) / np.sqrt(T)
    out["fcl"] = cl.reshape(TT, P, 2 * T).transpose(1, 0, 2).astype(f)
    ch = 2 * np.pi * np.outer(r, r) / P
    out["fcd"] = (np.stack([np.cos(ch), -np.sin(ch)], 1) / np.sqrt(P)).astype(f)
    t = np.arange(T)
    ang = 2 * np.pi * np.outer(t, np.arange(T)) / L2
    cos, sin = np.cos(ang), -np.sin(ang)
    alt = (-1.0) ** t
    im0, re0 = sin[:, :P].copy(), cos[:, :P].copy()
    im0[:, 0] = alt
    re0[:, 0] = alt
    ef = np.concatenate([cos, sin, im0, re0], 1)
    out["ef"] = ef.reshape(TT, P, 6 * P).transpose(1, 0, 2).astype(f)
    g = np.concatenate([cos.T * 2, sin.T * 2], 0) / L2
    g[0] /= 2
    g[T] = alt / L2
    out["gi"] = g.reshape(4, P, T).transpose(1, 0, 2).astype(f)
    pos = np.arange(T, dtype=f)[:, None]
    tn = pos / f(T - 1)
    bands = np.linspace(1e-4, 15, 16, dtype=f)
    a = (bands * f(2.0 * math.pi / T)).astype(f) * pos
    out["pz"] = np.ascontiguousarray(np.concatenate([tn, np.cos(a), -np.sin(a)], 1).T.astype(f))
    deltas = np.linspace(math.log(1e-2) / 1.5, math.log(1e-2) / 0.3, HW, dtype=f)
    decay = np.exp(-tn * np.abs(deltas)).astype(f)
    back = decay.copy()
    back[0] = 0
    out["dec"] = np.stack([decay, back]).reshape(2, TT, P, HW).transpose(2, 0, 1, 3)
    return out


def lay_out(v):
    def columns(a):
        return np.asarray(a).reshape(-1, P).T

    def padded(a):
        return np.concatenate([a, np.zeros((P - a.shape[0], a.shape[1]), a.dtype)], 0)

    a = {k: v[k][0] for k in ("w_in", "w_oa", "w_ob", "w_out", "w_ff1", "w_ff2", "w_in_2", "w_out_2")}
    a["ada_w"], a["w_up"], a["w_down"] = v["ada_w_2"][0], v["ffn_w_up_2"][0], v["ffn_w_down_2"][0]
    a["hy_w1"], a["hy_w2"], a["hy_w3"] = v["hy_w1_2"][0], v["hy_w2_2"][0], v["hy_w3_2"][0]
    a["x"], a["ctx"] = v["x"][0].T, v["ctx_2"][0].T
    ffw = np.concatenate([v["ffn_conv_w_2"][0], v["ffn_conv_b_2"]], 0)
    ffw = ffw.reshape(4, STEPS2, FT, P).transpose(3, 1, 2, 0).reshape(P, -1)
    parts = dict(g_mix=columns(v["g_mix"]), g_q=columns(v["g_q"]), g_k=columns(v["g_k"]), g_ff=columns(v["g_ff"]),
                 norm1=columns(v["norm1_g_2"]), norm2=columns(v["norm2_g_2"]), mix=columns(v["mix_norm_g_2"]),
                 final=columns(v["final_norm_g_2"]), ada_b=columns(v["ada_b_2"]), hy_w=columns(v["hy_conv_w_2"]),
                 hy_b=columns(v["hy_conv_b_2"]), hy_bias=columns(v["hy_bias_2"]), ff_w=ffw,
                 c=np.concatenate([columns(v["c_2"]), columns(v["c_ctx_2"])], 1),
                 mlp=padded(np.stack([v["hy_b1_2"][0], v["hy_b2_2"][0], v["hy_freq_2"][0]], 1)))
    assert all(parts[n].shape[1] == w for n, (_, w) in COLS.items())
    a["cols"] = np.concatenate([parts[n] for n in COLS], 1)
    a["ln_g"] = np.broadcast_to(v["sgu_ln_g"], (P, 1024))
    a["ln_b"] = np.broadcast_to(v["sgu_ln_b"], (P, 1024))
    a["b_sp"] = np.broadcast_to(v["b_spatial"], (P, 8, P))
    a["w_sp"] = v["w_spatial"][0].transpose(2, 0, 1)
    rpb = v["na_rpb_2"][0]
    rows = [[[NA_KH - 1 + r - (2 * t + half) for r in range(ROWS)] for t in range(TT)] for half in range(2)]
    b = rpb[:, np.array(rows), :].transpose(1, 4, 2, 0, 3)
    neg = np.full((2, 1) + b.shape[2:], NEG, b.dtype)
    a["brow"] = np.concatenate([b, neg], 1).reshape(64, 64)
    a.update(shape_constants())
    return {k: np.ascontiguousarray(x) for k, x in a.items()}


def kernel(**inputs):
    import concourse.bacc as bacc
    from concourse.bass_utils import run_bass_kernel_spmd

    nc = bacc.Bacc("TRN2", target_bir_lowering=False, num_devices=1)
    arrays = lay_out({k: np.asarray(x) for k, x in inputs.items()})
    d = {k: nc.dram_tensor("in_" + k, a.shape, mybir.dt.from_np(a.dtype), kind="ExternalInput").ap()
         for k, a in arrays.items()}
    out = nc.dram_tensor("out", (D, T), mybir.dt.float32, kind="ExternalOutput").ap()
    build_program(nc, d, out)
    r = run_bass_kernel_spmd(nc, [{"in_" + k: a for k, a in arrays.items()}], core_ids=[0])
    return np.ascontiguousarray(r.results[0]["out"].T)[None]
```
